# Optimizing a Trainium2 kernel written in Bass

```python
import math
import jax, jax.numpy as jnp
from jax import lax
import numpy as np

D_MODEL = 1024
BATCH = 1
SEQ = 256
DEPTH = 1

CTX_LEN = 256
GRID_W = 64
D_MIX = D_MODEL
S5_WIDTH = D_MIX // 2
S5_GROUP = 16
S5_GROUPS = S5_WIDTH // S5_GROUP
S5_STATE = 64
FOURIER_WIDTH = D_MIX - S5_WIDTH
FOURIER_GROUPS = 4
FOURIER_GROUP = FOURIER_WIDTH // FOURIER_GROUPS
PEER_HEADS = 8
PEER_KEYS = 128
PEER_EXPERTS = PEER_KEYS * PEER_KEYS
PEER_TOPK = 16
PEER_DKEY = 256
PEER_HALF = PEER_DKEY // 2
PEER_CHUNK = 128
N_MOD = 6
RMS_EPS = 1e-6
DT_MIN = 1e-3
DT_MAX = 1e-1
POS_BASE = 10000.0

kernel_name = 'hymba_s5_fnet_peer_dit_layer'

def rmsnorm(x, g):
    xf = x.astype(jnp.float32)
    inv = lax.rsqrt(jnp.mean(xf * xf, axis=-1, keepdims=True) + RMS_EPS)
    return (xf * inv).astype(x.dtype) * g

def modulate(h, shift, scale):
    return h * (1 + scale) + shift

def grid_pos_embed(rows, dim, dtype):
    quarter = dim // 4
    omega = 1.0 / (POS_BASE ** (jnp.arange(quarter, dtype=jnp.float32) / quarter))
    r = jnp.repeat(jnp.arange(rows, dtype=jnp.float32), GRID_W)[:, None] * omega
    col = jnp.tile(jnp.arange(GRID_W, dtype=jnp.float32), rows)[:, None] * omega
    emb = jnp.concatenate([jnp.sin(r), jnp.cos(r), jnp.sin(col), jnp.cos(col)], axis=-1)
    return emb.astype(dtype)

def _ssm_combine(e1, e2):
    a1r, a1i, b1r, b1i = e1
    a2r, a2i, b2r, b2i = e2
    return (a2r * a1r - a2i * a1i,
            a2r * a1i + a2i * a1r,
            a2r * b1r - a2i * b1i + b2r,
            a2r * b1i + a2i * b1r + b2i)

def s5_discretise(lam_re, lam_im, log_dt, b_re, b_im):
    dt = jnp.exp(log_dt.astype(jnp.float32))[:, None]
    lr = lam_re.astype(jnp.float32)
    li = lam_im.astype(jnp.float32)
    mag = jnp.exp(lr * dt)
    ar = mag * jnp.cos(li * dt)
    ai = mag * jnp.sin(li * dt)
    den = lr * lr + li * li
    cr = ((ar - 1.0) * lr + ai * li) / den
    ci = (ai * lr - (ar - 1.0) * li) / den
    bbr = cr[..., None] * b_re - ci[..., None] * b_im
    bbi = cr[..., None] * b_im + ci[..., None] * b_re
    return ar, ai, bbr, bbi

def s5_scan(u_t, disc, h0, reverse):
    ar, ai, bbr, bbi = disc
    bu_re = jnp.einsum('lbgp,gnp->lbgn', u_t, bbr)
    bu_im = jnp.einsum('lbgp,gnp->lbgn', u_t, bbi)
    h0_re, h0_im = h0
    first = u_t.shape[0] - 1 if reverse else 0
    bu_re = bu_re.at[first].add(ar * h0_re - ai * h0_im)
    bu_im = bu_im.at[first].add(ar * h0_im + ai * h0_re)
    a_shape = (u_t.shape[0], 1) + ar.shape
    a_re = jnp.broadcast_to(ar, a_shape)
    a_im = jnp.broadcast_to(ai, a_shape)
    _, _, s_re, s_im = lax.associative_scan(_ssm_combine, (a_re, a_im, bu_re, bu_im),
                                            reverse=reverse, axis=0)
    return s_re, s_im

def s5_states(u, h0s, lam_re, lam_im, log_dt, b_re, b_im):
    bsz, length, _ = u.shape
    u_t = jnp.moveaxis(u.astype(jnp.float32).reshape(bsz, length, S5_GROUPS, S5_GROUP), 1, 0)
    fwd = s5_scan(u_t, s5_discretise(lam_re[0], lam_im[0], log_dt[0], b_re[0], b_im[0]), h0s[0], False)
    bwd = s5_scan(u_t, s5_discretise(lam_re[1], lam_im[1], log_dt[1], b_re[1], b_im[1]), h0s[1], True)
    return fwd, bwd

def s5_final_states(states):
    fwd, bwd = states
    return (fwd[0][-1], fwd[1][-1]), (bwd[0][0], bwd[1][0])

def s5_readout(s_re, s_im, c_re, c_im):
    return jnp.einsum('lbgn,gpn->lbgp', s_re, c_re) - jnp.einsum('lbgn,gpn->lbgp', s_im, c_im)

def s5_output(u, states, c_re, c_im, d_skip, w_glu, b_glu):
    bsz, length, _ = u.shape
    (fr, fi), (br, bi) = states
    y_t = s5_readout(fr, fi, c_re[0], c_im[0]) + s5_readout(br, bi, c_re[1], c_im[1])
    y = jnp.moveaxis(y_t, 0, 1).reshape(bsz, length, S5_WIDTH) + d_skip * u.astype(jnp.float32)
    y = jax.nn.gelu(y)
    y = y * jax.nn.sigmoid(y @ w_glu + b_glu)
    return y.astype(u.dtype)

def fourier_branch(f, w_fourier):
    bsz, length, _ = f.shape
    fg = f.astype(jnp.float32).reshape(bsz, length, FOURIER_GROUPS, FOURIER_GROUP)
    mixed = jnp.fft.fft2(fg, axes=(1, 3), norm='ortho').real
    out = jnp.einsum('blgc,gcd->blgd', mixed, w_fourier)
    return out.reshape(bsz, length, FOURIER_WIDTH).astype(f.dtype)

def peer(h, w_q, sub_keys, u_tab, v_tab):
    bsz, length, dim = h.shape
    blocks = h.reshape(-1, PEER_CHUNK, dim)

    def block_fn(hc):
        q = (hc @ w_q).reshape(PEER_CHUNK, PEER_HEADS, 2, PEER_HALF)
        s = jnp.einsum('chsd,hskd->chsk', q, sub_keys).astype(jnp.float32)
        sv, si = lax.top_k(s, PEER_TOPK)
        cand = sv[:, :, 0, :, None] + sv[:, :, 1, None, :]
        best, flat = lax.top_k(cand.reshape(PEER_CHUNK, PEER_HEADS, PEER_TOPK * PEER_TOPK), PEER_TOPK)
        idx1 = jnp.take_along_axis(si[:, :, 0], flat // PEER_TOPK, axis=-1)
        idx2 = jnp.take_along_axis(si[:, :, 1], flat % PEER_TOPK, axis=-1)
        expert = idx1 * PEER_KEYS + idx2
        g = jax.nn.softmax(best, axis=-1)
        act = jax.nn.gelu(jnp.einsum('cd,chkd->chk', hc, u_tab[expert]))
        return jnp.einsum('chk,chkd->cd', (g * act).astype(hc.dtype), v_tab[expert])

    return lax.map(block_fn, blocks).reshape(bsz, length, dim)

def trunk_layer(x, ctx, c_act, cc_act, w_mod, b_mod, norm1_g, norm2_g, w_in, w_out,
                lam_re, lam_im, log_dt, b_re, b_im, c_re, c_im, d_skip, w_glu, b_glu,
                w_fourier, w_q, sub_keys, u_tab, v_tab, update_ctx):
    sh1, sc1, g1, sh2, sc2, g2 = jnp.split((c_act @ w_mod + b_mod)[:, None, :], N_MOD, axis=-1)
    csh1, csc1, cg1, csh2, csc2, cg2 = jnp.split(cc_act @ w_mod + b_mod, N_MOD, axis=-1)

    h = modulate(rmsnorm(x, norm1_g), sh1, sc1)
    hc = modulate(rmsnorm(ctx, norm1_g), csh1, csc1)
    z = h @ w_in
    u, f = z[..., :S5_WIDTH], z[..., S5_WIDTH:]
    zc = hc @ w_in if update_ctx else hc @ w_in[:, :S5_WIDTH]
    uc = zc[..., :S5_WIDTH]

    zero = jnp.zeros((ctx.shape[0], S5_GROUPS, S5_STATE), jnp.float32)
    ctx_states = s5_states(uc, ((zero, zero), (zero, zero)), lam_re, lam_im, log_dt, b_re, b_im)
    lat_states = s5_states(u, s5_final_states(ctx_states), lam_re, lam_im, log_dt, b_re, b_im)

    mix = jnp.concatenate([s5_output(u, lat_states, c_re, c_im, d_skip, w_glu, b_glu),
                           fourier_branch(f, w_fourier)], axis=-1) @ w_out
    x = x + g1 * mix
    x = x + g2 * peer(modulate(rmsnorm(x, norm2_g), sh2, sc2), w_q, sub_keys, u_tab, v_tab)

    if update_ctx:
        mix_c = jnp.concatenate([s5_output(uc, ctx_states, c_re, c_im, d_skip, w_glu, b_glu),
                                 fourier_branch(zc[..., S5_WIDTH:], w_fourier)], axis=-1) @ w_out
        ctx = ctx + cg1 * mix_c
        ctx = ctx + cg2 * peer(modulate(rmsnorm(ctx, norm2_g), csh2, csc2), w_q, sub_keys, u_tab, v_tab)
    return x, ctx

def setup_inputs(seed: int = 0) -> dict:
    key = jax.random.key(seed)
    ks = jax.random.split(key, 32)
    f32 = jnp.float32
    nrm = lambda k, shape, s: jax.random.normal(k, shape, f32) * s
    L, G, N, P = DEPTH, S5_GROUPS, S5_STATE, S5_GROUP
    lam_re = -0.5 + nrm(ks[16], (L, 2, G, N), 0.01)
    lam_im = math.pi * jnp.arange(N, dtype=f32) + nrm(ks[17], (L, 2, G, N), 0.01)
    log_dt = jax.random.uniform(ks[18], (L, 2, G), f32, math.log(DT_MIN), math.log(DT_MAX))
    return {
        'x': nrm(ks[0], (BATCH, SEQ, D_MODEL), 1.0),
        'c': nrm(ks[1], (BATCH, D_MODEL), 1.0),
        'ctx': nrm(ks[2], (BATCH, CTX_LEN, D_MODEL), 1.0),
        'c_ctx': nrm(ks[3], (D_MODEL,), 1.0),
        'w_mod': nrm(ks[4], (L, D_MODEL, N_MOD * D_MODEL), D_MODEL ** -0.5),
        'b_mod': nrm(ks[5], (L, N_MOD * D_MODEL), 0.01),
        'norm1_g': 1.0 + nrm(ks[6], (L, D_MODEL), 0.05),
        'norm2_g': 1.0 + nrm(ks[7], (L, D_MODEL), 0.05),
        'w_in': nrm(ks[8], (L, D_MODEL, D_MIX), D_MODEL ** -0.5),
        'w_out': nrm(ks[9], (L, D_MIX, D_MODEL), D_MIX ** -0.5),
        's5_lam_re': lam_re,
        's5_lam_im': lam_im,
        's5_log_dt': log_dt,
        's5_b_re': nrm(ks[10], (L, 2, G, N, P), (2 * P) ** -0.5),
        's5_b_im': nrm(ks[11], (L, 2, G, N, P), (2 * P) ** -0.5),
        's5_c_re': nrm(ks[12], (L, 2, G, P, N), N ** -0.5),
        's5_c_im': nrm(ks[13], (L, 2, G, P, N), N ** -0.5),
        's5_d': nrm(ks[14], (L, S5_WIDTH), 1.0),
        'w_glu': nrm(ks[15], (L, S5_WIDTH, S5_WIDTH), S5_WIDTH ** -0.5),
        'b_glu': nrm(ks[19], (L, S5_WIDTH), 0.01),
        'w_fourier': nrm(ks[20], (L, FOURIER_GROUPS, FOURIER_GROUP, FOURIER_GROUP), FOURIER_GROUP ** -0.5),
        'peer_w_q': nrm(ks[21], (L, D_MODEL, PEER_HEADS * PEER_DKEY), D_MODEL ** -0.5),
        'peer_sub_keys': nrm(ks[22], (L, PEER_HEADS, 2, PEER_KEYS, PEER_HALF), PEER_HALF ** -0.5),
        'peer_u': nrm(ks[23], (L, PEER_EXPERTS, D_MODEL), D_MODEL ** -0.5),
        'peer_v': nrm(ks[24], (L, PEER_EXPERTS, D_MODEL), 1.0),
        'final_g': 1.0 + nrm(ks[25], (D_MODEL,), 0.05),
    }

def reference(x, c, ctx, c_ctx, w_mod, b_mod, norm1_g, norm2_g, w_in, w_out,
              s5_lam_re, s5_lam_im, s5_log_dt, s5_b_re, s5_b_im, s5_c_re, s5_c_im, s5_d,
              w_glu, b_glu, w_fourier, peer_w_q, peer_sub_keys, peer_u, peer_v, final_g):
    rows = x.shape[1] // GRID_W
    x = x + grid_pos_embed(rows, D_MODEL, x.dtype)[None]
    c_act = jax.nn.silu(c)
    cc_act = jax.nn.silu(c_ctx)
    for l in range(DEPTH):
        x, ctx = trunk_layer(x, ctx, c_act, cc_act, w_mod[l], b_mod[l], norm1_g[l], norm2_g[l],
                             w_in[l], w_out[l], s5_lam_re[l], s5_lam_im[l], s5_log_dt[l],
                             s5_b_re[l], s5_b_im[l], s5_c_re[l], s5_c_im[l], s5_d[l],
                             w_glu[l], b_glu[l], w_fourier[l], peer_w_q[l], peer_sub_keys[l],
                             peer_u[l], peer_v[l], update_ctx=(l < DEPTH - 1))
    return rmsnorm(x, final_g)


_drawn_inputs = setup_inputs


def setup_inputs(seed=0):
    import zlib

    import numpy as np

    out = dict(_drawn_inputs(seed))
    spreads = {}
    factors = {}
    for name, (base, spread) in spreads.items():
        noise = np.random.default_rng([zlib.crc32(name.encode()), seed]).standard_normal(out[name].shape)
        drawn = base * np.exp(spread * noise) if base else spread * noise
        out[name] = __import__('jax').numpy.asarray(drawn.astype(out[name].dtype))
    for name, factor in factors.items():
        out[name] = (out[name] * factor).astype(out[name].dtype)
    return out
```

```python
from contextlib import ExitStack

import numpy as np

import concourse.bass as bass
from concourse import mybir

P = 128
D = 1024
KD = D // P
SEQ = 256
GRID_W = 64
G, NS, Q = 32, 64, 16
T = 8
C = SEQ // T
SW = G * Q
FG = 4
HEADS, KEYS, TOPK = 8, 128, 16
SLOTS = 20
NT = SEQ // P
U_RING, V_RING = 8, 8
EPS = 1e-6
ROUND = 12582912.0
TWO_PI = 6.283185
GELU_K = 0.7978845608028654
GELU_C = 0.044715
LOWEST = -3.0e38

V_C, V_CCTX, V_BMOD, V_N1, V_N2, V_BGLU, V_D, V_ROWS = 0, 8, 16, 64, 72, 80, 84, 88
SH1, SC1, G1, SH2, SC2, G2 = range(6)
PART_ORDER = [SH1, SC1, SH2, SC2, G1, G2]
WM_COLS = 256
WM_PER_PART = D // WM_COLS
WM_RING = 3


def hybrid_layer(nc, x, c, ctx_in, c_ctx, w_mod, b_mod, norm1_g, norm2_g, w_in, w_out, lam_re, lam_im,
                 log_dt, b_re, b_im, c_re, c_im, d_skip, w_glu, b_glu, w_fourier, peer_w_q, sub_keys,
                 peer_u, peer_v, final_g, pos, small_const, dft_const, out):
    F = mybir.dt.float32
    U32 = mybir.dt.uint32
    ALU = mybir.AluOpType
    ACT = mybir.ActivationFunctionType
    AX = mybir.AxisListType.X
    stack = ExitStack()
    with stack:
        def sem(name):
            return stack.enter_context(nc.semaphore(name))

        def region(name, cols):
            return stack.enter_context(nc.sbuf_tensor(name, [P, cols], F))

        R1 = region("R1", 16384)
        R2 = region("R2", 8192)
        R3 = region("R3", 16384)
        R4 = region("R4", 11520)
        R5 = region("R5", 728)
        psum = stack.enter_context(nc.psum_tensor("psum", [P, 8 * 512], F))
        bank = [psum[:, 512 * i:512 * (i + 1)] for i in range(8)]

        wm = [R1[:, 2048 * s:2048 * (s + 1)].rearrange("p (k n) -> p k n", k=KD) for s in range(WM_RING)]
        VSc = R1[:, 6144:8192].rearrange("p (c r g) -> p c r g", c=C, r=2)
        w_in_s = R1[:, 8192:16384].rearrange("p (k n) -> p k n", k=KD)
        VSl = R1[:, 8192:10240].rearrange("p (c r g) -> p c r g", c=C, r=2)
        M = R1[:, 10240:14336].rearrange("p (g n) -> p g n", g=G)
        w_glu_s = R1[:, 14336:16384].rearrange("p (k n) -> p k n", k=4)
        xr = R1[:, 0:2048].rearrange("p (i n) -> p i n", i=NT)
        posr = R1[:, 2048:4096].rearrange("p (i n) -> p i n", i=NT)
        keys_nat = R1[:, 4096:6144].rearrange("p (h n) -> p h n", h=2 * HEADS)
        w_q_s = R1[:, :].rearrange("p (k n) -> p k n", k=KD)
        Bnat = [R2[0:G, 0:2048], R2[0:G, 2048:4096]]
        Cnat = [R2[:, 4096 + 512 * r:4608 + 512 * r].rearrange("p (i d n) -> p i d n", i=4, d=2) for r in range(2)]
        W = R2[:, :].rearrange("p (g r n) -> p g r n", g=G, r=2)
        Kev = [R2[:, 512 * d:512 * d + 512].rearrange("p (i n) -> p i n", i=4) for d in range(2)]
        KK = R2[:, 1024:1984].rearrange("p (i e q) -> p i e q", i=4, e=15)
        Ktmp = R2[:, 1984:2048].rearrange("p (i q) -> p i q", i=4)
        w_out_s = R2[:, :].rearrange("p (k n) -> p k n", k=KD)
        Vring = R2[:, :].rearrange("p (s n) -> p s n", s=V_RING)
        CA = [R3[:, 5120 * r:5120 * (r + 1)].rearrange("p (g s q) -> p g s q", g=G, s=10) for r in range(2)]
        xl = R3[:, 10240:12288].rearrange("p (i n) -> p i n", i=NT)
        xc = R3[:, 12288:14336].rearrange("p (i n) -> p i n", i=NT)
        pl = R3[:, 14336:16384].rearrange("p (i n) -> p i n", i=NT)
        Z = R3[:, 10240:14336]
        Us = R3[:, 14336:16384].rearrange("p (g c) -> p g c", g=G)
        GC = [R3[:, 10240 + 1024 * r:11264 + 1024 * r].rearrange("p (i n) -> p i n", i=NT) for r in range(2)]
        Yc = R3[:, 12288:13312].rearrange("p (t n) -> p t n", t=T)
        Uring = R3[:, 0:8192].rearrange("p (s n) -> p s n", s=U_RING)
        g2b = R3[:, 8192:9216]
        fgb = R3[:, 9216:10240]
        diag = R3[:, 10240:11264].rearrange("p (s n) -> p s n", s=8)
        qT = R3[:, 11264:11776].rearrange("p (w s n) -> p w s n", w=2, s=2)
        rowA = R3[:, 12288:13312]
        rowB = R3[:, 13312:14336]
        tk = R3[:, 14336:16384]
        cand, wrk = tk[:, 0:256], tk[:, 256:512]
        wrk1 = tk[:, 512:768].rearrange("p (s n) -> p s n", s=2)
        sv = tk[:, 768:800].rearrange("p (s n) -> p s n", s=2)
        si = tk[:, 800:832].bitcast(U32).rearrange("p (s n) -> p s n", s=2)
        sif = tk[:, 832:864].rearrange("p (s n) -> p s n", s=2)
        best = tk[:, 864:880]
        flat = tk[:, 880:896].bitcast(U32)
        fij = tk[:, 896:928].bitcast(U32).rearrange("p (s n) -> p s n", s=2)
        fijf = tk[:, 928:960].rearrange("p (s n) -> p s n", s=2)
        pick = tk[:, 960:976]
        idx_all = tk[:, 976:1232].bitcast(U32)
        e_all = tk[:, 1232:1488]
        esum = tk[:, 1488:1504]
        dots = tk[:, 1504:1536].rearrange("p (w n) -> p w n", w=2)
        garg = tk[:, 1536:1552]
        wgt = tk[:, 1552:1808]
        idx_u = tk[:, 1824:1856].bitcast(U32).rearrange("p (w n) -> p w n", w=2)
        idx_v = tk[:, 1856:1888].bitcast(U32).rearrange("p (w n) -> p w n", w=2)
        gth = tk[:, 1888:1904]
        rsum = tk[:, 1904:1920]
        gdiag = tk[:, 1920:2048]
        hT = R4[:, 0:4096].rearrange("p (k n) -> p k n", k=KD)
        mixT = R4[:, 0:2048].rearrange("p (k n) -> p k n", k=KD)
        gA = R4[:, 2048:3072].rearrange("p (k n) -> p k n", k=4)
        gB = R4[:, 3072:4096].rearrange("p (k n) -> p k n", k=4)
        sc = R4[:, 2048:4096].rearrange("p (h s n) -> p h s n", h=HEADS, s=2)
        Pw = [R4[:, 4096 + 640 * r:4736 + 640 * r].rearrange("p (s g) -> p s g", s=SLOTS) for r in range(2)]
        fT = R4[:, 4096:5120].rearrange("p (j n) -> p j n", j=FG)
        Bb = [R4[:, 5376 + 512 * r:5888 + 512 * r].rearrange("p (g q) -> p g q", g=G) for r in range(2)]
        Cs = [R4[:, 6400 + 512 * r:6912 + 512 * r].rearrange("p (g q) -> p g q", g=G) for r in range(2)]
        CW = [R4[:, 6400 + 512 * r:6912 + 512 * r] for r in range(2)]
        dtmp = R4[:, 7424:9472]
        S2 = R4[:, 7424:9472].rearrange("p (r g c) -> p r g c", r=2, g=G)
        ptmp = R4[:, 9472:11520]
        dft = R4[:, 9472:10752]
        cosC, sinC = dft[:, 0:128], dft[:, 128:256]
        cosL = dft[:, 256:768].rearrange("p (i n) -> p i n", i=NT)
        nsinL = dft[:, 768:1280].rearrange("p (i n) -> p i n", i=NT)
        wf_s = R4[:, 10752:11264]
        ones = R4[:, 11264:11392]
        kT = R4[:, 4096:6144].rearrange("p (h n) -> p h n", h=2 * HEADS)
        x1T = R4[:, 6144:8192].rearrange("p (k n) -> p k n", k=KD)
        h2T = R4[:, 8192:9216].rearrange("p (k n) -> p k n", k=KD)
        diag2 = R4[:, 9216:9344]
        zrow = [R1[:, 6144:6656], R1[:, 6656:7168], R1[:, 7168:7680], R4[:, 4608:5120]]
        ident = R5[:, 0:128]
        kmul = R5[:, 128:148]
        iota16 = R5[:, 148:164]
        eyeq = R5[:, 164:180]
        vecT = R5[:, 180:268]
        modS = R5[:, 268:364].rearrange("p (a k w) -> p a k w", a=6, k=KD)
        cact = R5[:, 364:380]
        th_c = R5[:, 380:396]
        Gn1 = R5[:, 396:412].rearrange("p (k w) -> p k w", k=KD)
        Gn2 = R5[:, 412:420]
        Arr = R5[:, 420:484].rearrange("p (r g) -> p r g", r=2)
        Aii = R5[:, 484:548].rearrange("p (r g) -> p r g", r=2)
        half_bg = R5[:, 548:552]
        ss = R5[:, 552:556]
        inv = R5[:, 556:560]
        dE = R5[:, 568:632].rearrange("p (i q) -> p i q", i=4)
        ms, root, newton = R5[:, 560:564], R5[:, 564:568], R5[:, 724:728]
        par = R5[:, 632:728].rearrange("p (a g) -> p a g", a=3)
        vec_nat = R4[0:V_ROWS, 0:128]
        lam_nat = [R4[0:G, 128 * (1 + r):128 * (2 + r)] for r in range(3)]
        ld_nat = R4[0:G, 512:514]
        junk = R4[:, 1024:2048]

        kk_dram = nc.dram_tensor("kk_dram", [G, Q, 15 * Q], F).ap()

        vec_in, const_in, lam_in, b_in, c_in = sem("vec_in"), sem("const_in"), sem("lam_in"), sem("b_in"), sem("c_in")
        xc_in, xl_in, win_in, wout_in, wq_in = sem("xc_in"), sem("xl_in"), sem("win_in"), sem("wout_in"), sem("wq_in")
        glu_in, dft_in, xr_in, keys_in, fg_in = sem("glu_in"), sem("dft_in"), sem("xr_in"), sem("keys_in"), sem("fg_in")
        zc_in = [sem("zc_in_ctx"), sem("zc_in_lat")]
        kk_out, m_in, out_done = sem("kk_out"), sem("m_in"), sem("out_done")
        wm_in = [sem(f"wm_in{s}") for s in range(WM_RING)]
        u_in = [sem(f"u_in{s}") for s in range(U_RING)]
        v_in = [sem(f"v_in{s}") for s in range(V_RING)]
        dve_step, act_step, pool_step = sem("dve_step"), sem("act_step"), sem("pool_step")
        vec_T, par_T, b_T, c_T, x_T = sem("vec_T"), sem("par_T"), sem("b_T"), sem("c_T"), sem("x_T")
        mod_done, w_T, z_done, u_T, v_done = sem("mod_done"), sem("w_T"), sem("z_done"), sem("u_T"), sem("v_done")
        f_done, k_done, kt_done, cw_done = sem("f_done"), sem("k_done"), sem("kt_done"), sem("cw_done")
        gg_done, fft_done, y_done, yt_done = sem("gg_done"), sem("fft_done"), sem("y_done"), sem("yt_done")
        glu_done, keys_T, xt_T, o_done = sem("glu_done"), sem("keys_T"), sem("xt_T"), sem("o_done")
        ss_done, invb_done, h2_pd, q_done = sem("ss_done"), sem("invb_done"), sem("h2_pd"), sem("q_done")
        s_done, g2_done, x1r_done = sem("s_done"), sem("g2_done"), sem("x1r_done")
        v_used = sem("v_used")
        logdt_spread, vec_ready, par_ready, silu_th = sem("logdt_spread"), sem("vec_ready"), sem("par_ready"), sem("silu_th")
        cact_ready, dt_ready, trig_in, trig_out = sem("cact_ready"), sem("dt_ready"), sem("trig_in"), sem("trig_out")
        pw_ready, bb_ready, cs_ready = sem("pw_ready"), sem("bb_ready"), sem("cs_ready")
        wt_dve, wt_pool, w_ready, ca_ready = sem("wt_dve"), sem("wt_pool"), sem("w_ready"), sem("ca_ready")
        x_pos, ss_ready, ms_ready, root_ready = sem("x_pos"), sem("ss_ready"), sem("ms_ready"), sem("root_ready")
        xn_ready, hraw_dve, hraw_act, h_ready = sem("xn_ready"), sem("hraw_dve"), sem("hraw_act"), sem("h_ready")
        mod_read, z_evac, zg_act, zg_dve = sem("mod_read"), sem("z_evac"), sem("zg_act"), sem("zg_dve")
        u_ready, vs_act, vs_dve = sem("u_ready"), sem("vs_act"), sem("vs_dve")
        scan_step, s2_act, s2_dve = sem("scan_step"), sem("s2_act"), sem("s2_dve")
        f_ready, k_ready, kk_copied, kk_ready = sem("f_ready"), sem("k_ready"), sem("kk_copied"), sem("kk_ready")
        cw_ready, gg_ready, mix_f, mix_s5 = sem("cw_ready"), sem("gg_ready"), sem("mix_f"), sem("mix_s5")
        y_act, y_dve, yn_act, yn_dve = sem("y_act"), sem("y_dve"), sem("yn_act"), sem("yn_dve")
        y_sq, y_arg, y_th, g2y_ready, glu_th = sem("y_sq"), sem("y_arg"), sem("y_th"), sem("g2y_ready"), sem("glu_th")
        xr_ready, kt_ready, xt_ready, x1_ready = sem("xr_ready"), sem("kt_ready"), sem("xt_ready"), sem("x1_ready")
        sq_ready, diag2_ready = sem("sq_ready"), sem("diag2_ready")
        h2_ready, q_ready, s_ready, ones_ready = sem("h2_ready"), sem("q_ready"), sem("s_ready"), sem("ones_ready")
        top_ready, exp_ready, idx_ready = sem("top_ready"), sem("exp_ready"), sem("idx_ready")
        idx_copied, u_used = sem("idx_copied"), sem("u_used")
        pool_passed, act_passed, dve_passed = sem("pool_passed"), sem("act_passed"), sem("dve_passed")
        garg_ready, gth_ready, wgt_ready, diag_ready = sem("garg_ready"), sem("gth_ready"), sem("wgt_ready"), sem("diag_ready")
        gdiag_ready, g2b_ready, y_row, fin_ss, out_row = sem("gdiag_ready"), sem("g2b_ready"), sem("y_row"), sem("fin_ss"), sem("out_row")

        class Chain:

            def __init__(self, eng, s):
                self.eng, self.sem, self.n = eng, s, 0

            def step(self, ins):
                ins.then_inc(self.sem, 1)
                self.n += 1

            def after(self):
                self.eng.wait_ge(self.sem, self.n)

            def link(self, ins):
                self.step(ins)
                self.after()

        def query_place(n):
            return (bank[6 + n % 2] if n < HEADS else bank[6])[:, 0:2 * P]

        def score_place(n):
            return (bank[4 + n % 2] if n < HEADS else bank[7])[:, 0:2 * P]

        def wait_alone(eng, s, value, passed):
            eng.wait_ge(s, value)
            if not isinstance(value, int):
                eng.sem_inc(passed, 1)

        def spread(ap, axis, shape):
            return ap.unsqueeze(axis).to_broadcast(shape)

        block = stack.enter_context(nc.Block())

        @block.sync
        def _(sp):
            def load(dst, src, s):
                sp.dma_start(dst, src).then_inc(s, 16)

            load(R5[:, 0:180], small_const, const_in)
            for src, row, rows in ((c, V_C, 8), (c_ctx, V_CCTX, 8), (b_mod, V_BMOD, 48), (norm1_g, V_N1, 8),
                                   (norm2_g, V_N2, 8), (b_glu, V_BGLU, 4), (d_skip, V_D, 4)):
                load(R4[row:row + rows, 0:128], src, vec_in)
            load(lam_nat[0].rearrange("g (d n) -> g d n", d=2), lam_re.rearrange("d g n -> g d n"), lam_in)
            load(lam_nat[1].rearrange("g (d n) -> g d n", d=2), lam_im.rearrange("d g n -> g d n"), lam_in)
            with nc.allow_non_contiguous_dma(reason="64 values"):
                load(ld_nat, log_dt.rearrange("d g -> g d"), lam_in)
            load(xc, ctx_in.rearrange("(i p) n -> p i n", p=P), xc_in)
            load(xl, x.rearrange("(i p) n -> p i n", p=P), xl_in)
            load(pl, pos.rearrange("(i p) n -> p i n", p=P), xl_in)

            def load_mod(n):
                part, quarter = PART_ORDER[n // WM_PER_PART], n % WM_PER_PART
                if n >= WM_RING:
                    sp.wait_ge(mod_done, n - WM_RING + 1)
                col = part * D + quarter * WM_COLS
                load(wm[n % WM_RING], w_mod[:, col:col + WM_COLS].rearrange("(k p) n -> p k n", p=P), wm_in[n % WM_RING])

            for n in range(2 * WM_PER_PART):
                load_mod(n)
            load(w_in_s, w_in.rearrange("(k p) n -> p k n", p=P), win_in)
            for n in range(2 * WM_PER_PART, 2 * WM_PER_PART + WM_RING):
                load_mod(n)
            sp.wait_ge(w_T, 8)
            load(dft, dft_const, dft_in)
            load(wf_s.rearrange("p (j n) -> p j n", j=FG), w_fourier.rearrange("j c n -> c j n"), dft_in)
            sp.wait_ge(f_done, 2)
            load(w_glu_s, w_glu.rearrange("(k p) n -> p k n", p=P), glu_in)
            for n in range(2 * WM_PER_PART + WM_RING, 6 * WM_PER_PART):
                load_mod(n)
            sp.wait_ge(kk_ready, 1)
            for i in range(4):
                sp.dma_start(kk_dram[8 * i:8 * i + 8].rearrange("g q n -> (g q) n"),
                             KK[:, i].rearrange("p e q -> p (e q)")).then_inc(kk_out, 16)
            sp.wait_ge(kk_out, 64)
            for t in range(T):
                load(M[Q * t:Q * (t + 1)], kk_dram[:, :, Q * (T - 1 - t):Q * (2 * T - 1 - t)].rearrange("g q n -> q g n"), m_in)
            load(w_out_s, w_out.rearrange("(k p) n -> p k n", p=P), wout_in)
            sp.wait_ge(mod_done, 6 * WM_PER_PART)
            load(xr, x.rearrange("(i p) n -> p i n", p=P), xr_in)
            load(posr, pos.rearrange("(i p) n -> p i n", p=P), xr_in)
            load(keys_nat, sub_keys.rearrange("h s k d -> k (h s) d"), keys_in)
            sp.wait_ge(xt_T, 4)
            sp.wait_ge(keys_T, 4)
            sp.wait_ge(s2_act, 2)
            sp.wait_ge(s2_dve, 2)
            load(w_q_s[:, 0:4], peer_w_q[0:D // 2].rearrange("(k p) n -> p k n", p=P), wq_in)
            sp.wait_ge(y_done, 1)
            sp.wait_ge(glu_done, 1)
            load(w_q_s[:, 4:8], peer_w_q[D // 2:D].rearrange("(k p) n -> p k n", p=P), wq_in)
            load(fgb, final_g.partition_broadcast(P), fg_in)
            for i in range(NT):
                sp.wait_ge(out_row, i + 1)
                sp.dma_start(out[P * i:P * (i + 1), :], rowA).then_inc(out_done, 16)
            sp.wait_ge(out_done, 16 * NT)

        @block.tensor
        def _(pe):
            pe.wait_ge(const_in, 16)
            pe.wait_ge(vec_in, 7 * 16)
            nc.tensor.transpose(bank[6][:, 0:V_ROWS], vec_nat, ident[0:V_ROWS, 0:V_ROWS]).then_inc(vec_T, 1)
            pe.wait_ge(lam_in, 3 * 16)
            pe.wait_ge(logdt_spread, 1)
            for r in range(3):
                last = nc.tensor.transpose(bank[7][:, G * r:G * (r + 1)], lam_nat[r], ident[0:G, 0:G])
            last.then_inc(par_T, 1)
            pe.wait_ge(b_in, 2 * 16)
            for r in range(2):
                for q in range(Q):
                    last = nc.tensor.transpose(bank[4 + r][:, G * q:G * (q + 1)],
                                               Bnat[r][:, q:2048:Q], ident[0:G, 0:G])
            last.then_inc(b_T, 1)
            pe.wait_ge(c_in, 4 * 16)
            for r in range(2):
                for i in range(4):
                    last = nc.tensor.transpose(bank[2 + r][:, P * i:P * (i + 1)],
                                               Cnat[r][:, i].rearrange("p d n -> p (d n)"), ident)
            last.then_inc(c_T, 1)

            pe.wait_ge(xn_ready, 4)
            for k in range(KD):
                if k in (2, 3):
                    pe.wait_ge(cs_ready, 2)
                if k >= 4:
                    pe.wait_ge(hraw_act if k % 2 else hraw_dve, k // 2 - 1)
                for tt in range(4):
                    src = (xc if tt < 2 else xl)[:, tt % 2, P * k:P * (k + 1)]
                    last = nc.tensor.transpose(bank[k % 4][:, P * tt:P * (tt + 1)], src, ident)
                last.then_inc(x_T, 1)

            def mod_block(n):
                slot, pi = n % WM_RING, n // WM_PER_PART
                pe.wait_ge(wm_in[slot], 16 * (n // WM_RING + 1))
                if n == 0:
                    pe.wait_ge(cact_ready, 1)
                    pe.wait_ge(vec_ready, 1)
                if n == 2 * WM_PER_PART:
                    pe.wait_ge(par_ready, 1)
                b = bank[6] if pi < 2 else bank[7]
                for j in range(WM_COLS // P):
                    at = 16 * (pi % 2 if pi < 2 else pi - 2) + 2 * ((n % WM_PER_PART) * (WM_COLS // P) + j)
                    for k in range(KD):
                        last = nc.tensor.matmul(b[:, at:at + 2], wm[slot][:, k, P * j:P * (j + 1)],
                                                cact[:, k:16:8], start=(k == 0), stop=(k == KD - 1))
                last.then_inc(mod_done, 1)

            w_batches = [0]

            def w_transpose(ready, count, tmp):
                pe.wait_ge(ready, count)
                if w_batches[0]:
                    pe.wait_ge(w_ready, 2 * w_batches[0])
                else:
                    pe.wait_ge(bb_ready, 1)
                w_batches[0] += 1
                for r in range(2):
                    for gg in range(4):
                        last = nc.tensor.transpose(bank[4 + r][:, P * gg:P * (gg + 1)],
                                                   tmp[:, 1024 * r + P * gg:1024 * r + P * (gg + 1)], ident)
                last.then_inc(w_T, 1)

            for n in range(4):
                mod_block(n)
            w_transpose(wt_dve, 1, dtmp)
            w_transpose(wt_pool, 1, ptmp)
            for n in range(4, 8):
                mod_block(n)
            w_transpose(wt_dve, 2, dtmp)
            w_transpose(wt_pool, 2, ptmp)
            w_transpose(wt_dve, 3, dtmp)
            w_transpose(wt_dve, 4, dtmp)
            w_transpose(wt_pool, 3, ptmp)

            def z_tile(tt):
                for k in range(KD):
                    last = nc.tensor.matmul(bank[tt][:, :], hT[:, k, P * tt:P * (tt + 1)], w_in_s[:, k, 0:SW],
                                            start=(k == 0), stop=(k == KD - 1))
                last.then_inc(z_done, 1)

            def u_transpose(side):
                pe.wait_ge(zg_act, side + 1)
                pe.wait_ge(zg_dve, side + 1)
                lo = 64 + 32 * side
                for g in range(G):
                    last = nc.tensor.transpose(bank[2 * side + g // 16][:, C * (g % 16):C * (g % 16 + 1)],
                                               Z[lo:lo + C, P * g:P * (g + 1)], ident[lo:lo + C, lo:lo + C])
                last.then_inc(u_T, 1)

            def v_products(side):
                pe.wait_ge(u_ready, 2 * (side + 1))
                for b in range(4):
                    n = 4 * side + b
                    if n == 0:
                        pe.wait_ge(w_ready, 16)
                    if n >= 2:
                        pe.wait_ge(vs_act, n - 1)
                        pe.wait_ge(vs_dve, n - 1)
                    for gg in range(8):
                        for r in range(2):
                            at = C * (2 * gg + r)
                            last = nc.tensor.matmul(bank[4 + n % 2][:, at:at + C], W[:, 8 * b + gg, r, :],
                                                    Us[:, 8 * b + gg, C * side:C * (side + 1)], start=True, stop=True)
                    last.then_inc(v_done, 1)

            pe.wait_ge(h_ready, 16)
            pe.wait_ge(win_in, 16)
            z_tile(0)
            z_tile(1)
            z_tile(2)
            w_transpose(wt_pool, 4, ptmp)
            u_transpose(0)
            v_products(0)
            pe.wait_ge(z_evac, 3)
            z_tile(3)
            pe.wait_ge(u_ready, 2)
            for j in range(FG):
                for k in range(KD):
                    last = nc.tensor.matmul(bank[j // 2][:, SEQ * (j % 2):SEQ * (j % 2 + 1)],
                                            w_in_s[:, k, SW + P * j:SW + P * (j + 1)], hT[:, k, SEQ:2 * SEQ],
                                            start=(k == 0), stop=(k == KD - 1))
                if j % 2:
                    last.then_inc(f_done, 1)
            u_transpose(1)
            v_products(1)

            for n in range(8, 12):
                mod_block(n)
            pe.wait_ge(ca_ready, 1)
            pe.wait_ge(vs_act, 8)
            pe.wait_ge(vs_dve, 8)
            for d in range(2):
                rows, first = slice(64 * d, 64 * (d + 1)), 2 * d
                for g in range(G):
                    for r in range(2):
                        last = nc.tensor.matmul(bank[4 + d][:, Q * g:Q * (g + 1)],
                                                CA[r][rows, g, first:first + T, :].rearrange("p s q -> p (s q)"),
                                                Bb[r][rows, g, :], start=(r == 0), stop=(r == 1))
            last.then_inc(k_done, 1)
            pe.wait_ge(dft_in, 2 * 16)
            pe.wait_ge(u_ready, 4)
            for r, m in enumerate((cosC, sinC)):
                nc.tensor.matmul(bank[2 + r][:, :], m, wf_s, start=True, stop=True).then_inc(cw_done, 1)
            pe.wait_ge(k_ready, 2)
            for d in range(2):
                for i in range(4):
                    last = nc.tensor.transpose(bank[4 + d][:, P * i:P * (i + 1)], Kev[d][:, i, :], ident)
            last.then_inc(kt_done, 1)
            pe.wait_ge(f_ready, 2)
            pe.wait_ge(cw_ready, 2)
            for r in range(2):
                for i in range(NT):
                    for j in range(FG):
                        last = nc.tensor.matmul(bank[2 * r + i][:, P * j:P * (j + 1)], fT[:, j, P * i:P * (i + 1)],
                                                CW[r][:, P * j:P * (j + 1)], start=True, stop=True)
                    last.then_inc(gg_done, 1)
            for n in range(12, 16):
                mod_block(n)
            pe.wait_ge(gg_ready, 4)
            for j in range(FG):
                for n, (r, i) in enumerate(((0, 0), (0, 1), (1, 0), (1, 1))):
                    last = nc.tensor.matmul(bank[j // 2][:, SEQ * (j % 2):SEQ * (j % 2 + 1)],
                                            GC[r][:, i, P * j:P * (j + 1)], (cosL, nsinL)[r][:, i, :],
                                            start=(n == 0), stop=(n == 3))
                if j % 2:
                    last.then_inc(fft_done, 1)
            for n in range(16, 24):
                mod_block(n)

            pe.wait_ge(m_in, T * 16)
            pe.wait_ge(s2_act, 2)
            pe.wait_ge(s2_dve, 2)
            for g in range(G):
                j, i = g // 8, g % 8
                o = bank[2 + i // 4][C * j:C * (j + 1), P * (i % 4):P * (i % 4 + 1)]
                nc.tensor.matmul(o, Us[:, g, C:2 * C], M[:, g, :], start=True, stop=False)
                for r in range(2):
                    last = nc.tensor.matmul(o, S2[:, r, g, :], CA[r][:, g, 1:1 + T, :].rearrange("p s q -> p (s q)"),
                                            start=False, stop=(r == 1))
            last.then_inc(y_done, 1)
            pe.wait_ge(kk_copied, 3)
            pe.wait_ge(y_act, 1)
            pe.wait_ge(y_dve, 1)
            for j in range(4):
                for t in range(T):
                    last = nc.tensor.transpose(bank[2 + j][:, C * t:C * (t + 1)], Yc[C * j:C * (j + 1), t, :],
                                               ident[C * j:C * (j + 1), C * j:C * (j + 1)])
            last.then_inc(yt_done, 1)

            def keys_transpose(b):
                if b >= 2:
                    pe.wait_ge(kt_ready, b - 1)
                for i in range(4):
                    last = nc.tensor.transpose(bank[6 + b % 2][:, P * i:P * (i + 1)], keys_nat[:, 4 * b + i, :], ident)
                last.then_inc(keys_T, 1)

            pe.wait_ge(mod_read, 6)
            pe.wait_ge(keys_in, 16)
            keys_transpose(0)
            keys_transpose(1)
            pe.wait_ge(g2y_ready, 1)
            pe.wait_ge(glu_in, 16)
            pe.wait_ge(mix_f, 2)
            for n in range(4):
                for k in range(4):
                    last = nc.tensor.matmul(bank[n // 2][:, SEQ * (n % 2):SEQ * (n % 2 + 1)],
                                            w_glu_s[:, k, P * n:P * (n + 1)], gA[:, k, :], start=(k == 0), stop=(k == 3))
            last.then_inc(glu_done, 1)
            keys_transpose(2)
            keys_transpose(3)
            pe.wait_ge(xr_ready, 1)
            for i in range(NT):
                for b in range(2):
                    if i == 0:
                        pe.wait_ge(kt_ready, 3 + b)
                    else:
                        pe.wait_ge(xt_ready, 1 + b)
                    for k in range(4):
                        last = nc.tensor.transpose(bank[6 + b][:, P * k:P * (k + 1)],
                                                   xr[:, i, P * (4 * b + k):P * (4 * b + k + 1)], ident)
                    last.then_inc(xt_T, 1)

            def out_projection(i):
                for n in range(KD):
                    for k in range(KD):
                        last = nc.tensor.matmul(bank[2 + n // 4][:, P * (n % 4):P * (n % 4 + 1)],
                                                w_out_s[:, k, P * n:P * (n + 1)], mixT[:, k, P * i:P * (i + 1)],
                                                start=(k == 0), stop=(k == KD - 1))
                last.then_inc(o_done, 1)

            def second_norm(i):
                pe.wait_ge(sq_ready, i + 1)
                if i:
                    pe.wait_ge(q_ready, HEADS)
                for k in range(KD):
                    last = nc.tensor.matmul(bank[6][:, 0:1], h2T[:, k, :], ones[:, 0:1], start=(k == 0), stop=(k == KD - 1))
                last.then_inc(ss_done, 1)
                pe.wait_ge(diag2_ready, i + 1)
                nc.tensor.matmul(bank[6][:, P:2 * P], ones, diag2, start=True, stop=True).then_inc(invb_done, 1)
                pe.wait_ge(h2_ready, i + 1)
                for k in range(KD):
                    last = nc.tensor.transpose(bank[2 * i + k // 4][:, P * (k % 4):P * (k % 4 + 1)], h2T[:, k, :], ident)
                last.then_inc(h2_pd, 1)

            def queries(i, h):
                n = HEADS * i + h
                if n >= 2:
                    pe.wait_ge(q_ready, n - 1 if n < HEADS else n)
                for s in range(2):
                    for k in range(KD):
                        at = 2 * P * h + P * s
                        last = nc.tensor.matmul(query_place(n)[:, P * s:P * (s + 1)],
                                                w_q_s[:, k, at:at + P], h2T[:, k, :], start=(k == 0), stop=(k == KD - 1))
                last.then_inc(q_done, 1)

            def scores(i, h):
                n = HEADS * i + h
                pe.wait_ge(q_ready, n + 1)
                if n >= 2:
                    pe.wait_ge(s_ready, n - 1 if n < HEADS else n)
                for s in range(2):
                    last = nc.tensor.matmul(score_place(n)[:, P * s:P * (s + 1)],
                                            qT[:, h % 2, s, :], kT[:, 2 * h + s, :], start=True, stop=True)
                last.then_inc(s_done, 1)

            pe.wait_ge(mix_s5, 1)
            pe.wait_ge(wout_in, 16)
            out_projection(0)
            pe.wait_ge(ones_ready, 1)
            pe.wait_ge(xt_ready, 4)
            second_norm(0)
            pe.wait_ge(wq_in, 2 * 16)
            queries(0, 0)
            for h in range(1, HEADS):
                queries(0, h)
                scores(0, h - 1)
            scores(0, HEADS - 1)
            pe.wait_ge(x1_ready, 1)
            out_projection(1)
            pe.wait_ge(x1_ready, 2)
            for k in range(KD):
                pe.wait_ge(gdiag_ready, k + 1)
                last = nc.tensor.matmul(bank[2 + k // 4][:, P * (k % 4):P * (k % 4 + 1)], ones, gdiag, start=True, stop=True)
                last.then_inc(g2_done, 1)
            pe.wait_ge(g2b_ready, 1)
            second_norm(1)

            def add_up(h_at, h, first, last_head):
                for j in range(TOPK):
                    pe.wait_ge(diag_ready, h_at * TOPK + (j + 1))
                    pe.wait_ge(v_in[j % V_RING], h_at * 32 + 16 * (j // V_RING + 1))
                    for b in range(2):
                        last = nc.tensor.matmul(bank[4 + b][:, :], diag[:, j % 8, :], Vring[:, j % V_RING, 512 * b:512 * (b + 1)],
                                                start=(first and j == 0), stop=(last_head and j == TOPK - 1))
                    last.then_inc(v_used, 1)

            def row_of_x1(i):
                pe.wait_ge(s_ready, 2 * HEADS)
                if i:
                    pe.wait_ge(out_row, 1)
                for k in range(KD):
                    last = nc.tensor.transpose(bank[6 + k // 4][:, P * (k % 4):P * (k % 4 + 1)],
                                               x1T[:, k, P * i:P * (i + 1)], ident)
                last.then_inc(x1r_done, 1)

            for h in range(HEADS):
                queries(1, h)
                scores(1, h)
                if h == 0:
                    pe.wait_ge(s_ready, HEADS)
                add_up(h, h, h == 0, h == HEADS - 1)
            row_of_x1(0)
            pe.wait_ge(y_row, 1)
            add_up(HEADS, 0, True, False)
            with pe.Fori(HEADS + 1, 2 * HEADS - 1) as h:
                add_up(h, None, False, False)
            add_up(2 * HEADS - 1, HEADS - 1, False, True)
            row_of_x1(1)

        @block.vector
        def _(dve):
            v = nc.vector
            ch = Chain(dve, dve_step)
            dve.wait_ge(lam_in, 3 * 16)
            v.tensor_copy(lam_nat[2].rearrange("g (d n) -> g d n", d=2), spread(ld_nat, 2, [G, 2, NS])).then_inc(logdt_spread, 1)
            dve.wait_ge(vec_T, 1)
            v.tensor_copy(vecT, bank[6][:, 0:V_ROWS]).then_inc(vec_ready, 1)
            dve.wait_ge(vec_ready, 1)
            v.tensor_scalar(half_bg, vecT[:, V_BGLU:V_BGLU + 4], 0.5, None, ALU.mult)
            for i in range(4):
                v.tensor_scalar(dE[:, i, :], eyeq, vecT[:, V_D + i:V_D + i + 1], None, ALU.mult)
            dve.wait_ge(silu_th, 1)
            ch.link(v.scalar_tensor_tensor(cact, th_c, 1.0, vecT[:, 0:16], ALU.add, ALU.mult))
            v.tensor_scalar(cact, cact, 0.5, None, ALU.mult).then_inc(cact_ready, 1)
            dve.wait_ge(par_T, 1)
            v.tensor_copy(par, bank[7][:, 0:3 * G].rearrange("p (a g) -> p a g", a=3)).then_inc(par_ready, 1)
            dve.wait_ge(par_ready, 1)
            lr, li = par[:, 0, :], par[:, 1, :]
            dt_, ld_, y1, t0 = (dtmp[:, 32 * n:32 * (n + 1)] for n in range(4))
            cr, ci = dtmp[:, 1920:1952], dtmp[:, 1952:1984]
            A_, B_, C_ = dtmp[:, 128:768], dtmp[:, 768:1408], ptmp[:, 0:640]
            a3, b3 = (z.rearrange("p (s g) -> p s g", s=SLOTS) for z in (A_, B_))
            shape = [P, SLOTS, G]
            dve.wait_ge(dt_ready, 1)
            ch.link(v.tensor_tensor(y1, li, dt_, ALU.mult))
            ch.step(v.tensor_tensor(ld_, lr, dt_, ALU.mult))
            ch.link(v.tensor_scalar(y1, y1, 0.15915494309189535, None, ALU.mult))
            ch.link(v.tensor_scalar(t0, y1, ROUND, ROUND, ALU.add, ALU.subtract))
            ch.link(v.tensor_tensor(y1, y1, t0, ALU.subtract))
            dve.wait_ge(const_in, 16)
            ch.link(v.tensor_tensor(a3, spread(y1, 1, shape), spread(kmul, 2, shape), ALU.mult))
            ch.step(v.tensor_scalar(B_, A_, ROUND, ROUND, ALU.add, ALU.subtract))
            ch.link(v.tensor_scalar(C_, A_, 0.25, None, ALU.add))
            ch.link(v.tensor_tensor(A_, A_, B_, ALU.subtract))
            ch.link(v.tensor_scalar(B_, C_, ROUND, ROUND, ALU.add, ALU.subtract))
            v.tensor_tensor(C_, C_, B_, ALU.subtract).then_inc(trig_in, 1)
            dve.wait_ge(trig_in, 1)
            v.tensor_tensor(b3, spread(ld_, 1, shape), spread(kmul, 2, shape), ALU.mult).then_inc(trig_in, 1)
            dve.wait_ge(trig_out, 3)
            v.tensor_tensor(Pw[0], Pw[0], b3, ALU.mult).then_inc(pw_ready, 1)
            v.tensor_tensor(Pw[1], Pw[1], b3, ALU.mult).then_inc(pw_ready, 1)
            dve.wait_ge(pw_ready, 2)
            for r in range(2):
                v.tensor_copy(Arr[:, r, :], Pw[0][:, 19, :])
                v.tensor_scalar(Aii[:, r, :], Pw[1][:, 19, :], (1.0, -1.0)[r], None, ALU.mult)
            ar, ai = t0, Pw[1][:, 18, :]
            den, t1, t2 = y1, dt_, ld_
            ch.step(v.tensor_scalar(ar, Pw[0][:, 18, :], -1.0, None, ALU.add))
            ch.step(v.tensor_tensor(den, lr, lr, ALU.mult))
            ch.link(v.tensor_tensor(t1, li, li, ALU.mult))
            ch.link(v.tensor_tensor(den, den, t1, ALU.add))
            ch.link(v.reciprocal(den, den))
            ch.step(v.tensor_tensor(t1, ar, lr, ALU.mult))
            ch.link(v.tensor_tensor(t2, ai, li, ALU.mult))
            ch.link(v.tensor_tensor(t1, t1, t2, ALU.add))
            ch.link(v.tensor_tensor(cr, t1, den, ALU.mult))
            ch.step(v.tensor_tensor(t1, ai, lr, ALU.mult))
            ch.link(v.tensor_tensor(t2, ar, li, ALU.mult))
            ch.link(v.tensor_tensor(t1, t1, t2, ALU.subtract))
            ch.link(v.tensor_tensor(ci, t1, den, ALU.mult))
            dve.wait_ge(b_T, 1)
            gq = [P, G, Q]
            br, bi = (bank[4 + r][:, :].rearrange("p (q g) -> p g q", q=Q) for r in range(2))
            m1, m2 = (dtmp[:, 128 + 512 * n:640 + 512 * n].rearrange("p (g q) -> p g q", g=G) for n in range(2))
            cr3, ci3 = spread(cr, 2, gq), spread(ci, 2, gq)
            ch.step(v.tensor_tensor(m1, br, cr3, ALU.mult))
            ch.link(v.tensor_tensor(m2, bi, ci3, ALU.mult))
            ch.link(v.tensor_tensor(Bb[0], m1, m2, ALU.subtract))
            ch.step(v.tensor_tensor(m1, bi, cr3, ALU.mult))
            ch.link(v.tensor_tensor(m2, br, ci3, ALU.mult))
            v.tensor_tensor(Bb[1], m1, m2, ALU.add).then_inc(bb_ready, 1)
            dve.wait_ge(bb_ready, 1)

            dve.wait_ge(xl_in, 32)
            v.tensor_tensor(xl[:, :, :], xl[:, :, :], pl[:, :, :], ALU.add).then_inc(x_pos, 1)

            def w_batch(n):
                g0 = 4 * n
                if n:
                    dve.wait_ge(w_T, (0, 1, 3, 5)[n])
                w4 = [P, 4, T, Q]
                for r in range(2):
                    ta, tb = (dtmp[:, 1024 * r + 512 * z:1024 * r + 512 * z + 512].rearrange("p (g t q) -> p g t q", g=4, t=T) for z in range(2))
                    pr, pi = (spread(Pw[z][:, 10:18, g0:g0 + 4].rearrange("p s g -> p g s"), 3, w4) for z in range(2))
                    b0, b1 = (spread(Bb[z][:, g0:g0 + 4, :], 2, w4) for z in range(2))
                    ch.step(v.tensor_tensor(ta, pr, (b0, b1)[r], ALU.mult))
                    ch.link(v.tensor_tensor(tb, pi, (b1, b0)[r], ALU.mult))
                    last = v.tensor_tensor(ta, ta, tb, (ALU.subtract, ALU.add)[r])
                    if r == 0:
                        ch.step(last)
                ch.after()
                last.then_inc(wt_dve, 1)

            def mean_square(n, total, cols):
                v.tensor_scalar(ms[:, 0:cols], total, 1.0 / D, EPS, ALU.mult, ALU.add).then_inc(ms_ready, 1)

            def inverse_root(n, out_, cols):
                m, r, q = ms[:, 0:cols], root[:, 0:cols], newton[:, 0:cols]
                dve.wait_ge(root_ready, n)
                ch.link(v.reciprocal(r, r))
                ch.link(v.tensor_tensor(q, r, r, ALU.mult))
                ch.link(v.tensor_tensor(q, q, m, ALU.mult))
                ch.link(v.tensor_scalar(q, q, -0.5, 1.5, ALU.mult, ALU.add))
                ch.link(v.tensor_tensor(out_, r, q, ALU.mult))

            w_batch(0)
            dve.wait_ge(ss_ready, 4)
            mean_square(1, ss, 4)
            inverse_root(1, inv, 4)
            for tt in range(4):
                src = (xc if tt < 2 else xl)[:, tt % 2, :]
                v.tensor_scalar(src, src, inv[:, tt:tt + 1], None, ALU.mult).then_inc(xn_ready, 1)
            for k in range(0, KD, 2):
                dve.wait_ge(x_T, k + 1)
                v.tensor_copy(hT[:, k, :], bank[k % 4][:, :]).then_inc(hraw_dve, 1)
            w_batch(1)
            w_batch(2)

            def mod_out(first, parts, read):
                for n in range(parts):
                    part = PART_ORDER[first + n]
                    src = bank[6 if first < 2 else 7][:, 16 * n:16 * (n + 1)].rearrange("p (k w) -> p k w", k=KD)
                    bias = spread(vecT[:, V_BMOD + KD * part:V_BMOD + KD * (part + 1)], 2, [P, KD, 2])
                    v.tensor_tensor(modS[:, part], src, bias, ALU.add).then_inc(mod_read, read)

            dve.wait_ge(mod_done, 8)
            mod_out(0, 2, 1)
            dve.wait_ge(mod_read, 2)
            ch.link(v.scalar_tensor_tensor(Gn1, modS[:, SC1], 1.0, spread(vecT[:, V_N1:V_N1 + KD], 2, [P, KD, 2]), ALU.add, ALU.mult))
            dve.wait_ge(hraw_act, 4)
            dve.wait_ge(hraw_dve, 4)
            for k in range(KD):
                for w in (1, 0):
                    at = hT[:, k, SEQ * (1 - w):SEQ * (2 - w)]
                    v.tensor_scalar(at, at, Gn1[:, k, w:w + 1], modS[:, SH1, k, w:w + 1], ALU.mult, ALU.add).then_inc(h_ready, 1)
            w_batch(3)

            def ca_batch(n):
                g0 = 4 * n
                if n == 0:
                    dve.wait_ge(cs_ready, 2)
                    dve.wait_ge(w_T, 6)
                c4 = [P, 4, 10, Q]
                pr, pi = (spread(Pw[z][:, 0:10, g0:g0 + 4].rearrange("p s g -> p g s"), 3, c4) for z in range(2))
                c0, c1 = (spread(Cs[z][:, g0:g0 + 4, :], 2, c4) for z in range(2))
                ta, tb = (dtmp[:, 640 * z:640 * z + 640].rearrange("p (g s q) -> p g s q", g=4, s=10) for z in range(2))
                ch.step(v.tensor_tensor(ta, pr, c0, ALU.mult))
                ch.link(v.tensor_tensor(tb, pi, c1, ALU.mult))
                ch.link(v.tensor_tensor(CA[0][:, g0:g0 + 4], ta, tb, ALU.subtract))
                fa, fb = dtmp[:, 0:640], dtmp[:, 640:1280]
                ch.step(v.tensor_tensor(ta, pr, c1, ALU.mult))
                ch.link(v.tensor_tensor(tb, pi, c0, ALU.mult))
                last = v.scalar_tensor_tensor(CA[1][:, g0:g0 + 4].rearrange("p g s q -> p (g s q)"), fa, -1.0, fb, ALU.mult, ALU.subtract)
                if n == 7:
                    last.then_inc(ca_ready, 1)
                else:
                    ch.link(last)

            def z_permute(side):
                dve.wait_ge(zc_in[side], 32)
                lo = C * side
                src = Z[lo:lo + C, :].rearrange("p (t g q) -> p g t q", t=T, g=G)
                dst = Z[64 + lo:64 + lo + C, :].rearrange("p (g t q) -> p g t q", g=G, t=T)
                v.tensor_copy(dst[:, 0:16], src[:, 0:16]).then_inc(zg_dve, 1)

            def v_backward(side):
                vs = (VSc, VSl)[side]
                if side:
                    dve.wait_ge(f_done, 2)
                for b in range(4):
                    n = 4 * side + b
                    dve.wait_ge(v_done, n + 1)
                    if side == 0:
                        dve.wait_ge(zc_in[0], 32)
                        dve.wait_ge(z_evac, 3)
                        dve.wait_ge(zc_in[1], 16)
                    src = bank[4 + n % 2][64:128, :].rearrange("p (g r c) -> p r g c", g=8, r=2)
                    for r in range(2):
                        last = v.tensor_copy(vs[64:128, :, r, 8 * b:8 * b + 8].rearrange("p c g -> p g c"), src[:, r, :, ::-1])
                    last.then_inc(vs_dve, 1)

            scratch1, scratch2 = (dtmp[:, 64 * z:64 * (z + 1)].rearrange("p (r g) -> p r g", r=2) for z in range(2))

            def advance(prev, cur, base):
                v.tensor_tensor(scratch1, prev, Arr, ALU.mult).then_inc(scan_step, 1)
                v.tensor_tensor(scratch2, prev, Aii, ALU.mult).then_inc(scan_step, 1)
                dve.wait_ge(scan_step, base + 1)
                v.tensor_tensor(cur, cur, scratch1, ALU.add).then_inc(scan_step, 1)
                dve.wait_ge(scan_step, base + 3)
                v.tensor_tensor(cur, cur, scratch2[:, ::-1, :], ALU.add).then_inc(scan_step, 1)
                dve.wait_ge(scan_step, base + 4)

            for n in range(5):
                ca_batch(n)
            z_permute(0)
            ca_batch(5)
            ca_batch(6)
            ca_batch(7)
            v_backward(0)
            dve.wait_ge(ca_ready, 1)
            dve.wait_ge(vs_act, 4)
            dve.wait_ge(vs_dve, 4)
            with dve.Fori(1, C // 2) as j:
                advance(VSc[:, bass.ds(j - 1, 1)][:, 0], VSc[:, bass.ds(j, 1)][:, 0], (j - 1) * 4)
            z_permute(1)
            with dve.Fori(C // 2, C) as j:
                advance(VSc[:, bass.ds(j - 1, 1)][:, 0], VSc[:, bass.ds(j, 1)][:, 0], (j - 1) * 4)
            v_backward(1)
            dve.wait_ge(vs_act, 8)
            dve.wait_ge(vs_dve, 8)
            advance(VSc[:, C - 1], VSl[:, 0], 4 * (C - 1))
            with dve.Fori(1, C) as j:
                advance(VSl[:, bass.ds(j - 1, 1)][:, 0], VSl[:, bass.ds(j, 1)][:, 0], j * 4 + 4 * (C - 1))
            v.tensor_copy(S2[64:128, :, :, C - 1], VSc[64:128, C - 1]).then_inc(s2_dve, 1)
            for r in range(2):
                last = v.tensor_copy(S2[64:128, r, :, 0:C - 1], VSl[64:128, 0:C - 1, r][:, ::-1, :].rearrange("p c g -> p g c"))
            last.then_inc(s2_dve, 1)
            dve.wait_ge(w_T, 8)
            v.memset(ones, 1.0).then_inc(ones_ready, 1)
            dve.wait_ge(mod_done, 24)
            mod_out(2, 4, 1)
            dve.wait_ge(mod_read, 6)
            ch.link(v.scalar_tensor_tensor(Gn2, modS[:, SC2, :, 0], 1.0, vecT[:, V_N2:V_N2 + KD], ALU.add, ALU.mult))
            dve.wait_ge(y_done, 1)
            dve.wait_ge(fft_done, 2)
            v.tensor_copy(Yc.rearrange("p t (i q) -> p i t q", q=Q)[:, 4:8],
                          bank[3][:, :].rearrange("p (i t q) -> p i t q", i=4, t=T)).then_inc(y_dve, 1)
            dve.wait_ge(yt_done, 1)
            dve.wait_ge(f_done, 2)
            for j in range(2):
                last = v.tensor_copy(gA[:, 2 + j, :].rearrange("p (c t) -> p c t", t=T),
                                     bank[4 + j][:, 0:SEQ].rearrange("p (t c) -> p c t", t=T))
            last.then_inc(yn_dve, 1)
            dve.wait_ge(yn_dve, 1)
            dve.wait_ge(yn_act, 1)
            dve.wait_ge(y_sq, 1)
            ch.link(v.tensor_scalar(gB, gB, GELU_K * GELU_C, GELU_K, ALU.mult, ALU.add))
            v.tensor_tensor(gB, gB, gA, ALU.mult).then_inc(y_arg, 1)
            dve.wait_ge(y_th, 1)
            v.scalar_tensor_tensor(gA, gB, 1.0, gA, ALU.add, ALU.mult).then_inc(g2y_ready, 1)
            dve.wait_ge(glu_th, 4)
            dve.wait_ge(g2y_ready, 1)
            ch.link(v.tensor_scalar(gB, gB, 0.25, 0.25, ALU.mult, ALU.add))
            v.tensor_tensor(mixT[:, 0:4, :], gB, gA, ALU.mult).then_inc(mix_s5, 1)

            def residual(i):
                at = slice(P * i, P * (i + 1))
                dve.wait_ge(o_done, i + 1)
                dve.wait_ge(xt_ready, 4)
                for n in range(KD):
                    last = v.scalar_tensor_tensor(x1T[:, n, at], bank[2 + n // 4][:, P * (n % 4):P * (n % 4 + 1)],
                                                  modS[:, G1, n, 0:1], x1T[:, n, at], ALU.mult, ALU.add)
                last.then_inc(x1_ready, 1)

            def norm_two(i):
                at = slice(P * i, P * (i + 1))
                dve.wait_ge(ss_done, i + 1)
                mean_square(2 + i, bank[6][:, 0:1], 1)
                inverse_root(2 + i, inv[:, 0:1], 1)
                v.tensor_scalar(diag2, ident, inv[:, 0:1], None, ALU.mult).then_inc(diag2_ready, 1)
                dve.wait_ge(invb_done, i + 1)
                ch.link(v.tensor_tensor(h2T[:, :, :], spread(bank[6][:, P:2 * P], 1, [P, KD, P]), x1T[:, :, at], ALU.mult))
                for k in range(KD):
                    last = v.tensor_scalar(h2T[:, k, :], h2T[:, k, :], Gn2[:, k:k + 1], modS[:, SH2, k, 0:1], ALU.mult, ALU.add)
                last.then_inc(h2_ready, 1)

            def top_k(n, h, base):
                k = [0]

                def link(ins, wait=True):
                    ins.then_inc(dve_step, 1)
                    k[0] += 1
                    if wait:
                        wait_alone(dve, dve_step, base + k[0], dve_passed)

                wait_alone(dve, s_ready, n + 1, dve_passed)
                hs = wrk.rearrange("p (s n) -> p s n", s=2)
                link(v.tensor_copy(hs, sc[:, h] if isinstance(h, int) else sc[:, bass.ds(h, 1)][:, 0]))
                for s in range(2):
                    link(v.max(sv[:, s, 0:8], hs[:, s]))
                    link(v.max_index(si[:, s, 0:8], sv[:, s, 0:8], hs[:, s]), False)
                    link(v.match_replace(wrk1[:, s], sv[:, s, 0:8], hs[:, s], LOWEST))
                    link(v.max(sv[:, s, 8:16], wrk1[:, s]))
                    link(v.max_index(si[:, s, 8:16], sv[:, s, 8:16], wrk1[:, s]))
                sq = [P, TOPK, TOPK]
                c3 = cand.rearrange("p (a b) -> p a b", a=TOPK)
                w3 = wrk.rearrange("p (a b) -> p a b", a=TOPK)
                link(v.tensor_copy(sif, si), False)
                link(v.tensor_tensor(c3, spread(sv[:, 0, :], 2, sq), spread(sv[:, 1, :], 1, sq), ALU.add))
                link(v.max(best[:, 0:8], cand))
                link(v.max_index(flat[:, 0:8], best[:, 0:8], cand), False)
                link(v.match_replace(wrk, best[:, 0:8], cand, LOWEST))
                link(v.max(best[:, 8:16], wrk))
                link(v.max_index(flat[:, 8:16], best[:, 8:16], wrk))
                eh = e_all[:, bass.ds(n * TOPK, TOPK)]
                v.tensor_scalar(eh, best, best[:, 0:1], None, ALU.subtract).then_inc(top_ready, 1)
                link(v.tensor_scalar(fij[:, 0, :], flat, 4, None, ALU.logical_shift_right), False)
                link(v.tensor_scalar(fij[:, 1, :], flat, 15, None, ALU.bitwise_and))
                link(v.tensor_copy(fijf, fij))
                io = spread(iota16, 1, sq)
                link(v.tensor_tensor(c3, spread(fijf[:, 0, :], 2, sq), io, ALU.is_equal), False)
                link(v.tensor_tensor(w3, spread(fijf[:, 1, :], 2, sq), io, ALU.is_equal))
                link(v.tensor_scalar(sif[:, 0, :], sif[:, 0, :], float(KEYS), None, ALU.mult))
                link(v.tensor_tensor(c3, c3, spread(sif[:, 0, :], 1, sq), ALU.mult), False)
                link(v.tensor_tensor(w3, w3, spread(sif[:, 1, :], 1, sq), ALU.mult))
                link(v.tensor_tensor(cand, cand, wrk, ALU.add))
                link(v.tensor_reduce(pick, c3, AX, ALU.add))
                wait_alone(dve, top_ready, n + 1, dve_passed)
                v.tensor_copy(idx_all[:, bass.ds(n * TOPK, TOPK)], pick).then_inc(idx_ready, 1)
                dve.wait_ge(idx_ready, n + 1)
                return k[0]

            def dot_products(n, tile, base):
                k = [0]

                def link(ins, wait=True):
                    ins.then_inc(dve_step, 1)
                    k[0] += 1
                    if wait:
                        wait_alone(dve, dve_step, base + k[0], dve_passed)

                h2 = bank_pair[tile]
                dd = dots[:, 0, :]
                for j in range(TOPK):
                    dve.wait_ge(u_in[j % U_RING], n * 32 + 16 * (j // U_RING + 1))
                    ur = Uring[:, j % U_RING, :]
                    v.scalar_tensor_tensor(ur, ur, 1.0, h2, ALU.mult, ALU.mult, accum_out=dd[:, j:j + 1]).then_inc(u_used, 1)
                dve.wait_ge(u_used, n * TOPK + TOPK)
                link(v.tensor_tensor(garg, dd, dd, ALU.mult))
                link(v.tensor_scalar(garg, garg, GELU_K * GELU_C, GELU_K, ALU.mult, ALU.add))
                v.tensor_tensor(garg, garg, dd, ALU.mult).then_inc(garg_ready, 1)
                wait_alone(dve, exp_ready, n + 1, dve_passed)
                link(v.reciprocal(rsum[:, 0:1], esum[:, bass.ds(n, 1)]))
                link(v.tensor_scalar(rsum[:, 1:2], rsum[:, 0:1], 0.5, None, ALU.mult), False)
                link(v.tensor_tensor(dd, dd, e_all[:, bass.ds(n * TOPK, TOPK)], ALU.mult))
                dve.wait_ge(gth_ready, n + 1)
                link(v.scalar_tensor_tensor(dd, gth, 1.0, dd, ALU.add, ALU.mult))
                v.tensor_scalar(wgt[:, bass.ds(n * TOPK, TOPK)], dd, rsum[:, 1:2], None, ALU.mult).then_inc(wgt_ready, 1)
                dve.wait_ge(wgt_ready, n + 1)
                return k[0]

            def finish(i):
                dve.wait_ge(v_used, TOPK * HEADS * (i + 1))
                dve.wait_ge(x1r_done, i + 1)
                if i:
                    dve.wait_ge(out_done, 16)
                for b in range(2):
                    last = v.tensor_tensor(rowB[:, 512 * b:512 * (b + 1)], bank[4 + b][:, :], g2b[:, 512 * b:512 * (b + 1)], ALU.mult)
                    ch.step(last)
                ch.after()
                for b in range(2):
                    last = v.tensor_tensor(rowB[:, 512 * b:512 * (b + 1)], rowB[:, 512 * b:512 * (b + 1)], bank[6 + b][:, :], ALU.add)
                last.then_inc(y_row, 1)
                dve.wait_ge(fin_ss, i + 1)
                mean_square(4 + i, ss[:, 0:1], 1)
                inverse_root(4 + i, inv[:, 0:1], 1)
                dve.wait_ge(fg_in, 16)
                v.scalar_tensor_tensor(rowA, rowB, inv[:, 0:1], fgb, ALU.mult, ALU.mult).then_inc(out_row, 1)

            bank_pair = [None, None]
            for i in range(NT):
                bank_pair[i] = psum[:, D * i:D * (i + 1)]
            residual(0)
            norm_two(0)
            dve.wait_ge(h2_pd, 1)
            ch.n += top_k(0, 0, ch.n)
            ch.n += top_k(1, 1, ch.n)
            ch.n += dot_products(0, 0, ch.n)
            residual(1)
            for k in range(KD):
                if k:
                    dve.wait_ge(g2_done, k)
                v.tensor_scalar(gdiag, ident, modS[:, G2, k, 0:1], None, ALU.mult).then_inc(gdiag_ready, 1)
            dve.wait_ge(g2_done, KD)
            for b in range(2):
                last = v.tensor_copy(g2b[:, 512 * b:512 * (b + 1)], bank[2 + b][:, :])
            last.then_inc(g2b_ready, 1)
            norm_two(1)
            ch.n += top_k(2, 2, ch.n)
            n0, per = ch.n, 34
            with dve.Fori(1, HEADS - 2) as h:
                a = dot_products(h, 0, (h - 1) * per + n0)
                b_ = top_k(h + 2, h + 2, (h - 1) * per + (n0 + a))
                assert a + b_ == per, (a, b_)
            n0 += per * (HEADS - 3)
            dve.wait_ge(h2_pd, 2)
            with dve.Fori(HEADS - 2, HEADS) as h:
                a = dot_products(h, 0, (h - (HEADS - 2)) * per + n0)
                top_k(h + 2, h - (HEADS - 2), (h - (HEADS - 2)) * per + (n0 + a))
            n0 += 2 * per
            ch.n = n0
            ch.n += dot_products(HEADS, 1, ch.n)
            ch.n += top_k(HEADS + 2, 2, ch.n)
            finish(0)
            n0 = ch.n
            with dve.Fori(HEADS + 1, 2 * HEADS - 2) as h:
                a = dot_products(h, 1, (h - (HEADS + 1)) * per + n0)
                top_k(h + 2, h - (HEADS - 2), (h - (HEADS + 1)) * per + (n0 + a))
            ch.n = n0 + per * (HEADS - 3)
            for h in range(2 * HEADS - 2, 2 * HEADS):
                ch.n += dot_products(h, 1, ch.n)
            finish(1)

        @block.scalar
        def _(act):
            a = nc.scalar
            ch = Chain(act, act_step)
            for r, t in enumerate((b_re, b_im)):
                act.dma_start(Bnat[r].rearrange("g (d m) -> g d m", d=2), t.rearrange("d g n q -> g d (n q)")).then_inc(b_in, 16)
            for r, t in enumerate((c_re, c_im)):
                for d in range(2):
                    act.dma_start(Cnat[r][:, :, d, :], t[d].rearrange("(i g) q n -> (g q) i n", g=8)).then_inc(c_in, 16)
            act.wait_ge(vec_ready, 1)
            a.activation(th_c, vecT[:, 0:16], ACT.Tanh, scale=0.5).then_inc(silu_th, 1)
            act.wait_ge(par_ready, 1)
            a.activation(dtmp[:, 0:32], par[:, 2, :], ACT.Exp).then_inc(dt_ready, 1)
            act.wait_ge(trig_in, 1)
            a.activation(Pw[1].rearrange("p s g -> p (s g)"), dtmp[:, 128:768], ACT.Sin, scale=TWO_PI).then_inc(trig_out, 1)
            a.activation(Pw[0].rearrange("p s g -> p (s g)"), ptmp[:, 0:640], ACT.Sin, scale=TWO_PI).then_inc(trig_out, 1)
            act.wait_ge(trig_in, 2)
            a.activation(dtmp[:, 768:1408], dtmp[:, 768:1408], ACT.Exp).then_inc(trig_out, 1)
            act.wait_ge(c_T, 1)
            for r in range(2):
                a.copy(Cs[r].rearrange("p g q -> p (g q)"), bank[2 + r][:, :]).then_inc(cs_ready, 1)
            act.wait_ge(xc_in, 16)
            for tt in range(4):
                if tt == 2:
                    act.wait_ge(x_pos, 1)
                if tt:
                    act.wait_ge(ss_ready, tt)
                a.activation(junk, (xc if tt < 2 else xl)[:, tt % 2, :], ACT.Square, accum_out=ss[:, tt:tt + 1]).then_inc(ss_ready, 1)

            def square_root(n, cols):
                act.wait_ge(ms_ready, n)
                a.activation(root[:, 0:cols], ms[:, 0:cols], ACT.Sqrt).then_inc(root_ready, 1)

            square_root(1, 4)
            for k in range(1, KD, 2):
                act.wait_ge(x_T, k + 1)
                a.copy(hT[:, k, :], bank[k % 4][:, :]).then_inc(hraw_act, 1)

            def w_out_of_psum(n, g0):
                act.wait_ge(w_T, n + 1)
                for r in range(2):
                    a.copy(W[:, g0:g0 + 4, r, :], bank[4 + r][:, :].rearrange("p (g n) -> p g n", g=4)).then_inc(w_ready, 1)

            for n, g0 in enumerate((0, 16, 4, 20, 8, 12, 24)):
                w_out_of_psum(n, g0)

            def z_out(tt):
                act.wait_ge(z_done, tt + 1)
                if tt == 3:
                    act.wait_ge(ca_ready, 1)
                a.copy(zrow[tt], bank[tt][:, :]).then_inc(z_evac, 1)
                act.wait_ge(z_evac, tt + 1)
                lo = C * (tt // 2) + 16 * (tt % 2)
                act.dma_start(Z[lo:lo + 16, :].rearrange("c (t n) -> c t n", t=T), zrow[tt]).then_inc(zc_in[tt // 2], 16)

            def z_permute(side):
                act.wait_ge(zc_in[side], 32)
                lo = C * side
                src = Z[lo:lo + C, :].rearrange("p (t g q) -> p g t q", t=T, g=G)
                dst = Z[64 + lo:64 + lo + C, :].rearrange("p (g t q) -> p g t q", g=G, t=T)
                a.copy(dst[:, 16:32], src[:, 16:32]).then_inc(zg_act, 1)

            def u_out(side):
                act.wait_ge(u_T, side + 1)
                for b in range(2):
                    a.copy(Us[:, 16 * b:16 * (b + 1), C * side:C * (side + 1)],
                           bank[2 * side + b][:, :].rearrange("p (g c) -> p g c", g=16)).then_inc(u_ready, 1)

            def v_forward(side):
                vs = (VSc, VSl)[side]
                for b in range(4):
                    n = 4 * side + b
                    act.wait_ge(v_done, n + 1)
                    if n == 0:
                        act.wait_ge(zc_in[1], 16)
                    src = bank[4 + n % 2][0:64, :].rearrange("p (g r c) -> p g r c", g=8, r=2)
                    for r in range(2):
                        last = a.copy(vs[0:64, :, r, 8 * b:8 * b + 8].rearrange("p c g -> p g c"), src[:, :, r, :])
                    last.then_inc(vs_act, 1)

            z_out(0)
            z_out(1)
            z_out(2)
            w_out_of_psum(7, 28)
            z_permute(0)
            u_out(0)
            v_forward(0)
            z_out(3)
            z_permute(1)
            for b in range(2):
                act.wait_ge(f_done, b + 1)
                a.copy(fT[:, 2 * b:2 * b + 2, :], bank[b][:, :].rearrange("p (j n) -> p j n", j=2)).then_inc(f_ready, 1)
            u_out(1)
            v_forward(1)
            act.wait_ge(k_done, 1)
            for d in range(2):
                a.copy(Kev[d].rearrange("p i n -> p (i n)"), bank[4 + d][:, :]).then_inc(k_ready, 1)
            for r in range(2):
                act.wait_ge(cw_done, r + 1)
                a.copy(CW[r], bank[2 + r][:, :]).then_inc(cw_ready, 1)
            act.wait_ge(kt_done, 1)
            back, fwd = (bank[5 - d][:, :].rearrange("p (i e q) -> p i e q", i=4, e=T) for d in range(2))
            a.copy(KK[:, :, 0:T, :], back).then_inc(kk_copied, 1)
            a.copy(KK[:, :, T:2 * T - 1, :], fwd[:, :, 1:T, :]).then_inc(kk_copied, 1)
            a.copy(Ktmp, fwd[:, :, 0, :]).then_inc(kk_copied, 1)
            for r in range(2):
                for i in range(NT):
                    act.wait_ge(gg_done, 2 * r + i + 1)
                    if r == 0 and i == 0:
                        act.wait_ge(u_T, 2)
                    a.copy(GC[r][:, i, :], bank[2 * r + i][:, :]).then_inc(gg_ready, 1)
            for b in range(2):
                act.wait_ge(fft_done, b + 1)
                a.copy(mixT[:, 4 + 2 * b:6 + 2 * b, :], bank[b][:, :].rearrange("p (j n) -> p j n", j=2)).then_inc(mix_f, 1)
            act.wait_ge(scan_step, 4 * (2 * C - 1))
            a.copy(S2[0:64, :, :, 0], VSc[0:64, C - 1]).then_inc(s2_act, 1)
            for r in range(2):
                last = a.copy(S2[0:64, r, :, 1:C], VSl[0:64, 0:C - 1, r].rearrange("p c g -> p g c"))
            last.then_inc(s2_act, 1)
            act.wait_ge(y_done, 1)
            a.copy(Yc.rearrange("p t (i q) -> p i t q", q=Q)[:, 0:4],
                   bank[2][:, :].rearrange("p (i t q) -> p i t q", i=4, t=T)).then_inc(y_act, 1)
            act.wait_ge(yt_done, 1)
            for j in range(2):
                last = a.copy(gA[:, j, :].rearrange("p (c t) -> p c t", t=T),
                              bank[2 + j][:, 0:SEQ].rearrange("p (t c) -> p c t", t=T))
            last.then_inc(yn_act, 1)
            act.wait_ge(yn_act, 1)
            act.wait_ge(yn_dve, 1)
            a.activation(gB, gA, ACT.Square).then_inc(y_sq, 1)

            def keys_out(b):
                act.wait_ge(keys_T, b + 1)
                a.copy(kT[:, 4 * b:4 * b + 4, :], bank[6 + b % 2][:, :].rearrange("p (h n) -> p h n", h=4)).then_inc(kt_ready, 1)

            keys_out(0)
            keys_out(1)
            act.wait_ge(y_arg, 1)
            a.activation(gB, gB, ACT.Tanh).then_inc(y_th, 1)
            act.wait_ge(glu_done, 1)
            for n in range(4):
                a.activation(gB[:, n, :], bank[n // 2][:, SEQ * (n % 2):SEQ * (n % 2 + 1)], ACT.Tanh,
                             bias=half_bg[:, n:n + 1], scale=0.25).then_inc(glu_th, 1)
            keys_out(2)
            keys_out(3)
            for n in range(4):
                i, b = n // 2, n % 2
                act.wait_ge(xt_T, n + 1)
                a.copy(x1T[:, 4 * b:4 * b + 4, P * i:P * (i + 1)],
                       bank[6 + b][:, :].rearrange("p (k n) -> p k n", k=4)).then_inc(xt_ready, 1)

            def squares(i):
                act.wait_ge(x1_ready, i + 1)
                if i:
                    act.wait_ge(q_done, HEADS)
                a.activation(h2T[:, :, :], x1T[:, :, P * i:P * (i + 1)], ACT.Square).then_inc(sq_ready, 1)

            def query_out(n):
                act.wait_ge(q_done, n + 1)
                if n >= 2:
                    act.wait_ge(s_done, n - 1)
                w = n % 2
                a.copy(qT[:, w], query_place(n).rearrange("p (s n) -> p s n", s=2)).then_inc(q_ready, 1)

            def scores_out(n):
                act.wait_ge(s_done, n + 1)
                if n == 0:
                    act.wait_ge(mix_s5, 1)
                if n >= HEADS:
                    act.wait_ge(idx_ready, n - HEADS + 1)
                a.copy(sc[:, n % HEADS], score_place(n).rearrange("p (s n) -> p s n", s=2)).then_inc(s_ready, 1)

            def softmax_exp(n):
                wait_alone(act, top_ready, n + 1, act_passed)
                eh = e_all[:, bass.ds(n * TOPK, TOPK)]
                a.activation(eh, eh, ACT.Exp, accum_out=esum[:, bass.ds(n, 1)]).then_inc(exp_ready, 1)

            def gelu_tanh(n):
                act.wait_ge(garg_ready, n + 1)
                a.activation(gth, garg, ACT.Tanh).then_inc(gth_ready, 1)

            def diagonals(n):
                wait_alone(act, wgt_ready, n + 1, act_passed)
                for j in range(TOPK):
                    if not (isinstance(n, int) and n == 0 and j < 8):
                        wait_alone(act, v_used, n * TOPK + (j - 7), act_passed)
                    a.activation(diag[:, j % 8, :], ident, ACT.Copy, scale=wgt[:, bass.ds(n * TOPK + j, 1)]).then_inc(diag_ready, 1)

            def row_squares(i):
                act.wait_ge(y_row, i + 1)
                a.activation(rowA, rowB, ACT.Square, accum_out=ss[:, 0:1]).then_inc(fin_ss, 1)

            squares(0)
            square_root(2, 1)
            query_out(0)
            for n in range(1, HEADS):
                query_out(n)
                scores_out(n - 1)
            scores_out(HEADS - 1)
            softmax_exp(0)
            softmax_exp(1)
            gelu_tanh(0)
            squares(1)
            square_root(3, 1)
            for h in range(HEADS):
                query_out(HEADS + h)
                scores_out(HEADS + h)
                diagonals(h)
                softmax_exp(h + 2)
                gelu_tanh(h + 1)
            row_squares(0)
            square_root(4, 1)
            diagonals(HEADS)
            softmax_exp(HEADS + 2)
            gelu_tanh(HEADS + 1)
            with act.Fori(HEADS + 1, 2 * HEADS - 2) as h:
                diagonals(h)
                softmax_exp(h + 2)
                gelu_tanh(h + 1)
            diagonals(2 * HEADS - 2)
            gelu_tanh(2 * HEADS - 1)
            diagonals(2 * HEADS - 1)
            row_squares(1)
            square_root(5, 1)

        @block.gpsimd
        def _(pool):
            g_ = nc.gpsimd
            ch = Chain(pool, pool_step)
            pool.wait_ge(pw_ready, 2)
            pool.wait_ge(bb_ready, 1)
            w4 = [P, 4, T, Q]
            for n in range(4):
                g0 = 16 + 4 * n
                if n:
                    pool.wait_ge(w_T, (0, 2, 4, 7)[n])
                for r in range(2):
                    ta, tb = (ptmp[:, 1024 * r + 512 * z:1024 * r + 512 * z + 512].rearrange("p (g t q) -> p g t q", g=4, t=T) for z in range(2))
                    pr, pi = (spread(Pw[z][:, 10:18, g0:g0 + 4].rearrange("p s g -> p g s"), 3, w4) for z in range(2))
                    b0, b1 = (spread(Bb[z][:, g0:g0 + 4, :], 2, w4) for z in range(2))
                    ch.step(g_.tensor_tensor(ta, pr, (b0, b1)[r], ALU.mult))
                    ch.link(g_.tensor_tensor(tb, pi, (b1, b0)[r], ALU.mult))
                    last = g_.tensor_tensor(ta, ta, tb, (ALU.subtract, ALU.add)[r])
                    if r == 0:
                        ch.step(last)
                ch.after()
                last.then_inc(wt_pool, 1)
            pool.wait_ge(kk_copied, 3)
            ch.link(g_.tensor_tensor(KK[:, :, T - 1, :], KK[:, :, T - 1, :], Ktmp, ALU.add))
            g_.tensor_tensor(KK[:, :, T - 1, :], KK[:, :, T - 1, :], dE, ALU.add).then_inc(kk_ready, 1)
            pool.wait_ge(xr_in, 2 * 16)
            g_.tensor_tensor(xr[:, :, :], xr[:, :, :], posr[:, :, :], ALU.add).then_inc(xr_ready, 1)

            def fetch_indices(n, to, copies):
                wait_alone(pool, idx_ready, n + 1, pool_passed)
                g_.tensor_copy(to, idx_all[:, bass.ds(n * TOPK, TOPK)]).then_inc(idx_copied, 1)
                wait_alone(pool, idx_copied, copies, pool_passed)

            def gather(dst, table, idx, s):
                pool.indirect_dma_start(dst, None, table, bass.IndirectOffsetOnAxis(ap=idx, axis=0)).then_inc(s, 16)

            def gather_u(n, w, j):
                gather(Uring[:, j % U_RING, :], peer_u, idx_u[:, w, j:j + 1], u_in[j % U_RING])

            def gather_v(n, w, j):
                gather(Vring[:, j % V_RING, :], peer_v, idx_v[:, w, j:j + 1], v_in[j % V_RING])

            def both(n, w):
                fetch_indices(n + 1, idx_u[:, 1 - w, :], 2 * n + 2)
                fetch_indices(n, idx_v[:, w, :], 2 * n + 3)
                for j in range(TOPK):
                    wait_alone(pool, u_used, (n + 1) * TOPK + (j - (U_RING - 1)), pool_passed)
                    gather_u(n + 1, 1 - w, j)
                    if not (isinstance(n, int) and n == 0 and j < V_RING):
                        wait_alone(pool, v_used, n * TOPK + (j - (V_RING - 1)), pool_passed)
                    gather_v(n, w, j)

            pool.wait_ge(y_done, 1)
            fetch_indices(0, idx_u[:, 0, :], 1)
            for j in range(TOPK):
                if j >= U_RING:
                    wait_alone(pool, u_used, j - (U_RING - 1), pool_passed)
                gather_u(0, 0, j)
            pool.wait_ge(o_done, NT)
            both(0, 0)
            with pool.Fori(1, 2 * HEADS - 3, 2) as m:
                both(m, 1)
                both(m + 1, 0)
            last = 2 * HEADS - 2
            both(last - 1, 1)
            both(last, 0)
            fetch_indices(last + 1, idx_v[:, 1, :], 2 * last + 4)
            for j in range(TOPK):
                wait_alone(pool, v_used, (last + 1) * TOPK + (j - (V_RING - 1)), pool_passed)
                gather_v(last + 1, 1, j)


_IN_ORDER = ["x", "c", "ctx", "c_ctx", "w_mod", "b_mod", "norm1_g", "norm2_g", "w_in", "w_out", "s5_lam_re",
             "s5_lam_im", "s5_log_dt", "s5_b_re", "s5_b_im", "s5_c_re", "s5_c_im", "s5_d", "w_glu", "b_glu",
             "w_fourier", "peer_w_q", "peer_sub_keys", "peer_u", "peer_v", "final_g"]
_VIEWS = {"x": (SEQ, D), "c": (8, P), "ctx": (SEQ, D), "c_ctx": (8, P), "w_mod": (D, 6 * D), "b_mod": (48, P),
          "norm1_g": (8, P), "norm2_g": (8, P), "w_in": (D, D), "w_out": (D, D), "s5_lam_re": (2, G, NS),
          "s5_lam_im": (2, G, NS), "s5_log_dt": (2, G), "s5_b_re": (2, G, NS, Q), "s5_b_im": (2, G, NS, Q),
          "s5_c_re": (2, G, Q, NS), "s5_c_im": (2, G, Q, NS), "s5_d": (4, P), "w_glu": (SW, SW), "b_glu": (4, P),
          "w_fourier": (FG, P, P), "peer_w_q": (D, 2 * HEADS * P), "peer_sub_keys": (HEADS, 2, KEYS, P),
          "peer_u": (KEYS * KEYS, D), "peer_v": (KEYS * KEYS, D), "final_g": (D,)}


def shape_constants():
    f32 = np.float32
    quarter = D // 4
    omega = (f32(1.0) / (f32(10000.0) ** (np.arange(quarter, dtype=f32) / f32(quarter)))).astype(f32)
    rows = SEQ // GRID_W
    r = np.repeat(np.arange(rows, dtype=f32), GRID_W)[:, None] * omega
    col = np.tile(np.arange(GRID_W, dtype=f32), rows)[:, None] * omega
    pos = np.concatenate([np.sin(r), np.cos(r), np.sin(col), np.cos(col)], axis=-1).astype(f32)
    fwd = [0, 1, 2, 3, 4, 5, 6, 7, 8, 0] + [7 - t for t in range(T)] + [1, 8]
    bwd = [0, 8, 7, 6, 5, 4, 3, 2, 1, 0] + [t for t in range(T)] + [1, 8]
    small = np.zeros((P, 180), f32)
    small[:, 0:128] = np.eye(P)
    small[0:64, 128:148] = fwd
    small[64:128, 128:148] = bwd
    small[:, 148:164] = np.arange(16)
    small[:, 164:180] = np.tile(np.eye(Q), (8, 1))
    dft = np.zeros((P, 1280), f32)
    ang = 2 * np.pi * (np.outer(np.arange(P), np.arange(P)) % P) / P
    dft[:, 0:128], dft[:, 128:256] = np.cos(ang) / np.sqrt(P), np.sin(ang) / np.sqrt(P)
    ang = 2 * np.pi * (np.outer(np.arange(SEQ), np.arange(SEQ)) % SEQ) / SEQ
    for at, m in ((256, np.cos(ang)), (768, -np.sin(ang))):
        dft[:, at:at + 512] = (m / np.sqrt(SEQ)).reshape(NT, P, SEQ).transpose(1, 0, 2).reshape(P, 512)
    return {"pos": pos, "small_const": small, "dft_const": dft}


def kernel(**inputs):
    import concourse.bacc as bacc
    from concourse.bass_utils import run_bass_kernel_spmd

    nc = bacc.Bacc("TRN2", target_bir_lowering=False, num_devices=1)
    arrays = {n: np.ascontiguousarray(np.asarray(inputs[n]).reshape(_VIEWS[n])) for n in _IN_ORDER}
    constants = shape_constants()
    args = []
    for n, a in [(n, arrays[n]) for n in _IN_ORDER] + list(constants.items()):
        arrays["in_" + n] = a
        args.append(nc.dram_tensor("in_" + n, a.shape, mybir.dt.float32, kind="ExternalInput").ap())
    arrays = {n: a for n, a in arrays.items() if n.startswith("in_")}
    args.append(nc.dram_tensor("out", (SEQ, D), mybir.dt.float32, kind="ExternalOutput").ap())
    hybrid_layer(nc, *args)
    r = run_bass_kernel_spmd(nc, [arrays], core_ids=[0])
    return np.asarray(r.results[0]["out"]).reshape(1, SEQ, D)
```

```python
from contextlib import ExitStack

import numpy as np

import concourse.bass as bass
from concourse import mybir

P = 128
D = 1024
KD = D // P
SEQ = 256
GRID_W = 64
G, NS, Q = 32, 64, 16
T = 8
C = SEQ // T
SEGS, SEG_LEN = 8, 2 * C // 8
SW = G * Q
FG = 4
HEADS, KEYS, TOPK = 8, 128, 16
SLOTS = 20
NT = SEQ // P
U_RING, V_RING = 8, 8
EPS = 1e-6
ROUND = 12582912.0
TWO_PI = 6.283185
GELU_K = 0.7978845608028654
GELU_C = 0.044715
LOWEST = -3.0e38

V_C, V_CCTX, V_BMOD, V_N1, V_N2, V_BGLU, V_D, V_ROWS = 0, 8, 16, 64, 72, 80, 84, 88
SH1, SC1, G1, SH2, SC2, G2 = range(6)
WM_RING = 3


def hybrid_layer(nc, x, c, ctx_in, c_ctx, w_mod, b_mod, norm1_g, norm2_g, w_in, w_out, lam_re, lam_im,
                 log_dt, b_re, b_im, c_re, c_im, d_skip, w_glu, b_glu, w_fourier, peer_w_q, sub_keys,
                 peer_u, peer_v, final_g, pos, small_const, dft_const, parity_const, out):
    F = mybir.dt.float32
    U32 = mybir.dt.uint32
    ALU = mybir.AluOpType
    ACT = mybir.ActivationFunctionType
    AX = mybir.AxisListType.X
    stack = ExitStack()
    with stack:
        def sem(name):
            return stack.enter_context(nc.semaphore(name))

        def region(name, cols):
            return stack.enter_context(nc.sbuf_tensor(name, [P, cols], F))

        R1 = region("R1", 16384)
        R2 = region("R2", 8192)
        R3 = region("R3", 16384)
        R4 = region("R4", 11520)
        R5 = region("R5", 728)
        psum = stack.enter_context(nc.psum_tensor("psum", [P, 8 * 512], F))
        bank = [psum[:, 512 * i:512 * (i + 1)] for i in range(8)]

        wm = [R1[:, 2048 * s:2048 * (s + 1)] for s in range(WM_RING)]
        GC = [R1[:, 6144 + 1024 * r:7168 + 1024 * r].rearrange("p (i n) -> p i n", i=NT) for r in range(2)]
        w_in_s = R1[:, 8192:16384].rearrange("p (k n) -> p k n", k=KD)
        M = R1[:, 10240:14336].rearrange("p (g n) -> p g n", g=G)
        w_glu_s = R1[:, 14336:16384].rearrange("p (k n) -> p k n", k=4)
        xr = R1[:, 0:2048].rearrange("p (i n) -> p i n", i=NT)
        posr = R1[:, 2048:4096].rearrange("p (i n) -> p i n", i=NT)
        keys_nat = R1[:, 4096:6144].rearrange("p (h n) -> p h n", h=2 * HEADS)
        w_q_s = R1[:, :].rearrange("p (k n) -> p k n", k=KD)
        mrow = [R1[:, 7680:8192], R2[:, 2048:2560], R2[:, 2560:3072]]
        Bnat = [R2[0:G, 0:2048], R2[0:G, 2048:4096]]
        Cnat = [R2[:, 4096 + 512 * r:4608 + 512 * r].rearrange("p (i d n) -> p i d n", i=4, d=2) for r in range(2)]
        W = R2[:, :].rearrange("p (g r n) -> p g r n", g=G, r=2)
        Khalf = [[R2[:, 3072 + 512 * (2 * d + h):3584 + 512 * (2 * d + h)].rearrange("p (i n) -> p i n", i=4) for h in range(2)]
                 for d in range(2)]
        KK = R2[:, 1024:1984].rearrange("p (i e q) -> p i e q", i=4, e=15)
        Ktmp = R2[:, 1984:2048].rearrange("p (i q) -> p i q", i=4)
        scan_scr = [R2[:, 5120:6144], R2[:, 7168:8192]]
        scan_tab = R2[:, 6144:7168].rearrange("p (k j r g) -> p k j r g", k=2, j=SEG_LEN, r=2)
        w_out_s = R2[:, :].rearrange("p (k n) -> p k n", k=KD)
        Vring = R2[:, :].rearrange("p (s n) -> p s n", s=V_RING)
        CA = [R3[:, 5120 * r:5120 * (r + 1)].rearrange("p (g s q) -> p g s q", g=G, s=10) for r in range(2)]
        xl = R3[:, 10240:12288].rearrange("p (i n) -> p i n", i=NT)
        xc = R3[:, 12288:14336].rearrange("p (i n) -> p i n", i=NT)
        pl = R3[:, 14336:16384].rearrange("p (i n) -> p i n", i=NT)
        Z = R3[:, 10240:14336]
        Us = R3[:, 14336:16384].rearrange("p (g c) -> p g c", g=G)
        VS = Z.rearrange("p (c r g) -> p c r g", c=2 * C, r=2)
        Yc = R3[:, 12288:13312].rearrange("p (t n) -> p t n", t=T)
        Uring = R3[:, 0:8192].rearrange("p (s n) -> p s n", s=U_RING)
        g2b = R3[:, 8192:9216]
        fgb = R3[:, 9216:10240]
        diag = R3[:, 10240:11264].rearrange("p (s n) -> p s n", s=8)
        qT = R3[:, 11264:11776].rearrange("p (w s n) -> p w s n", w=2, s=2)
        rowA = R3[:, 12288:13312]
        rowB = R3[:, 13312:14336]
        tk = R3[:, 14336:16384]
        cand, wrk = tk[:, 0:256], tk[:, 256:512]
        wrk1 = tk[:, 512:768].rearrange("p (s n) -> p s n", s=2)
        sv = tk[:, 768:800].rearrange("p (s n) -> p s n", s=2)
        si = tk[:, 800:832].bitcast(U32).rearrange("p (s n) -> p s n", s=2)
        sif = tk[:, 832:864].rearrange("p (s n) -> p s n", s=2)
        best = tk[:, 864:880]
        flat = tk[:, 880:896].bitcast(U32)
        fij = tk[:, 896:928].bitcast(U32).rearrange("p (s n) -> p s n", s=2)
        fijf = tk[:, 928:960].rearrange("p (s n) -> p s n", s=2)
        pick = tk[:, 960:976]
        idx_all = tk[:, 976:1232].bitcast(U32)
        e_all = tk[:, 1232:1488]
        esum = tk[:, 1488:1504]
        dots = tk[:, 1504:1536].rearrange("p (w n) -> p w n", w=2)
        garg = tk[:, 1536:1552]
        wgt = tk[:, 1552:1808]
        idx_u = tk[:, 1824:1856].bitcast(U32).rearrange("p (w n) -> p w n", w=2)
        idx_v = tk[:, 1856:1888].bitcast(U32).rearrange("p (w n) -> p w n", w=2)
        gth = tk[:, 1888:1904]
        rsum = tk[:, 1904:1920]
        gdiag = tk[:, 1920:2048]
        hT = R4[:, 0:4096].rearrange("p (k n) -> p k n", k=KD)
        mixT = R4[:, 0:2048].rearrange("p (k n) -> p k n", k=KD)
        gA = R4[:, 2048:3072].rearrange("p (k n) -> p k n", k=4)
        gB = R4[:, 3072:4096].rearrange("p (k n) -> p k n", k=4)
        sc = R4[:, 2048:4096].rearrange("p (h s n) -> p h s n", h=HEADS, s=2)
        Pw = [R4[:, 4096 + 640 * r:4736 + 640 * r].rearrange("p (s g) -> p s g", s=SLOTS) for r in range(2)]
        fT = R4[:, 4096:5120].rearrange("p (j n) -> p j n", j=FG)
        Bb = [R4[:, 5376 + 512 * r:5888 + 512 * r].rearrange("p (g q) -> p g q", g=G) for r in range(2)]
        Cs = [R4[:, 6400 + 512 * r:6912 + 512 * r].rearrange("p (g q) -> p g q", g=G) for r in range(2)]
        CW = [R4[:, 6400 + 512 * r:6912 + 512 * r] for r in range(2)]
        dtmp = R4[:, 7424:9472]
        S2 = R4[:, 7424:9472].rearrange("p (r g c) -> p r g c", r=2, g=G)
        ptmp = R4[:, 9472:11520]
        dft = R4[:, 9472:10752]
        cosC, sinC = dft[:, 0:128], dft[:, 128:256]
        cosL = dft[:, 256:768].rearrange("p (i n) -> p i n", i=NT)
        nsinL = dft[:, 768:1280].rearrange("p (i n) -> p i n", i=NT)
        wf_s = R4[:, 10752:11264]
        parity = R4[:, 11392:11394]
        ones = R4[:, 11264:11392]
        kT = R4[:, 4096:6144].rearrange("p (h n) -> p h n", h=2 * HEADS)
        x1T = R4[:, 6144:8192].rearrange("p (k n) -> p k n", k=KD)
        h2T = R4[:, 8192:9216].rearrange("p (k n) -> p k n", k=KD)
        diag2 = R4[:, 9216:9344]
        zrow = [R1[:, 6144 + 512 * i:6656 + 512 * i] for i in range(4)]
        ident = R5[:, 0:128]
        kmul = R5[:, 128:148]
        iota16 = R5[:, 148:164]
        eyeq = R5[:, 164:180]
        vecT = R5[:, 180:268]
        modS = R5[:, 268:364].rearrange("p (a k w) -> p a k w", a=6, k=KD)
        cact = R5[:, 364:380]
        th_c = R5[:, 380:396]
        Gn1 = R5[:, 396:412].rearrange("p (k w) -> p k w", k=KD)
        Gn2 = R5[:, 412:420]
        A8 = R5[:, 420:548].rearrange("p (k r g) -> p k r g", k=2, r=2)
        half_bg = R5[:, 548:552]
        ss = R5[:, 552:556]
        inv = R5[:, 556:560]
        dE = R5[:, 568:632].rearrange("p (i q) -> p i q", i=4)
        ms, root, newton = R5[:, 560:564], R5[:, 564:568], R5[:, 724:728]
        par = R5[:, 632:728].rearrange("p (a g) -> p a g", a=3)
        vec_nat = R4[0:V_ROWS, 0:128]
        lam_nat = [R4[0:G, 128 * (1 + r):128 * (2 + r)] for r in range(3)]
        ld_nat = R4[0:G, 512:514]
        junk = R4[:, 1024:2048]

        kk_dram = nc.dram_tensor("kk_dram", [G, Q, 15 * Q], F).ap()

        vec_in, const_in, lam_in, b_in, c_in = sem("vec_in"), sem("const_in"), sem("lam_in"), sem("b_in"), sem("c_in")
        xc_in, xl_in, win_in, wout_in, wq_in = sem("xc_in"), sem("xl_in"), sem("win_in"), sem("wout_in"), sem("wq_in")
        glu_in, dft_in, xr_in, keys_in, fg_in = sem("glu_in"), sem("dft_in"), sem("xr_in"), sem("keys_in"), sem("fg_in")
        zc_in = [sem("zc_in_ctx"), sem("zc_in_lat")]
        modT_done, mrow_ready, rows_cleared = sem("modT_done"), sem("mrow_ready"), sem("rows_cleared")
        ca_pool, tab_ready = sem("ca_pool"), sem("tab_ready")
        kk_out, m_in, out_done = sem("kk_out"), sem("m_in"), sem("out_done")
        wm_in = [sem(f"wm_in{s}") for s in range(WM_RING)]
        u_in = [sem(f"u_in{s}") for s in range(U_RING)]
        v_in = [sem(f"v_in{s}") for s in range(V_RING)]
        dve_step, act_step, pool_step = sem("dve_step"), sem("act_step"), sem("pool_step")
        vec_T, par_T, b_T, c_T, x_T = sem("vec_T"), sem("par_T"), sem("b_T"), sem("c_T"), sem("x_T")
        mod_done, w_T, z_done, u_T, v_done = sem("mod_done"), sem("w_T"), sem("z_done"), sem("u_T"), sem("v_done")
        f_done, k_done, cw_done = sem("f_done"), sem("k_done"), sem("cw_done")
        gg_done, fft_done, y_done, yt_done = sem("gg_done"), sem("fft_done"), sem("y_done"), sem("yt_done")
        glu_done, keys_T, xt_T, o_done = sem("glu_done"), sem("keys_T"), sem("xt_T"), sem("o_done")
        ss_done, invb_done, h2_pd, q_done = sem("ss_done"), sem("invb_done"), sem("h2_pd"), sem("q_done")
        s_done, g2_done, x1r_done = sem("s_done"), sem("g2_done"), sem("x1r_done")
        v_used = sem("v_used")
        logdt_spread, vec_ready, par_ready, silu_th = sem("logdt_spread"), sem("vec_ready"), sem("par_ready"), sem("silu_th")
        cact_ready, dt_ready, trig_in, trig_out = sem("cact_ready"), sem("dt_ready"), sem("trig_in"), sem("trig_out")
        pw_ready, bb_ready, cs_ready = sem("pw_ready"), sem("bb_ready"), sem("cs_ready")
        wt_dve, wt_pool, w_ready, ca_ready = sem("wt_dve"), sem("wt_pool"), sem("w_ready"), sem("ca_ready")
        x_pos, ss_ready, ms_ready, root_ready = sem("x_pos"), sem("ss_ready"), sem("ms_ready"), sem("root_ready")
        xn_ready, hraw_dve, hraw_act, h_ready = sem("xn_ready"), sem("hraw_dve"), sem("hraw_act"), sem("h_ready")
        mod_read, z_evac, zg_act, zg_dve = sem("mod_read"), sem("z_evac"), sem("zg_act"), sem("zg_dve")
        u_ready, vs_act, vs_dve = sem("u_ready"), sem("vs_act"), sem("vs_dve")
        scan_step, s2_act, s2_dve = sem("scan_step"), sem("s2_act"), sem("s2_dve")
        f_ready, k_ready, kk_ready = sem("f_ready"), sem("k_ready"), sem("kk_ready")
        cw_ready, gg_ready, mix_f, mix_s5 = sem("cw_ready"), sem("gg_ready"), sem("mix_f"), sem("mix_s5")
        y_act, y_dve, yn_act, yn_dve = sem("y_act"), sem("y_dve"), sem("yn_act"), sem("yn_dve")
        y_sq, y_arg, y_th, g2y_ready, glu_th = sem("y_sq"), sem("y_arg"), sem("y_th"), sem("g2y_ready"), sem("glu_th")
        xr_ready, kt_ready, xt_ready, x1_ready = sem("xr_ready"), sem("kt_ready"), sem("xt_ready"), sem("x1_ready")
        sq_ready, diag2_ready = sem("sq_ready"), sem("diag2_ready")
        h2_ready, q_ready, s_ready, ones_ready = sem("h2_ready"), sem("q_ready"), sem("s_ready"), sem("ones_ready")
        top_ready, exp_ready, idx_ready = sem("top_ready"), sem("exp_ready"), sem("idx_ready")
        idx_copied, u_used = sem("idx_copied"), sem("u_used")
        pool_passed, act_passed, dve_passed = sem("pool_passed"), sem("act_passed"), sem("dve_passed")
        garg_ready, gth_ready, wgt_ready, diag_ready = sem("garg_ready"), sem("gth_ready"), sem("wgt_ready"), sem("diag_ready")
        gdiag_ready, g2b_ready, y_row, fin_ss, out_row = sem("gdiag_ready"), sem("g2b_ready"), sem("y_row"), sem("fin_ss"), sem("out_row")

        class Chain:

            def __init__(self, eng, s):
                self.eng, self.sem, self.n = eng, s, 0

            def step(self, ins):
                ins.then_inc(self.sem, 1)
                self.n += 1

            def after(self):
                self.eng.wait_ge(self.sem, self.n)

            def link(self, ins):
                self.step(ins)
                self.after()

        def query_place(n):
            return (bank[6 + n % 2] if n < HEADS else bank[6])[:, 0:2 * P]

        def score_place(n):
            return (bank[4 + n % 2] if n < HEADS else bank[7])[:, 0:2 * P]

        def wait_alone(eng, s, value, passed):
            eng.wait_ge(s, value)
            if not isinstance(value, int):
                eng.sem_inc(passed, 1)

        def spread(ap, axis, shape):
            return ap.unsqueeze(axis).to_broadcast(shape)

        block = stack.enter_context(nc.Block())

        @block.sync
        def _(sp):
            def load(dst, src, s):
                sp.dma_start(dst, src).then_inc(s, 16)

            load(R5[:, 0:180], small_const, const_in)
            for src, row, rows in ((c, V_C, 8), (c_ctx, V_CCTX, 8), (b_mod, V_BMOD, 48), (norm1_g, V_N1, 8),
                                   (norm2_g, V_N2, 8), (b_glu, V_BGLU, 4), (d_skip, V_D, 4)):
                load(R4[row:row + rows, 0:128], src, vec_in)
            load(lam_nat[0].rearrange("g (d n) -> g d n", d=2), lam_re.rearrange("d g n -> g d n"), lam_in)
            load(lam_nat[1].rearrange("g (d n) -> g d n", d=2), lam_im.rearrange("d g n -> g d n"), lam_in)
            with nc.allow_non_contiguous_dma(reason="64 values"):
                load(ld_nat, log_dt.rearrange("d g -> g d"), lam_in)
            load(xc, ctx_in.rearrange("(i p) n -> p i n", p=P), xc_in)
            load(xl, x.rearrange("(i p) n -> p i n", p=P), xl_in)
            load(pl, pos.rearrange("(i p) n -> p i n", p=P), xl_in)

            def load_mod(n):
                pair, k = n // KD, n % KD
                if n >= WM_RING:
                    sp.wait_ge(mod_done, n - WM_RING + 1)
                load(wm[n % WM_RING], w_mod[P * k:P * (k + 1), 2 * D * pair:2 * D * (pair + 1)], wm_in[n % WM_RING])

            for n in range(KD):
                load_mod(n)
            load(w_in_s, w_in.rearrange("(k p) n -> p k n", p=P), win_in)
            for n in range(KD, KD + 6):
                load_mod(n)
            sp.wait_ge(w_T, 8)
            sp.wait_ge(ca_pool, 1)
            load(dft, dft_const, dft_in)
            load(parity, parity_const, dft_in)
            load(wf_s.rearrange("p (j n) -> p j n", j=FG), w_fourier.rearrange("j c n -> c j n"), dft_in)
            for n in range(KD + 6, KD + 9):
                load_mod(n)
            sp.wait_ge(f_done, 2)
            load(w_glu_s, w_glu.rearrange("(k p) n -> p k n", p=P), glu_in)
            for n in range(KD + 9, KD + 12):
                load_mod(n)
            sp.wait_ge(kk_ready, 1)
            for i in range(4):
                sp.dma_start(kk_dram[8 * i:8 * i + 8].rearrange("g q n -> (g q) n"),
                             KK[:, i].rearrange("p e q -> p (e q)")).then_inc(kk_out, 16)
            sp.wait_ge(kk_out, 64)
            for t in range(T):
                load(M[Q * t:Q * (t + 1)], kk_dram[:, :, Q * (T - 1 - t):Q * (2 * T - 1 - t)].rearrange("g q n -> q g n"), m_in)
            for n in range(KD + 12, 3 * KD):
                load_mod(n)
            sp.wait_ge(s2_act, 1)
            sp.wait_ge(s2_dve, 1)
            sp.wait_ge(modT_done, 3)
            load(w_out_s, w_out.rearrange("(k p) n -> p k n", p=P), wout_in)
            sp.wait_ge(mod_done, 3 * KD)
            load(xr, x.rearrange("(i p) n -> p i n", p=P), xr_in)
            load(posr, pos.rearrange("(i p) n -> p i n", p=P), xr_in)
            load(keys_nat, sub_keys.rearrange("h s k d -> k (h s) d"), keys_in)
            sp.wait_ge(xt_T, 4)
            sp.wait_ge(keys_T, 4)
            sp.wait_ge(fft_done, 2)
            load(w_q_s[:, 0:4], peer_w_q[0:D // 2].rearrange("(k p) n -> p k n", p=P), wq_in)
            sp.wait_ge(y_done, 1)
            sp.wait_ge(glu_done, 1)
            load(w_q_s[:, 4:8], peer_w_q[D // 2:D].rearrange("(k p) n -> p k n", p=P), wq_in)
            load(fgb, final_g.partition_broadcast(P), fg_in)
            for i in range(NT):
                sp.wait_ge(out_row, i + 1)
                sp.dma_start(out[P * i:P * (i + 1), :], rowA).then_inc(out_done, 16)
            sp.wait_ge(out_done, 16 * NT)

        @block.tensor
        def _(pe):
            pe.wait_ge(const_in, 16)
            pe.wait_ge(vec_in, 7 * 16)
            nc.tensor.transpose(bank[6][:, 0:V_ROWS], vec_nat, ident[0:V_ROWS, 0:V_ROWS]).then_inc(vec_T, 1)
            pe.wait_ge(lam_in, 3 * 16)
            pe.wait_ge(logdt_spread, 1)
            for r in range(3):
                last = nc.tensor.transpose(bank[7][:, G * r:G * (r + 1)], lam_nat[r], ident[0:G, 0:G])
            last.then_inc(par_T, 1)
            pe.wait_ge(b_in, 2 * 16)
            for r in range(2):
                for q in range(Q):
                    last = nc.tensor.transpose(bank[4 + r][:, G * q:G * (q + 1)],
                                               Bnat[r][:, q:2048:Q], ident[0:G, 0:G])
            last.then_inc(b_T, 1)
            pe.wait_ge(c_in, 4 * 16)
            for r in range(2):
                for i in range(4):
                    last = nc.tensor.transpose(bank[2 + r][:, P * i:P * (i + 1)],
                                               Cnat[r][:, i].rearrange("p d n -> p (d n)"), ident)
            last.then_inc(c_T, 1)

            def mod_block(n):
                slot, k = n % WM_RING, n % KD
                pe.wait_ge(wm_in[slot], 16 * (n // WM_RING + 1))
                if n == 0:
                    pe.wait_ge(cact_ready, 1)
                    pe.wait_ge(rows_cleared, 1)
                if k == 0 and n:
                    pe.wait_ge(mrow_ready, n // KD)
                for j in range(4):
                    last = nc.tensor.matmul(bank[6][32 * j:32 * j + 2, :], cact[:, k:16:8],
                                            wm[slot][:, 512 * j:512 * (j + 1)], start=(k == 0), stop=(k == KD - 1))
                last.then_inc(mod_done, 1)

            def mod_transpose(pair):
                pe.wait_ge(mrow_ready, pair + 1)
                if pair:
                    pe.wait_ge(mod_read, 2 * pair)
                else:
                    pe.wait_ge(par_ready, 1)
                for m in range(4):
                    last = nc.tensor.transpose(bank[7][:, P * m:P * (m + 1)], mrow[pair][:, P * m:P * (m + 1)], ident)
                last.then_inc(modT_done, 1)

            for n in range(KD):
                mod_block(n)

            pe.wait_ge(xn_ready, 4)
            for k in range(KD):
                if k in (2, 3):
                    pe.wait_ge(cs_ready, 2)
                if k >= 4:
                    pe.wait_ge(hraw_act if k % 2 else hraw_dve, k // 2 - 1)
                for tt in range(4):
                    src = (xc if tt < 2 else xl)[:, tt % 2, P * k:P * (k + 1)]
                    last = nc.tensor.transpose(bank[k % 4][:, P * tt:P * (tt + 1)], src, ident)
                last.then_inc(x_T, 1)
            mod_transpose(0)

            w_batches = [0]

            def w_transpose(ready, count, tmp):
                pe.wait_ge(ready, count)
                if w_batches[0]:
                    pe.wait_ge(w_ready, 2 * w_batches[0])
                else:
                    pe.wait_ge(bb_ready, 1)
                w_batches[0] += 1
                for r in range(2):
                    for gg in range(4):
                        last = nc.tensor.transpose(bank[4 + r][:, P * gg:P * (gg + 1)],
                                                   tmp[:, 1024 * r + P * gg:1024 * r + P * (gg + 1)], ident)
                last.then_inc(w_T, 1)

            def z_tile(tt):
                for k in range(KD):
                    last = nc.tensor.matmul(bank[tt][:, :], hT[:, k, P * tt:P * (tt + 1)], w_in_s[:, k, 0:SW],
                                            start=(k == 0), stop=(k == KD - 1))
                last.then_inc(z_done, 1)

            def u_transpose():
                pe.wait_ge(zg_act, 1)
                pe.wait_ge(zg_dve, 1)
                pe.wait_ge(z_evac, 4)
                for g in range(G):
                    last = nc.tensor.transpose(bank[g // 8][:, 2 * C * (g % 8):2 * C * (g % 8 + 1)],
                                               Z[64:128, P * g:P * (g + 1)], ident[64:128, 64:128])
                    if g % 8 == 7:
                        last.then_inc(u_T, 1)

            def v_products():
                pe.wait_ge(u_ready, 4)
                pe.wait_ge(w_ready, 16)
                for b in range(8):
                    if b >= 4:
                        pe.wait_ge(vs_act, b - 3)
                        pe.wait_ge(vs_dve, b - 3)
                    for gg in range(4):
                        for r in range(2):
                            at = 2 * C * (2 * gg + r)
                            last = nc.tensor.matmul(bank[b % 4][:, at:at + 2 * C], W[:, 4 * b + gg, r, :],
                                                    Us[:, 4 * b + gg, :], start=True, stop=True)
                    last.then_inc(v_done, 1)

            w_transpose(wt_dve, 1, dtmp)
            w_transpose(wt_pool, 1, ptmp)
            pe.wait_ge(h_ready, 16)
            pe.wait_ge(win_in, 16)
            for tt in range(4):
                z_tile(tt)
                if tt < 3:
                    w_transpose(wt_dve, tt + 2, dtmp)
                    w_transpose(wt_pool, tt + 2, ptmp)
            for n in range(KD, KD + 3):
                mod_block(n)
            u_transpose()
            v_products()
            for n in range(KD + 3, KD + 6):
                mod_block(n)
            for j in range(FG):
                for k in range(KD):
                    last = nc.tensor.matmul(bank[4 + j // 2][:, SEQ * (j % 2):SEQ * (j % 2 + 1)],
                                            w_in_s[:, k, SW + P * j:SW + P * (j + 1)], hT[:, k, SEQ:2 * SEQ],
                                            start=(k == 0), stop=(k == KD - 1))
                if j % 2:
                    last.then_inc(f_done, 1)
            for n in range(KD + 6, 2 * KD):
                mod_block(n)

            pe.wait_ge(dft_in, 3 * 16)
            pe.wait_ge(vs_act, 8)
            pe.wait_ge(vs_dve, 8)
            for r, m in enumerate((cosC, sinC)):
                nc.tensor.matmul(bank[2 + r][:, :], m, wf_s, start=True, stop=True).then_inc(cw_done, 1)
            mod_transpose(1)
            pe.wait_ge(ca_ready, 1)
            pe.wait_ge(ca_pool, 1)
            pe.wait_ge(f_ready, 2)
            pe.wait_ge(cw_ready, 2)
            for i in range(4):
                for h in range(2):
                    for d in range(2):
                        rows, first = slice(64 * d, 64 * (d + 1)), 2 * d
                        at = 2 * P * (i % 2) + P * h
                        for r in range(2):
                            for j in range(4):
                                g = 8 * i + 2 * j
                                last = nc.tensor.matmul(bank[2 + 2 * d + i // 2][32 * j:32 * (j + 1), at:at + P],
                                                        Bb[r][rows, g:g + 2, :].rearrange("p g q -> p (g q)"),
                                                        CA[r][rows, g + h, first:first + T, :].rearrange("p s q -> p (s q)"),
                                                        start=(r == 0), stop=(r == 1))
            last.then_inc(k_done, 1)
            pe.wait_ge(k_ready, 8)
            for n in range(2 * KD, 2 * KD + 4):
                mod_block(n)
            for r in range(2):
                for i in range(NT):
                    for j in range(FG):
                        last = nc.tensor.matmul(bank[2 * r + i][:, P * j:P * (j + 1)], fT[:, j, P * i:P * (i + 1)],
                                                CW[r][:, P * j:P * (j + 1)], start=True, stop=True)
                    last.then_inc(gg_done, 1)
            pe.wait_ge(gg_ready, 4)
            for j in range(FG):
                for n, (r, i) in enumerate(((0, 0), (0, 1), (1, 0), (1, 1))):
                    last = nc.tensor.matmul(bank[j // 2][:, SEQ * (j % 2):SEQ * (j % 2 + 1)],
                                            GC[r][:, i, P * j:P * (j + 1)], (cosL, nsinL)[r][:, i, :],
                                            start=(n == 0), stop=(n == 3))
                if j % 2:
                    last.then_inc(fft_done, 1)
            for n in range(2 * KD + 4, 3 * KD):
                mod_block(n)
            mod_transpose(2)

            pe.wait_ge(m_in, T * 16)
            pe.wait_ge(s2_act, 1)
            pe.wait_ge(s2_dve, 1)
            for i in range(8):
                for r in (None, 0, 1):
                    for j in range(4):
                        g = 8 * j + i
                        o = bank[2 + i // 4][C * j:C * (j + 1), P * (i % 4):P * (i % 4 + 1)]
                        if r is None:
                            nc.tensor.matmul(o, Us[:, g, C:2 * C], M[:, g, :], start=True, stop=False)
                        else:
                            last = nc.tensor.matmul(o, S2[:, r, g, :], CA[r][:, g, 1:1 + T, :].rearrange("p s q -> p (s q)"),
                                                    start=False, stop=(r == 1))
            last.then_inc(y_done, 1)
            pe.wait_ge(y_act, 1)
            pe.wait_ge(y_dve, 1)
            for j in range(4):
                for t in range(T):
                    last = nc.tensor.transpose(bank[2 + j][:, C * t:C * (t + 1)], Yc[C * j:C * (j + 1), t, :],
                                               ident[C * j:C * (j + 1), C * j:C * (j + 1)])
            last.then_inc(yt_done, 1)

            def keys_transpose(b):
                if b >= 2:
                    pe.wait_ge(kt_ready, b - 1)
                for i in range(4):
                    last = nc.tensor.transpose(bank[6 + b % 2][:, P * i:P * (i + 1)], keys_nat[:, 4 * b + i, :], ident)
                last.then_inc(keys_T, 1)

            pe.wait_ge(mod_read, 6)
            pe.wait_ge(keys_in, 16)
            keys_transpose(0)
            keys_transpose(1)
            pe.wait_ge(g2y_ready, 1)
            pe.wait_ge(glu_in, 16)
            pe.wait_ge(mix_f, 2)
            for n in range(4):
                for k in range(4):
                    last = nc.tensor.matmul(bank[n // 2][:, SEQ * (n % 2):SEQ * (n % 2 + 1)],
                                            w_glu_s[:, k, P * n:P * (n + 1)], gA[:, k, :], start=(k == 0), stop=(k == 3))
            last.then_inc(glu_done, 1)
            keys_transpose(2)
            keys_transpose(3)
            pe.wait_ge(xr_ready, 1)
            for i in range(NT):
                for b in range(2):
                    if i == 0:
                        pe.wait_ge(kt_ready, 3 + b)
                    else:
                        pe.wait_ge(xt_ready, 1 + b)
                    for k in range(4):
                        last = nc.tensor.transpose(bank[6 + b][:, P * k:P * (k + 1)],
                                                   xr[:, i, P * (4 * b + k):P * (4 * b + k + 1)], ident)
                    last.then_inc(xt_T, 1)

            def out_projection(i):
                for n in range(KD):
                    for k in range(KD):
                        last = nc.tensor.matmul(bank[2 + n // 4][:, P * (n % 4):P * (n % 4 + 1)],
                                                w_out_s[:, k, P * n:P * (n + 1)], mixT[:, k, P * i:P * (i + 1)],
                                                start=(k == 0), stop=(k == KD - 1))
                last.then_inc(o_done, 1)

            def second_norm(i):
                pe.wait_ge(sq_ready, i + 1)
                if i:
                    pe.wait_ge(q_ready, HEADS)
                for k in range(KD):
                    last = nc.tensor.matmul(bank[6][:, 0:1], h2T[:, k, :], ones[:, 0:1], start=(k == 0), stop=(k == KD - 1))
                last.then_inc(ss_done, 1)
                pe.wait_ge(diag2_ready, i + 1)
                nc.tensor.matmul(bank[6][:, P:2 * P], ones, diag2, start=True, stop=True).then_inc(invb_done, 1)
                pe.wait_ge(h2_ready, i + 1)
                for k in range(KD):
                    last = nc.tensor.transpose(bank[2 * i + k // 4][:, P * (k % 4):P * (k % 4 + 1)], h2T[:, k, :], ident)
                last.then_inc(h2_pd, 1)

            def queries(i, h):
                n = HEADS * i + h
                if n >= 2:
                    pe.wait_ge(q_ready, n - 1 if n < HEADS else n)
                for s in range(2):
                    for k in range(KD):
                        at = 2 * P * h + P * s
                        last = nc.tensor.matmul(query_place(n)[:, P * s:P * (s + 1)],
                                                w_q_s[:, k, at:at + P], h2T[:, k, :], start=(k == 0), stop=(k == KD - 1))
                last.then_inc(q_done, 1)

            def scores(i, h):
                n = HEADS * i + h
                pe.wait_ge(q_ready, n + 1)
                if n >= 2:
                    pe.wait_ge(s_ready, n - 1 if n < HEADS else n)
                for s in range(2):
                    last = nc.tensor.matmul(score_place(n)[:, P * s:P * (s + 1)],
                                            qT[:, h % 2, s, :], kT[:, 2 * h + s, :], start=True, stop=True)
                last.then_inc(s_done, 1)

            pe.wait_ge(mix_s5, 1)
            pe.wait_ge(wout_in, 16)
            out_projection(0)
            pe.wait_ge(ones_ready, 1)
            pe.wait_ge(xt_ready, 4)
            second_norm(0)
            pe.wait_ge(wq_in, 2 * 16)
            queries(0, 0)
            for h in range(1, HEADS):
                queries(0, h)
                scores(0, h - 1)
            scores(0, HEADS - 1)
            pe.wait_ge(x1_ready, 1)
            out_projection(1)
            pe.wait_ge(x1_ready, 2)
            for k in range(KD):
                pe.wait_ge(gdiag_ready, k + 1)
                last = nc.tensor.matmul(bank[2 + k // 4][:, P * (k % 4):P * (k % 4 + 1)], ones, gdiag, start=True, stop=True)
                last.then_inc(g2_done, 1)
            pe.wait_ge(g2b_ready, 1)
            second_norm(1)

            def add_up(h_at, h, first, last_head):
                for j in range(TOPK):
                    pe.wait_ge(diag_ready, h_at * TOPK + (j + 1))
                    pe.wait_ge(v_in[j % V_RING], h_at * 32 + 16 * (j // V_RING + 1))
                    for b in range(2):
                        last = nc.tensor.matmul(bank[4 + b][:, :], diag[:, j % 8, :], Vring[:, j % V_RING, 512 * b:512 * (b + 1)],
                                                start=(first and j == 0), stop=(last_head and j == TOPK - 1))
                    last.then_inc(v_used, 1)

            def row_of_x1(i):
                pe.wait_ge(s_ready, 2 * HEADS)
                if i:
                    pe.wait_ge(out_row, 1)
                for k in range(KD):
                    last = nc.tensor.transpose(bank[6 + k // 4][:, P * (k % 4):P * (k % 4 + 1)],
                                               x1T[:, k, P * i:P * (i + 1)], ident)
                last.then_inc(x1r_done, 1)

            for h in range(HEADS):
                queries(1, h)
                scores(1, h)
                if h == 0:
                    pe.wait_ge(s_ready, HEADS)
                add_up(h, h, h == 0, h == HEADS - 1)
            row_of_x1(0)
            pe.wait_ge(y_row, 1)
            add_up(HEADS, 0, True, False)
            with pe.Fori(HEADS + 1, 2 * HEADS - 1) as h:
                add_up(h, None, False, False)
            add_up(2 * HEADS - 1, HEADS - 1, False, True)
            row_of_x1(1)

        @block.vector
        def _(dve):
            v = nc.vector
            ch = Chain(dve, dve_step)
            dve.wait_ge(lam_in, 3 * 16)
            v.tensor_copy(lam_nat[2].rearrange("g (d n) -> g d n", d=2), spread(ld_nat, 2, [G, 2, NS])).then_inc(logdt_spread, 1)
            dve.wait_ge(vec_T, 1)
            v.tensor_copy(vecT, bank[6][:, 0:V_ROWS]).then_inc(vec_ready, 1)
            dve.wait_ge(vec_ready, 1)
            v.tensor_scalar(half_bg, vecT[:, V_BGLU:V_BGLU + 4], 0.5, None, ALU.mult)
            for i in range(4):
                v.tensor_scalar(dE[:, i, :], eyeq, vecT[:, V_D + i:V_D + i + 1], None, ALU.mult)
            dve.wait_ge(silu_th, 1)
            ch.link(v.scalar_tensor_tensor(cact, th_c, 1.0, vecT[:, 0:16], ALU.add, ALU.mult))
            v.tensor_scalar(cact, cact, 0.5, None, ALU.mult).then_inc(cact_ready, 1)
            dve.wait_ge(par_T, 1)
            v.tensor_copy(par, bank[7][:, 0:3 * G].rearrange("p (a g) -> p a g", a=3)).then_inc(par_ready, 1)
            v.memset(bank[6][:, :], 0.0).then_inc(rows_cleared, 1)
            dve.wait_ge(par_ready, 1)
            lr, li = par[:, 0, :], par[:, 1, :]
            dt_, ld_, y1, t0 = (dtmp[:, 32 * n:32 * (n + 1)] for n in range(4))
            cr, ci = dtmp[:, 1920:1952], dtmp[:, 1952:1984]
            A_, B_, C_ = dtmp[:, 128:768], dtmp[:, 768:1408], ptmp[:, 0:640]
            a3, b3 = (z.rearrange("p (s g) -> p s g", s=SLOTS) for z in (A_, B_))
            shape = [P, SLOTS, G]
            dve.wait_ge(dt_ready, 1)
            ch.link(v.tensor_tensor(y1, li, dt_, ALU.mult))
            ch.step(v.tensor_tensor(ld_, lr, dt_, ALU.mult))
            ch.link(v.tensor_scalar(y1, y1, 0.15915494309189535, None, ALU.mult))
            ch.link(v.tensor_scalar(t0, y1, ROUND, ROUND, ALU.add, ALU.subtract))
            ch.link(v.tensor_tensor(y1, y1, t0, ALU.subtract))
            dve.wait_ge(const_in, 16)
            ch.link(v.tensor_tensor(a3, spread(y1, 1, shape), spread(kmul, 2, shape), ALU.mult))
            ch.step(v.tensor_scalar(B_, A_, ROUND, ROUND, ALU.add, ALU.subtract))
            ch.link(v.tensor_scalar(C_, A_, 0.25, None, ALU.add))
            ch.link(v.tensor_tensor(A_, A_, B_, ALU.subtract))
            ch.link(v.tensor_scalar(B_, C_, ROUND, ROUND, ALU.add, ALU.subtract))
            v.tensor_tensor(C_, C_, B_, ALU.subtract).then_inc(trig_in, 1)
            dve.wait_ge(trig_in, 1)
            v.tensor_tensor(b3, spread(ld_, 1, shape), spread(kmul, 2, shape), ALU.mult).then_inc(trig_in, 1)
            dve.wait_ge(trig_out, 3)
            v.tensor_tensor(Pw[0], Pw[0], b3, ALU.mult).then_inc(pw_ready, 1)
            v.tensor_tensor(Pw[1], Pw[1], b3, ALU.mult).then_inc(pw_ready, 1)
            dve.wait_ge(pw_ready, 2)
            for r in range(2):
                v.tensor_copy(A8[:, 0, r, :], Pw[0][:, 19, :])
                v.tensor_scalar(A8[:, 1, r, :], Pw[1][:, 19, :], (1.0, -1.0)[r], None, ALU.mult)
            ar, ai = t0, Pw[1][:, 18, :]
            den, t1, t2 = y1, dt_, ld_
            ch.step(v.tensor_scalar(ar, Pw[0][:, 18, :], -1.0, None, ALU.add))
            ch.step(v.tensor_tensor(den, lr, lr, ALU.mult))
            ch.link(v.tensor_tensor(t1, li, li, ALU.mult))
            ch.link(v.tensor_tensor(den, den, t1, ALU.add))
            ch.link(v.reciprocal(den, den))
            ch.step(v.tensor_tensor(t1, ar, lr, ALU.mult))
            ch.link(v.tensor_tensor(t2, ai, li, ALU.mult))
            ch.link(v.tensor_tensor(t1, t1, t2, ALU.add))
            ch.link(v.tensor_tensor(cr, t1, den, ALU.mult))
            ch.step(v.tensor_tensor(t1, ai, lr, ALU.mult))
            ch.link(v.tensor_tensor(t2, ar, li, ALU.mult))
            ch.link(v.tensor_tensor(t1, t1, t2, ALU.subtract))
            ch.link(v.tensor_tensor(ci, t1, den, ALU.mult))
            dve.wait_ge(b_T, 1)
            gq = [P, G, Q]
            br, bi = (bank[4 + r][:, :].rearrange("p (q g) -> p g q", q=Q) for r in range(2))
            m1, m2 = (dtmp[:, 128 + 512 * n:640 + 512 * n].rearrange("p (g q) -> p g q", g=G) for n in range(2))
            cr3, ci3 = spread(cr, 2, gq), spread(ci, 2, gq)
            ch.step(v.tensor_tensor(m1, br, cr3, ALU.mult))
            ch.link(v.tensor_tensor(m2, bi, ci3, ALU.mult))
            ch.link(v.tensor_tensor(Bb[0], m1, m2, ALU.subtract))
            ch.step(v.tensor_tensor(m1, bi, cr3, ALU.mult))
            ch.link(v.tensor_tensor(m2, br, ci3, ALU.mult))
            v.tensor_tensor(Bb[1], m1, m2, ALU.add).then_inc(bb_ready, 1)
            dve.wait_ge(bb_ready, 1)

            dve.wait_ge(xl_in, 32)
            v.tensor_tensor(xl[:, :, :], xl[:, :, :], pl[:, :, :], ALU.add).then_inc(x_pos, 1)

            def w_batch(n):
                g0 = 4 * n
                if n:
                    dve.wait_ge(w_T, (0, 1, 3, 5)[n])
                w4 = [P, 4, T, Q]
                for r in range(2):
                    ta, tb = (dtmp[:, 1024 * r + 512 * z:1024 * r + 512 * z + 512].rearrange("p (g t q) -> p g t q", g=4, t=T) for z in range(2))
                    pr, pi = (spread(Pw[z][:, 10:18, g0:g0 + 4].rearrange("p s g -> p g s"), 3, w4) for z in range(2))
                    b0, b1 = (spread(Bb[z][:, g0:g0 + 4, :], 2, w4) for z in range(2))
                    ch.step(v.tensor_tensor(ta, pr, (b0, b1)[r], ALU.mult))
                    ch.link(v.tensor_tensor(tb, pi, (b1, b0)[r], ALU.mult))
                    last = v.tensor_tensor(ta, ta, tb, (ALU.subtract, ALU.add)[r])
                    if r == 0:
                        ch.step(last)
                ch.after()
                last.then_inc(wt_dve, 1)

            def mean_square(n, total, cols):
                v.tensor_scalar(ms[:, 0:cols], total, 1.0 / D, EPS, ALU.mult, ALU.add).then_inc(ms_ready, 1)

            def inverse_root(n, out_, cols):
                m, r, q = ms[:, 0:cols], root[:, 0:cols], newton[:, 0:cols]
                dve.wait_ge(root_ready, n)
                ch.link(v.reciprocal(r, r))
                ch.link(v.tensor_tensor(q, r, r, ALU.mult))
                ch.link(v.tensor_tensor(q, q, m, ALU.mult))
                ch.link(v.tensor_scalar(q, q, -0.5, 1.5, ALU.mult, ALU.add))
                ch.link(v.tensor_tensor(out_, r, q, ALU.mult))

            w_batch(0)
            dve.wait_ge(ss_ready, 4)
            mean_square(1, ss, 4)
            inverse_root(1, inv, 4)
            for tt in range(4):
                src = (xc if tt < 2 else xl)[:, tt % 2, :]
                v.tensor_scalar(src, src, inv[:, tt:tt + 1], None, ALU.mult).then_inc(xn_ready, 1)
            for k in range(0, KD, 2):
                dve.wait_ge(x_T, k + 1)
                v.tensor_copy(hT[:, k, :], bank[k % 4][:, :]).then_inc(hraw_dve, 1)

            def mod_out(pair):
                dve.wait_ge(modT_done, pair + 1)
                for a in range(2):
                    part = 2 * pair + a
                    src = bank[7][:, :].rearrange("p (m a j x) -> p a j m x", m=4, a=2, j=2)[:, a, :, :, 0:2]
                    bias = vecT[:, V_BMOD + KD * part:V_BMOD + KD * (part + 1)].rearrange("p (j m) -> p j m", j=2)
                    v.tensor_tensor(modS[:, part].rearrange("p (j m) w -> p j m w", j=2), src,
                                    spread(bias, 3, [P, 2, 4, 2]), ALU.add).then_inc(mod_read, 1)

            mod_out(0)
            dve.wait_ge(mod_read, 2)
            ch.link(v.scalar_tensor_tensor(Gn1, modS[:, SC1], 1.0, spread(vecT[:, V_N1:V_N1 + KD], 2, [P, KD, 2]), ALU.add, ALU.mult))
            dve.wait_ge(hraw_act, 4)
            dve.wait_ge(hraw_dve, 4)
            for k in range(KD):
                for w in (1, 0):
                    at = hT[:, k, SEQ * (1 - w):SEQ * (2 - w)]
                    v.tensor_scalar(at, at, Gn1[:, k, w:w + 1], modS[:, SH1, k, w:w + 1], ALU.mult, ALU.add).then_inc(h_ready, 1)
            w_batch(1)
            w_batch(2)
            w_batch(3)

            def ca_batch(n):
                g0 = 4 * n
                if n == 0:
                    dve.wait_ge(cs_ready, 2)
                    dve.wait_ge(w_T, 7)
                c4 = [P, 4, 10, Q]
                pr, pi = (spread(Pw[z][:, 0:10, g0:g0 + 4].rearrange("p s g -> p g s"), 3, c4) for z in range(2))
                c0, c1 = (spread(Cs[z][:, g0:g0 + 4, :], 2, c4) for z in range(2))
                ta, tb = (dtmp[:, 640 * z:640 * z + 640].rearrange("p (g s q) -> p g s q", g=4, s=10) for z in range(2))
                ch.step(v.tensor_tensor(ta, pr, c0, ALU.mult))
                ch.link(v.tensor_tensor(tb, pi, c1, ALU.mult))
                ch.link(v.tensor_tensor(CA[0][:, g0:g0 + 4], ta, tb, ALU.subtract))
                fa, fb = dtmp[:, 0:640], dtmp[:, 640:1280]
                ch.step(v.tensor_tensor(ta, pr, c1, ALU.mult))
                ch.link(v.tensor_tensor(tb, pi, c0, ALU.mult))
                last = v.scalar_tensor_tensor(CA[1][:, g0:g0 + 4].rearrange("p g s q -> p (g s q)"), fa, -1.0, fb, ALU.mult, ALU.subtract)
                if n == 4:
                    last.then_inc(ca_ready, 1)
                else:
                    ch.link(last)

            def z_permute():
                for side in range(2):
                    dve.wait_ge(zc_in[side], 32)
                src = Z[0:64, :].rearrange("p (t g q) -> p g t q", t=T, g=G)
                dst = Z[64:128, :].rearrange("p (g t q) -> p g t q", g=G, t=T)
                v.tensor_copy(dst[:, 0:16], src[:, 0:16]).then_inc(zg_dve, 1)

            def v_backward():
                dve.wait_ge(u_T, 4)
                for b in range(8):
                    dve.wait_ge(v_done, b + 1)
                    src = bank[b % 4][64:128, :].rearrange("p (g r s c) -> p g r s c", g=4, r=2, s=2)
                    dst = VS[64:128].rearrange("p (s c) r g -> p g r s c", s=2)[:, 4 * b:4 * b + 4]
                    for r in range(2):
                        last = v.tensor_copy(dst[:, :, r], src[:, :, r, :, ::-1])
                    last.then_inc(vs_dve, 1)

            def advance(prev, cur, table, scr, base):
                n = cur.shape[1] if len(cur.shape) == 3 else 1
                shape = [P, 2] + list(cur.shape[1:])
                tab = table if n == 1 else spread(table, 2, shape)
                v.tensor_tensor(scr, spread(prev, 1, shape), tab, ALU.mult).then_inc(scan_step, 1)
                dve.wait_ge(scan_step, base + 1)
                v.tensor_tensor(cur, cur, scr[:, 0], ALU.add).then_inc(scan_step, 1)
                dve.wait_ge(scan_step, base + 2)
                w = "p n (r g) -> p n r g" if n > 1 else "p (r g) -> p r g"
                c4, s4 = cur.rearrange(w, r=2), scr[:, 1].rearrange(w, r=2)
                swapped = s4[:, :, ::-1] if n > 1 else s4[:, ::-1]
                v.tensor_tensor(c4, c4, swapped, ALU.add).then_inc(scan_step, 1)
                dve.wait_ge(scan_step, base + 3)

            for n in range(4):
                ca_batch(n)
            z_permute()
            ca_batch(4)
            v_backward()
            dve.wait_ge(vs_act, 8)
            dve.wait_ge(vs_dve, 8)
            seg = VS.rearrange("p (s j) r g -> p s j (r g)", s=SEGS)
            a8 = A8.rearrange("p k r g -> p k (r g)")
            scr_seg = scan_scr[0][:, 0:2 * SEGS * 64].rearrange("p (k s x) -> p k s x", k=2, s=SEGS)
            scr_one = scan_scr[0][:, 0:128].rearrange("p (k x) -> p k x", k=2)
            powers = scan_tab.rearrange("p k j r g -> p k j (r g)")
            with dve.Fori(1, SEG_LEN) as j:
                advance(seg[:, :, bass.ds(j - 1, 1)][:, :, 0], seg[:, :, bass.ds(j, 1)][:, :, 0], a8, scr_seg, (j - 1) * 3)
            steps = 3 * (SEG_LEN - 1)
            mod_out(1)
            dve.wait_ge(tab_ready, 1)
            with dve.Fori(1, SEGS) as s:
                advance(seg[:, bass.ds(s - 1, 1)][:, 0, SEG_LEN - 1], seg[:, bass.ds(s, 1)][:, 0, SEG_LEN - 1],
                        powers[:, :, SEG_LEN - 1], scr_one, (s - 1) * 3 + steps)
            steps += 3 * (SEGS - 1)
            for s in range(SEGS // 2, SEGS):
                n = SEG_LEN - 1
                scr = scan_scr[s % 2][:, 0:2 * n * 64].rearrange("p (k j x) -> p k j x", k=2, j=n)
                cur = seg[:, s, 0:n]
                v.tensor_tensor(scr, spread(spread(seg[:, s - 1, n], 1, [P, n, 64]), 1, [P, 2, n, 64]), powers[:, :, 0:n], ALU.mult).then_inc(scan_step, 1)
                dve.wait_ge(scan_step, steps + 1)
                v.tensor_tensor(cur, cur, scr[:, 0], ALU.add).then_inc(scan_step, 1)
                dve.wait_ge(scan_step, steps + 2)
                c4, s4 = (z.rearrange("p j (r g) -> p j r g", r=2) for z in (cur, scr[:, 1]))
                v.tensor_tensor(c4, c4, s4[:, :, ::-1], ALU.add).then_inc(scan_step, 1)
                steps += 3
            dve.wait_ge(scan_step, steps)
            for r in range(2):
                last = v.tensor_copy(S2[64:128, r], VS[64:128, C - 1:2 * C - 1, r][:, ::-1, :].rearrange("p c g -> p g c"))
            last.then_inc(s2_dve, 1)
            dve.wait_ge(w_T, 8)
            v.memset(ones, 1.0).then_inc(ones_ready, 1)
            mod_out(2)
            dve.wait_ge(mod_read, 6)
            ch.link(v.scalar_tensor_tensor(Gn2, modS[:, SC2, :, 0], 1.0, vecT[:, V_N2:V_N2 + KD], ALU.add, ALU.mult))
            dve.wait_ge(y_done, 1)
            dve.wait_ge(fft_done, 2)
            v.tensor_copy(Yc.rearrange("p t (i q) -> p i t q", q=Q)[:, 4:8],
                          bank[3][:, :].rearrange("p (i t q) -> p i t q", i=4, t=T)).then_inc(y_dve, 1)
            dve.wait_ge(yt_done, 1)
            dve.wait_ge(f_done, 2)
            for j in range(2):
                last = v.tensor_copy(gA[:, 2 + j, :].rearrange("p (c t) -> p c t", t=T),
                                     bank[4 + j][:, 0:SEQ].rearrange("p (t c) -> p c t", t=T))
            last.then_inc(yn_dve, 1)
            dve.wait_ge(yn_dve, 1)
            dve.wait_ge(yn_act, 1)
            dve.wait_ge(y_sq, 1)
            ch.link(v.tensor_scalar(gB, gB, GELU_K * GELU_C, GELU_K, ALU.mult, ALU.add))
            v.tensor_tensor(gB, gB, gA, ALU.mult).then_inc(y_arg, 1)
            dve.wait_ge(y_th, 1)
            v.scalar_tensor_tensor(gA, gB, 1.0, gA, ALU.add, ALU.mult).then_inc(g2y_ready, 1)
            dve.wait_ge(glu_th, 4)
            dve.wait_ge(g2y_ready, 1)
            ch.link(v.tensor_scalar(gB, gB, 0.25, 0.25, ALU.mult, ALU.add))
            v.tensor_tensor(mixT[:, 0:4, :], gB, gA, ALU.mult).then_inc(mix_s5, 1)

            def residual(i):
                at = slice(P * i, P * (i + 1))
                dve.wait_ge(o_done, i + 1)
                dve.wait_ge(xt_ready, 4)
                for n in range(KD):
                    last = v.scalar_tensor_tensor(x1T[:, n, at], bank[2 + n // 4][:, P * (n % 4):P * (n % 4 + 1)],
                                                  modS[:, G1, n, 0:1], x1T[:, n, at], ALU.mult, ALU.add)
                last.then_inc(x1_ready, 1)

            def norm_two(i):
                at = slice(P * i, P * (i + 1))
                dve.wait_ge(ss_done, i + 1)
                mean_square(2 + i, bank[6][:, 0:1], 1)
                inverse_root(2 + i, inv[:, 0:1], 1)
                v.tensor_scalar(diag2, ident, inv[:, 0:1], None, ALU.mult).then_inc(diag2_ready, 1)
                dve.wait_ge(invb_done, i + 1)
                ch.link(v.tensor_tensor(h2T[:, :, :], spread(bank[6][:, P:2 * P], 1, [P, KD, P]), x1T[:, :, at], ALU.mult))
                for k in range(KD):
                    last = v.tensor_scalar(h2T[:, k, :], h2T[:, k, :], Gn2[:, k:k + 1], modS[:, SH2, k, 0:1], ALU.mult, ALU.add)
                last.then_inc(h2_ready, 1)

            def top_k(n, h, base):
                k = [0]

                def link(ins, wait=True):
                    ins.then_inc(dve_step, 1)
                    k[0] += 1
                    if wait:
                        wait_alone(dve, dve_step, base + k[0], dve_passed)

                wait_alone(dve, s_ready, n + 1, dve_passed)
                hs = wrk.rearrange("p (s n) -> p s n", s=2)
                link(v.tensor_copy(hs, sc[:, h] if isinstance(h, int) else sc[:, bass.ds(h, 1)][:, 0]))
                for s in range(2):
                    link(v.max(sv[:, s, 0:8], hs[:, s]))
                    link(v.max_index(si[:, s, 0:8], sv[:, s, 0:8], hs[:, s]), False)
                    link(v.match_replace(wrk1[:, s], sv[:, s, 0:8], hs[:, s], LOWEST))
                    link(v.max(sv[:, s, 8:16], wrk1[:, s]))
                    link(v.max_index(si[:, s, 8:16], sv[:, s, 8:16], wrk1[:, s]))
                sq = [P, TOPK, TOPK]
                c3 = cand.rearrange("p (a b) -> p a b", a=TOPK)
                w3 = wrk.rearrange("p (a b) -> p a b", a=TOPK)
                link(v.tensor_copy(sif, si), False)
                link(v.tensor_tensor(c3, spread(sv[:, 0, :], 2, sq), spread(sv[:, 1, :], 1, sq), ALU.add))
                link(v.max(best[:, 0:8], cand))
                link(v.max_index(flat[:, 0:8], best[:, 0:8], cand), False)
                link(v.match_replace(wrk, best[:, 0:8], cand, LOWEST))
                link(v.max(best[:, 8:16], wrk))
                link(v.max_index(flat[:, 8:16], best[:, 8:16], wrk))
                eh = e_all[:, bass.ds(n * TOPK, TOPK)]
                v.tensor_scalar(eh, best, best[:, 0:1], None, ALU.subtract).then_inc(top_ready, 1)
                link(v.tensor_scalar(fij[:, 0, :], flat, 4, None, ALU.logical_shift_right), False)
                link(v.tensor_scalar(fij[:, 1, :], flat, 15, None, ALU.bitwise_and))
                link(v.tensor_copy(fijf, fij))
                io = spread(iota16, 1, sq)
                link(v.tensor_tensor(c3, spread(fijf[:, 0, :], 2, sq), io, ALU.is_equal), False)
                link(v.tensor_tensor(w3, spread(fijf[:, 1, :], 2, sq), io, ALU.is_equal))
                link(v.tensor_scalar(sif[:, 0, :], sif[:, 0, :], float(KEYS), None, ALU.mult))
                link(v.tensor_tensor(c3, c3, spread(sif[:, 0, :], 1, sq), ALU.mult), False)
                link(v.tensor_tensor(w3, w3, spread(sif[:, 1, :], 1, sq), ALU.mult))
                link(v.tensor_tensor(cand, cand, wrk, ALU.add))
                link(v.tensor_reduce(pick, c3, AX, ALU.add))
                wait_alone(dve, top_ready, n + 1, dve_passed)
                v.tensor_copy(idx_all[:, bass.ds(n * TOPK, TOPK)], pick).then_inc(idx_ready, 1)
                dve.wait_ge(idx_ready, n + 1)
                return k[0]

            def dot_products(n, tile, base):
                k = [0]

                def link(ins, wait=True):
                    ins.then_inc(dve_step, 1)
                    k[0] += 1
                    if wait:
                        wait_alone(dve, dve_step, base + k[0], dve_passed)

                h2 = bank_pair[tile]
                dd = dots[:, 0, :]
                for j in range(TOPK):
                    dve.wait_ge(u_in[j % U_RING], n * 32 + 16 * (j // U_RING + 1))
                    ur = Uring[:, j % U_RING, :]
                    v.scalar_tensor_tensor(ur, ur, 1.0, h2, ALU.mult, ALU.mult, accum_out=dd[:, j:j + 1]).then_inc(u_used, 1)
                dve.wait_ge(u_used, n * TOPK + TOPK)
                link(v.tensor_tensor(garg, dd, dd, ALU.mult))
                link(v.tensor_scalar(garg, garg, GELU_K * GELU_C, GELU_K, ALU.mult, ALU.add))
                v.tensor_tensor(garg, garg, dd, ALU.mult).then_inc(garg_ready, 1)
                wait_alone(dve, exp_ready, n + 1, dve_passed)
                link(v.reciprocal(rsum[:, 0:1], esum[:, bass.ds(n, 1)]))
                link(v.tensor_scalar(rsum[:, 1:2], rsum[:, 0:1], 0.5, None, ALU.mult), False)
                link(v.tensor_tensor(dd, dd, e_all[:, bass.ds(n * TOPK, TOPK)], ALU.mult))
                dve.wait_ge(gth_ready, n + 1)
                link(v.scalar_tensor_tensor(dd, gth, 1.0, dd, ALU.add, ALU.mult))
                v.tensor_scalar(wgt[:, bass.ds(n * TOPK, TOPK)], dd, rsum[:, 1:2], None, ALU.mult).then_inc(wgt_ready, 1)
                dve.wait_ge(wgt_ready, n + 1)
                return k[0]

            def finish(i):
                dve.wait_ge(v_used, TOPK * HEADS * (i + 1))
                dve.wait_ge(x1r_done, i + 1)
                if i:
                    dve.wait_ge(out_done, 16)
                for b in range(2):
                    last = v.tensor_tensor(rowB[:, 512 * b:512 * (b + 1)], bank[4 + b][:, :], g2b[:, 512 * b:512 * (b + 1)], ALU.mult)
                    ch.step(last)
                ch.after()
                for b in range(2):
                    last = v.tensor_tensor(rowB[:, 512 * b:512 * (b + 1)], rowB[:, 512 * b:512 * (b + 1)], bank[6 + b][:, :], ALU.add)
                last.then_inc(y_row, 1)
                dve.wait_ge(fin_ss, i + 1)
                mean_square(4 + i, ss[:, 0:1], 1)
                inverse_root(4 + i, inv[:, 0:1], 1)
                dve.wait_ge(fg_in, 16)
                v.scalar_tensor_tensor(rowA, rowB, inv[:, 0:1], fgb, ALU.mult, ALU.mult).then_inc(out_row, 1)

            bank_pair = [None, None]
            for i in range(NT):
                bank_pair[i] = psum[:, D * i:D * (i + 1)]
            residual(0)
            norm_two(0)
            dve.wait_ge(h2_pd, 1)
            ch.n += top_k(0, 0, ch.n)
            ch.n += top_k(1, 1, ch.n)
            ch.n += dot_products(0, 0, ch.n)
            residual(1)
            for k in range(KD):
                if k:
                    dve.wait_ge(g2_done, k)
                v.tensor_scalar(gdiag, ident, modS[:, G2, k, 0:1], None, ALU.mult).then_inc(gdiag_ready, 1)
            dve.wait_ge(g2_done, KD)
            for b in range(2):
                last = v.tensor_copy(g2b[:, 512 * b:512 * (b + 1)], bank[2 + b][:, :])
            last.then_inc(g2b_ready, 1)
            norm_two(1)
            ch.n += top_k(2, 2, ch.n)
            n0, per = ch.n, 34
            with dve.Fori(1, HEADS - 2) as h:
                a = dot_products(h, 0, (h - 1) * per + n0)
                b_ = top_k(h + 2, h + 2, (h - 1) * per + (n0 + a))
                assert a + b_ == per, (a, b_)
            n0 += per * (HEADS - 3)
            dve.wait_ge(h2_pd, 2)
            with dve.Fori(HEADS - 2, HEADS) as h:
                a = dot_products(h, 0, (h - (HEADS - 2)) * per + n0)
                top_k(h + 2, h - (HEADS - 2), (h - (HEADS - 2)) * per + (n0 + a))
            n0 += 2 * per
            ch.n = n0
            ch.n += dot_products(HEADS, 1, ch.n)
            ch.n += top_k(HEADS + 2, 2, ch.n)
            finish(0)
            n0 = ch.n
            with dve.Fori(HEADS + 1, 2 * HEADS - 2) as h:
                a = dot_products(h, 1, (h - (HEADS + 1)) * per + n0)
                top_k(h + 2, h - (HEADS - 2), (h - (HEADS + 1)) * per + (n0 + a))
            ch.n = n0 + per * (HEADS - 3)
            for h in range(2 * HEADS - 2, 2 * HEADS):
                ch.n += dot_products(h, 1, ch.n)
            finish(1)

        @block.scalar
        def _(act):
            a = nc.scalar
            ch = Chain(act, act_step)
            for r, t in enumerate((b_re, b_im)):
                act.dma_start(Bnat[r].rearrange("g (d m) -> g d m", d=2), t.rearrange("d g n q -> g d (n q)")).then_inc(b_in, 16)
            for r, t in enumerate((c_re, c_im)):
                for d in range(2):
                    act.dma_start(Cnat[r][:, :, d, :], t[d].rearrange("(i g) q n -> (g q) i n", g=8)).then_inc(c_in, 16)
            act.wait_ge(vec_ready, 1)
            a.activation(th_c, vecT[:, 0:16], ACT.Tanh, scale=0.5).then_inc(silu_th, 1)
            act.wait_ge(par_ready, 1)
            a.activation(dtmp[:, 0:32], par[:, 2, :], ACT.Exp).then_inc(dt_ready, 1)
            act.wait_ge(trig_in, 1)
            a.activation(Pw[1].rearrange("p s g -> p (s g)"), dtmp[:, 128:768], ACT.Sin, scale=TWO_PI).then_inc(trig_out, 1)
            a.activation(Pw[0].rearrange("p s g -> p (s g)"), ptmp[:, 0:640], ACT.Sin, scale=TWO_PI).then_inc(trig_out, 1)
            act.wait_ge(trig_in, 2)
            a.activation(dtmp[:, 768:1408], dtmp[:, 768:1408], ACT.Exp).then_inc(trig_out, 1)
            act.wait_ge(c_T, 1)
            for r in range(2):
                a.copy(Cs[r].rearrange("p g q -> p (g q)"), bank[2 + r][:, :]).then_inc(cs_ready, 1)
            act.wait_ge(xc_in, 16)
            for tt in range(4):
                if tt == 2:
                    act.wait_ge(x_pos, 1)
                if tt:
                    act.wait_ge(ss_ready, tt)
                a.activation(junk, (xc if tt < 2 else xl)[:, tt % 2, :], ACT.Square, accum_out=ss[:, tt:tt + 1]).then_inc(ss_ready, 1)

            def square_root(n, cols):
                act.wait_ge(ms_ready, n)
                a.activation(root[:, 0:cols], ms[:, 0:cols], ACT.Sqrt).then_inc(root_ready, 1)

            def mod_rows(pair):
                act.wait_ge(mod_done, KD * (pair + 1))
                if pair == 1:
                    act.wait_ge(v_done, 8)
                a.copy(mrow[pair], bank[6][:, :]).then_inc(mrow_ready, 1)

            square_root(1, 4)
            mod_rows(0)
            for k in range(1, KD, 2):
                act.wait_ge(x_T, k + 1)
                a.copy(hT[:, k, :], bank[k % 4][:, :]).then_inc(hraw_act, 1)

            def w_out_of_psum(n, g0):
                act.wait_ge(w_T, n + 1)
                for r in range(2):
                    a.copy(W[:, g0:g0 + 4, r, :], bank[4 + r][:, :].rearrange("p (g n) -> p g n", g=4)).then_inc(w_ready, 1)


            def z_out(tt):
                act.wait_ge(z_done, tt + 1)
                a.copy(zrow[tt], bank[tt][:, :]).then_inc(z_evac, 1)
                act.wait_ge(z_evac, tt + 1)
                lo = C * (tt // 2) + 16 * (tt % 2)
                act.dma_start(Z[lo:lo + 16, :].rearrange("c (t n) -> c t n", t=T), zrow[tt]).then_inc(zc_in[tt // 2], 16)

            def z_permute():
                for side in range(2):
                    act.wait_ge(zc_in[side], 32)
                src = Z[0:64, :].rearrange("p (t g q) -> p g t q", t=T, g=G)
                dst = Z[64:128, :].rearrange("p (g t q) -> p g t q", g=G, t=T)
                a.copy(dst[:, 16:32], src[:, 16:32]).then_inc(zg_act, 1)

            w_out_of_psum(0, 0)
            w_out_of_psum(1, 16)
            for tt in range(4):
                z_out(tt)
                if tt < 3:
                    w_out_of_psum(2 * tt + 2, 4 * (tt + 1))
                    w_out_of_psum(2 * tt + 3, 16 + 4 * (tt + 1))
            z_permute()
            for b in range(4):
                act.wait_ge(u_T, b + 1)
                a.copy(Us[:, 8 * b:8 * (b + 1), :], bank[b][:, :].rearrange("p (g c) -> p g c", g=8)).then_inc(u_ready, 1)
            for b in range(8):
                act.wait_ge(v_done, b + 1)
                src = bank[b % 4][0:64, :].rearrange("p (g r c) -> p g r c", g=4, r=2)
                for r in range(2):
                    last = a.copy(VS[0:64, :, r, 4 * b:4 * b + 4].rearrange("p c g -> p g c"), src[:, :, r, :])
                last.then_inc(vs_act, 1)
            act.wait_ge(ca_ready, 1)
            act.wait_ge(ca_pool, 1)
            for b in range(2):
                act.wait_ge(f_done, b + 1)
                a.copy(fT[:, 2 * b:2 * b + 2, :], bank[4 + b][:, :].rearrange("p (j n) -> p j n", j=2)).then_inc(f_ready, 1)
            mod_rows(1)
            for r in range(2):
                act.wait_ge(cw_done, r + 1)
                a.copy(CW[r], bank[2 + r][:, :]).then_inc(cw_ready, 1)
            act.wait_ge(k_done, 1)
            for d in (1, 0):
                for h in range(2):
                    for b in range(2):
                        src = bank[2 + 2 * d + b][:, :].rearrange("p (i h n) -> p i h n", i=2, h=2)[:, :, h]
                        a.activation(Khalf[d][h][:, 2 * b:2 * b + 2], src, ACT.Copy, scale=parity[:, h:h + 1]).then_inc(k_ready, 1)
            for r in range(2):
                for i in range(NT):
                    act.wait_ge(gg_done, 2 * r + i + 1)
                    a.copy(GC[r][:, i, :], bank[2 * r + i][:, :]).then_inc(gg_ready, 1)
            for b in range(2):
                act.wait_ge(fft_done, b + 1)
                a.copy(mixT[:, 4 + 2 * b:6 + 2 * b, :], bank[b][:, :].rearrange("p (j n) -> p j n", j=2)).then_inc(mix_f, 1)
            mod_rows(2)
            act.wait_ge(scan_step, 3 * (SEG_LEN - 1 + SEGS - 1 + SEGS // 2))
            for r in range(2):
                last = a.copy(S2[0:64, r], VS[0:64, C - 1:2 * C - 1, r].rearrange("p c g -> p g c"))
            last.then_inc(s2_act, 1)
            act.wait_ge(y_done, 1)
            a.copy(Yc.rearrange("p t (i q) -> p i t q", q=Q)[:, 0:4],
                   bank[2][:, :].rearrange("p (i t q) -> p i t q", i=4, t=T)).then_inc(y_act, 1)
            act.wait_ge(yt_done, 1)
            for j in range(2):
                last = a.copy(gA[:, j, :].rearrange("p (c t) -> p c t", t=T),
                              bank[2 + j][:, 0:SEQ].rearrange("p (t c) -> p c t", t=T))
            last.then_inc(yn_act, 1)
            act.wait_ge(yn_act, 1)
            act.wait_ge(yn_dve, 1)
            a.activation(gB, gA, ACT.Square).then_inc(y_sq, 1)

            def keys_out(b):
                act.wait_ge(keys_T, b + 1)
                a.copy(kT[:, 4 * b:4 * b + 4, :], bank[6 + b % 2][:, :].rearrange("p (h n) -> p h n", h=4)).then_inc(kt_ready, 1)

            keys_out(0)
            keys_out(1)
            act.wait_ge(y_arg, 1)
            a.activation(gB, gB, ACT.Tanh).then_inc(y_th, 1)
            act.wait_ge(glu_done, 1)
            for n in range(4):
                a.activation(gB[:, n, :], bank[n // 2][:, SEQ * (n % 2):SEQ * (n % 2 + 1)], ACT.Tanh,
                             bias=half_bg[:, n:n + 1], scale=0.25).then_inc(glu_th, 1)
            keys_out(2)
            keys_out(3)
            for n in range(4):
                i, b = n // 2, n % 2
                act.wait_ge(xt_T, n + 1)
                a.copy(x1T[:, 4 * b:4 * b + 4, P * i:P * (i + 1)],
                       bank[6 + b][:, :].rearrange("p (k n) -> p k n", k=4)).then_inc(xt_ready, 1)

            def squares(i):
                act.wait_ge(x1_ready, i + 1)
                if i:
                    act.wait_ge(q_done, HEADS)
                a.activation(h2T[:, :, :], x1T[:, :, P * i:P * (i + 1)], ACT.Square).then_inc(sq_ready, 1)

            def query_out(n):
                act.wait_ge(q_done, n + 1)
                if n >= 2:
                    act.wait_ge(s_done, n - 1)
                w = n % 2
                a.copy(qT[:, w], query_place(n).rearrange("p (s n) -> p s n", s=2)).then_inc(q_ready, 1)

            def scores_out(n):
                act.wait_ge(s_done, n + 1)
                if n == 0:
                    act.wait_ge(mix_s5, 1)
                if n >= HEADS:
                    act.wait_ge(idx_ready, n - HEADS + 1)
                a.copy(sc[:, n % HEADS], score_place(n).rearrange("p (s n) -> p s n", s=2)).then_inc(s_ready, 1)

            def softmax_exp(n):
                wait_alone(act, top_ready, n + 1, act_passed)
                eh = e_all[:, bass.ds(n * TOPK, TOPK)]
                a.activation(eh, eh, ACT.Exp, accum_out=esum[:, bass.ds(n, 1)]).then_inc(exp_ready, 1)

            def gelu_tanh(n):
                act.wait_ge(garg_ready, n + 1)
                a.activation(gth, garg, ACT.Tanh).then_inc(gth_ready, 1)

            def diagonals(n):
                wait_alone(act, wgt_ready, n + 1, act_passed)
                for j in range(TOPK):
                    if not (isinstance(n, int) and n == 0 and j < 8):
                        wait_alone(act, v_used, n * TOPK + (j - 7), act_passed)
                    a.activation(diag[:, j % 8, :], ident, ACT.Copy, scale=wgt[:, bass.ds(n * TOPK + j, 1)]).then_inc(diag_ready, 1)

            def row_squares(i):
                act.wait_ge(y_row, i + 1)
                a.activation(rowA, rowB, ACT.Square, accum_out=ss[:, 0:1]).then_inc(fin_ss, 1)

            squares(0)
            square_root(2, 1)
            query_out(0)
            for n in range(1, HEADS):
                query_out(n)
                scores_out(n - 1)
            scores_out(HEADS - 1)
            softmax_exp(0)
            softmax_exp(1)
            gelu_tanh(0)
            squares(1)
            square_root(3, 1)
            for h in range(HEADS):
                query_out(HEADS + h)
                scores_out(HEADS + h)
                diagonals(h)
                softmax_exp(h + 2)
                gelu_tanh(h + 1)
            row_squares(0)
            square_root(4, 1)
            diagonals(HEADS)
            softmax_exp(HEADS + 2)
            gelu_tanh(HEADS + 1)
            with act.Fori(HEADS + 1, 2 * HEADS - 2) as h:
                diagonals(h)
                softmax_exp(h + 2)
                gelu_tanh(h + 1)
            diagonals(2 * HEADS - 2)
            gelu_tanh(2 * HEADS - 1)
            diagonals(2 * HEADS - 1)
            row_squares(1)
            square_root(5, 1)

        @block.gpsimd
        def _(pool):
            g_ = nc.gpsimd
            ch = Chain(pool, pool_step)
            pool.wait_ge(pw_ready, 2)
            pool.wait_ge(bb_ready, 1)
            w4 = [P, 4, T, Q]
            for n in range(4):
                g0 = 16 + 4 * n
                if n:
                    pool.wait_ge(w_T, 2 * n)
                for r in range(2):
                    ta, tb = (ptmp[:, 1024 * r + 512 * z:1024 * r + 512 * z + 512].rearrange("p (g t q) -> p g t q", g=4, t=T) for z in range(2))
                    pr, pi = (spread(Pw[z][:, 10:18, g0:g0 + 4].rearrange("p s g -> p g s"), 3, w4) for z in range(2))
                    b0, b1 = (spread(Bb[z][:, g0:g0 + 4, :], 2, w4) for z in range(2))
                    ch.step(g_.tensor_tensor(ta, pr, (b0, b1)[r], ALU.mult))
                    ch.link(g_.tensor_tensor(tb, pi, (b1, b0)[r], ALU.mult))
                    last = g_.tensor_tensor(ta, ta, tb, (ALU.subtract, ALU.add)[r])
                    if r == 0:
                        ch.step(last)
                ch.after()
                last.then_inc(wt_pool, 1)
            pool.wait_ge(cs_ready, 2)
            pool.wait_ge(w_T, 8)
            c4 = [P, 4, 10, Q]
            ta, tb = (ptmp[:, 640 * z:640 * z + 640].rearrange("p (g s q) -> p g s q", g=4, s=10) for z in range(2))
            for n in range(5, 8):
                g0 = 4 * n
                pr, pi = (spread(Pw[z][:, 0:10, g0:g0 + 4].rearrange("p s g -> p g s"), 3, c4) for z in range(2))
                c0, c1 = (spread(Cs[z][:, g0:g0 + 4, :], 2, c4) for z in range(2))
                ch.step(g_.tensor_tensor(ta, pr, c0, ALU.mult))
                ch.link(g_.tensor_tensor(tb, pi, c1, ALU.mult))
                ch.link(g_.tensor_tensor(CA[0][:, g0:g0 + 4], ta, tb, ALU.subtract))
                ch.step(g_.tensor_tensor(ta, pr, c1, ALU.mult))
                ch.link(g_.tensor_tensor(tb, pi, c0, ALU.mult))
                ch.link(g_.tensor_tensor(ta, ta, tb, ALU.add))
                last = g_.tensor_scalar(CA[1][:, g0:g0 + 4].rearrange("p g s q -> p (g s q)"), ptmp[:, 0:640], -1.0, None, ALU.mult)
                if n == 7:
                    last.then_inc(ca_pool, 1)
                else:
                    ch.link(last)
            pool.wait_ge(v_done, 8)
            re, im = scan_tab[:, 0, :, 0], scan_tab[:, 1, :, 0]
            ch.step(g_.tensor_copy(re[:, 0], A8[:, 0, 0]))
            ch.link(g_.tensor_copy(im[:, 0], A8[:, 1, 0]))
            n = 1
            while n < SEG_LEN:
                shape = [P, n, G]
                t0, t1 = (R2[:, 128 * z:128 * z + G * n].rearrange("p (n g) -> p n g", n=n) for z in range(2))
                xr_, xi_, yr_, yi_ = re[:, 0:n], im[:, 0:n], spread(re[:, n - 1], 1, shape), spread(im[:, n - 1], 1, shape)
                for out_, a0, a1, b0, b1, op in ((re, xr_, yr_, xi_, yi_, ALU.subtract), (im, xr_, yi_, xi_, yr_, ALU.add)):
                    ch.step(g_.tensor_tensor(t0, a0, a1, ALU.mult))
                    ch.link(g_.tensor_tensor(t1, b0, b1, ALU.mult))
                    ch.link(g_.tensor_tensor(out_[:, n:2 * n], t0, t1, op))
                n *= 2
            ch.link(g_.tensor_copy(scan_tab[:, 0, :, 1], re))
            g_.tensor_scalar(scan_tab[:, 1, :, 1], im, -1.0, None, ALU.mult).then_inc(tab_ready, 1)
            back, fwd = ([x.rearrange("p i (e q) -> p i e q", e=T) for x in Khalf[d]] for d in (1, 0))
            pool.wait_ge(k_ready, 4)
            ch.step(g_.tensor_tensor(KK[:, :, 0:T, :], back[0], back[1], ALU.add))
            pool.wait_ge(k_ready, 8)
            ch.step(g_.tensor_tensor(KK[:, :, T:2 * T - 1, :], fwd[0][:, :, 1:T], fwd[1][:, :, 1:T], ALU.add))
            ch.link(g_.tensor_tensor(Ktmp, fwd[0][:, :, 0], fwd[1][:, :, 0], ALU.add))
            ch.link(g_.tensor_tensor(KK[:, :, T - 1, :], KK[:, :, T - 1, :], Ktmp, ALU.add))
            g_.tensor_tensor(KK[:, :, T - 1, :], KK[:, :, T - 1, :], dE, ALU.add).then_inc(kk_ready, 1)
            pool.wait_ge(xr_in, 2 * 16)
            g_.tensor_tensor(xr[:, :, :], xr[:, :, :], posr[:, :, :], ALU.add).then_inc(xr_ready, 1)

            def fetch_indices(n, to, copies):
                wait_alone(pool, idx_ready, n + 1, pool_passed)
                g_.tensor_copy(to, idx_all[:, bass.ds(n * TOPK, TOPK)]).then_inc(idx_copied, 1)
                wait_alone(pool, idx_copied, copies, pool_passed)

            def gather(dst, table, idx, s):
                pool.indirect_dma_start(dst, None, table, bass.IndirectOffsetOnAxis(ap=idx, axis=0)).then_inc(s, 16)

            def gather_u(n, w, j):
                gather(Uring[:, j % U_RING, :], peer_u, idx_u[:, w, j:j + 1], u_in[j % U_RING])

            def gather_v(n, w, j):
                gather(Vring[:, j % V_RING, :], peer_v, idx_v[:, w, j:j + 1], v_in[j % V_RING])

            def both(n, w):
                fetch_indices(n + 1, idx_u[:, 1 - w, :], 2 * n + 2)
                fetch_indices(n, idx_v[:, w, :], 2 * n + 3)
                for j in range(TOPK):
                    wait_alone(pool, u_used, (n + 1) * TOPK + (j - (U_RING - 1)), pool_passed)
                    gather_u(n + 1, 1 - w, j)
                    if not (isinstance(n, int) and n == 0 and j < V_RING):
                        wait_alone(pool, v_used, n * TOPK + (j - (V_RING - 1)), pool_passed)
                    gather_v(n, w, j)

            pool.wait_ge(y_done, 1)
            fetch_indices(0, idx_u[:, 0, :], 1)
            for j in range(TOPK):
                if j >= U_RING:
                    wait_alone(pool, u_used, j - (U_RING - 1), pool_passed)
                gather_u(0, 0, j)
            pool.wait_ge(o_done, NT)
            both(0, 0)
            with pool.Fori(1, 2 * HEADS - 3, 2) as m:
                both(m, 1)
                both(m + 1, 0)
            last = 2 * HEADS - 2
            both(last - 1, 1)
            both(last, 0)
            fetch_indices(last + 1, idx_v[:, 1, :], 2 * last + 4)
            for j in range(TOPK):
                wait_alone(pool, v_used, (last + 1) * TOPK + (j - (V_RING - 1)), pool_passed)
                gather_v(last + 1, 1, j)


_IN_ORDER = ["x", "c", "ctx", "c_ctx", "w_mod", "b_mod", "norm1_g", "norm2_g", "w_in", "w_out", "s5_lam_re",
             "s5_lam_im", "s5_log_dt", "s5_b_re", "s5_b_im", "s5_c_re", "s5_c_im", "s5_d", "w_glu", "b_glu",
             "w_fourier", "peer_w_q", "peer_sub_keys", "peer_u", "peer_v", "final_g"]
_VIEWS = {"x": (SEQ, D), "c": (8, P), "ctx": (SEQ, D), "c_ctx": (8, P), "w_mod": (D, 6 * D), "b_mod": (48, P),
          "norm1_g": (8, P), "norm2_g": (8, P), "w_in": (D, D), "w_out": (D, D), "s5_lam_re": (2, G, NS),
          "s5_lam_im": (2, G, NS), "s5_log_dt": (2, G), "s5_b_re": (2, G, NS, Q), "s5_b_im": (2, G, NS, Q),
          "s5_c_re": (2, G, Q, NS), "s5_c_im": (2, G, Q, NS), "s5_d": (4, P), "w_glu": (SW, SW), "b_glu": (4, P),
          "w_fourier": (FG, P, P), "peer_w_q": (D, 2 * HEADS * P), "peer_sub_keys": (HEADS, 2, KEYS, P),
          "peer_u": (KEYS * KEYS, D), "peer_v": (KEYS * KEYS, D), "final_g": (D,)}


def shape_constants():
    f32 = np.float32
    quarter = D // 4
    omega = (f32(1.0) / (f32(10000.0) ** (np.arange(quarter, dtype=f32) / f32(quarter)))).astype(f32)
    rows = SEQ // GRID_W
    r = np.repeat(np.arange(rows, dtype=f32), GRID_W)[:, None] * omega
    col = np.tile(np.arange(GRID_W, dtype=f32), rows)[:, None] * omega
    pos = np.concatenate([np.sin(r), np.cos(r), np.sin(col), np.cos(col)], axis=-1).astype(f32)
    fwd = [0, 1, 2, 3, 4, 5, 6, 7, 8, 0] + [7 - t for t in range(T)] + [1, 8]
    bwd = [0, 8, 7, 6, 5, 4, 3, 2, 1, 0] + [t for t in range(T)] + [1, 8]
    small = np.zeros((P, 180), f32)
    small[:, 0:128] = np.eye(P)
    small[0:64, 128:148] = fwd
    small[64:128, 128:148] = bwd
    small[:, 148:164] = np.arange(16)
    small[:, 164:180] = np.tile(np.eye(Q), (8, 1))
    dft = np.zeros((P, 1280), f32)
    ang = 2 * np.pi * (np.outer(np.arange(P), np.arange(P)) % P) / P
    dft[:, 0:128], dft[:, 128:256] = np.cos(ang) / np.sqrt(P), np.sin(ang) / np.sqrt(P)
    ang = 2 * np.pi * (np.outer(np.arange(SEQ), np.arange(SEQ)) % SEQ) / SEQ
    for at, m in ((256, np.cos(ang)), (768, -np.sin(ang))):
        dft[:, at:at + 512] = (m / np.sqrt(SEQ)).reshape(NT, P, SEQ).transpose(1, 0, 2).reshape(P, 512)
    group = np.arange(P) // Q
    parity = np.stack([group % 2 == 0, group % 2 == 1], axis=1).astype(f32)
    return {"pos": pos, "small_const": small, "dft_const": dft, "parity_const": parity}


def kernel(**inputs):
    import concourse.bacc as bacc
    from concourse.bass_utils import run_bass_kernel_spmd

    nc = bacc.Bacc("TRN2", target_bir_lowering=False, num_devices=1)
    arrays = {n: np.ascontiguousarray(np.asarray(inputs[n]).reshape(_VIEWS[n])) for n in _IN_ORDER}
    constants = shape_constants()
    args = []
    for n, a in [(n, arrays[n]) for n in _IN_ORDER] + list(constants.items()):
        arrays["in_" + n] = a
        args.append(nc.dram_tensor("in_" + n, a.shape, mybir.dt.float32, kind="ExternalInput").ap())
    arrays = {n: a for n, a in arrays.items() if n.startswith("in_")}
    args.append(nc.dram_tensor("out", (SEQ, D), mybir.dt.float32, kind="ExternalOutput").ap())
    hybrid_layer(nc, *args)
    r = run_bass_kernel_spmd(nc, [arrays], core_ids=[0])
    return np.asarray(r.results[0]["out"]).reshape(1, SEQ, D)
```

```python
from contextlib import ExitStack

import numpy as np

import concourse.bass as bass
from concourse import mybir

P = 128
D = 1024
KD = D // P
SEQ = 256
GRID_W = 64
G, NS, Q = 32, 64, 16
T = 8
C = SEQ // T
SEGS, SEG_LEN = 8, 2 * C // 8
SW = G * Q
FG = 4
HEADS, KEYS, TOPK = 8, 128, 16
SLOTS = 20
NT = SEQ // P
U_RING, V_RING = 8, 8
DVE_RANKS = 5
EPS = 1e-6
ROUND = 12582912.0
TWO_PI = 6.283185
GELU_K = 0.7978845608028654
GELU_C = 0.044715
LOWEST = -3.0e38

V_C, V_CCTX, V_BMOD, V_N1, V_N2, V_BGLU, V_D, V_ROWS = 0, 8, 16, 64, 72, 80, 84, 88
SH1, SC1, G1, SH2, SC2, G2 = range(6)
V_BANKS = (4, 5, 7)
WM_RING = 3


def hybrid_layer(nc, x, c, ctx_in, c_ctx, w_mod, b_mod, norm1_g, norm2_g, w_in, w_out, lam_re, lam_im,
                 log_dt, b_re, b_im, c_re, c_im, d_skip, w_glu, b_glu, w_fourier, peer_w_q, sub_keys,
                 peer_u, peer_v, final_g, pos, small_const, dft_const, parity_const, out):
    F = mybir.dt.float32
    U32 = mybir.dt.uint32
    ALU = mybir.AluOpType
    ACT = mybir.ActivationFunctionType
    AX = mybir.AxisListType.X
    stack = ExitStack()
    with stack:
        def sem(name):
            return stack.enter_context(nc.semaphore(name))

        def region(name, cols):
            return stack.enter_context(nc.sbuf_tensor(name, [P, cols], F))

        R1 = region("R1", 16384)
        R2 = region("R2", 8192)
        R3 = region("R3", 16384)
        R4 = region("R4", 11520)
        R5 = region("R5", 728)
        psum = stack.enter_context(nc.psum_tensor("psum", [P, 8 * 512], F))
        bank = [psum[:, 512 * i:512 * (i + 1)] for i in range(8)]

        wm = [R1[:, 2048 * s:2048 * (s + 1)] for s in range(WM_RING)]
        GC = [R1[:, 6144 + 1024 * r:7168 + 1024 * r].rearrange("p (i n) -> p i n", i=NT) for r in range(2)]
        w_in_s = [R1[:, 8192 + 4096 * z:12288 + 4096 * z].rearrange("p (k n) -> p k n", k=KD) for z in range(2)]
        Vrow = R1[:, 8192:12288].rearrange("p (b a r n) -> p b a r n", b=8, a=2, r=2)
        M = R1[:, 8192:12288].rearrange("p (g n) -> p g n", g=G)
        w_glu_s = R1[:, 14336:16384].rearrange("p (k n) -> p k n", k=4)
        xr = R1[:, 12288:14336].rearrange("p (i n) -> p i n", i=NT)
        posr = R4[:, 5376:7424].rearrange("p (i n) -> p i n", i=NT)
        keys_nat = R3[:, 10240:12288].rearrange("p (h n) -> p h n", h=2 * HEADS)
        w_q_s = R1[:, :].rearrange("p (k n) -> p k n", k=KD)
        mrow = [R1[:, 7680:8192], R1[:, 6144:6656], R3[:, 13312:13824]]
        Bnat = [R2[0:G, 0:2048], R2[0:G, 2048:4096]]
        Cnat = [R2[:, 4096 + 512 * r:4608 + 512 * r].rearrange("p (i d n) -> p i d n", i=4, d=2) for r in range(2)]
        W = R2[:, :].rearrange("p (g r n) -> p g r n", g=G, r=2)
        Khalf = [[R2[:, 3072 + 512 * (2 * d + h):3584 + 512 * (2 * d + h)].rearrange("p (i n) -> p i n", i=4) for h in range(2)]
                 for d in range(2)]
        KK = R2[:, 1024:1984].rearrange("p (i e q) -> p i e q", i=4, e=15)
        Ktmp = R2[:, 1984:2048].rearrange("p (i q) -> p i q", i=4)
        scan_scr = [R2[:, 5120:6144], R2[:, 7168:8192]]
        scan_tab = R2[:, 6144:7168].rearrange("p (k j r g) -> p k j r g", k=2, j=SEG_LEN, r=2)
        w_out_s = R2[:, :].rearrange("p (k n) -> p k n", k=KD)
        Vring = R2[:, :].rearrange("p (s n) -> p s n", s=V_RING)
        CA = [R3[:, 5120 * r:5120 * (r + 1)].rearrange("p (g s q) -> p g s q", g=G, s=10) for r in range(2)]
        xl = R3[:, 10240:12288].rearrange("p (i n) -> p i n", i=NT)
        xc = R3[:, 12288:14336].rearrange("p (i n) -> p i n", i=NT)
        pl = R3[:, 14336:16384].rearrange("p (i n) -> p i n", i=NT)
        Z = R3[:, 10240:14336]
        ca_scr = R3[:, 14336:15616]
        Us = R3[:, 14336:16384].rearrange("p (g c) -> p g c", g=G)
        VS = Z.rearrange("p (c r g) -> p c r g", c=2 * C, r=2)
        Yc = R3[:, 12288:13312].rearrange("p (t n) -> p t n", t=T)
        Uring = R3[:, 0:8192].rearrange("p (s n) -> p s n", s=U_RING)
        last_sum = Uring[:, 0, :]
        g2b = R3[:, 8192:9216]
        fgb = R3[:, 9216:10240]
        diag = R3[:, 10240:11264].rearrange("p (s n) -> p s n", s=8)
        qT = R3[:, 11264:11776].rearrange("p (w s n) -> p w s n", w=2, s=2)
        rowA = R3[:, 12288:13312]
        rowB = R3[:, 13312:14336]
        x1g = rowB.rearrange("p (k n) -> p k n", k=KD)
        tk = R3[:, 14336:16384]
        cand, wrk = tk[:, 0:256], tk[:, 256:512]
        wrk1 = tk[:, 512:768].rearrange("p (s n) -> p s n", s=2)
        sv = tk[:, 768:800].rearrange("p (s n) -> p s n", s=2)
        si = tk[:, 800:832].bitcast(U32).rearrange("p (s n) -> p s n", s=2)
        sif = tk[:, 832:864].rearrange("p (s n) -> p s n", s=2)
        best = tk[:, 864:880]
        flat = tk[:, 880:896].bitcast(U32)
        fij = tk[:, 896:928].bitcast(U32).rearrange("p (s n) -> p s n", s=2)
        fijf = tk[:, 928:960].rearrange("p (s n) -> p s n", s=2)
        pick = tk[:, 960:976]
        idx_all = tk[:, 976:1232].bitcast(U32)
        e_all = tk[:, 1232:1488]
        esum = tk[:, 1488:1504]
        dots = tk[:, 1504:1536].rearrange("p (w n) -> p w n", w=2)
        garg = tk[:, 1536:1552]
        wgt = tk[:, 1552:1808]
        idx_u = tk[:, 1824:1856].bitcast(U32).rearrange("p (w n) -> p w n", w=2)
        idx_v = tk[:, 1856:1888].bitcast(U32).rearrange("p (w n) -> p w n", w=2)
        gth = tk[:, 1888:1904]
        rsum = tk[:, 1904:1920]
        gdiag = rowA
        hT = R4[:, 0:4096].rearrange("p (k n) -> p k n", k=KD)
        mixT = R4[:, 0:2048].rearrange("p (k n) -> p k n", k=KD)
        gA = R4[:, 2048:3072].rearrange("p (k n) -> p k n", k=4)
        gB = R4[:, 3072:4096].rearrange("p (k n) -> p k n", k=4)
        sc = R4[:, 2048:4096].rearrange("p (h s n) -> p h s n", h=HEADS, s=2)
        Pw = [R4[:, 4096 + 640 * r:4736 + 640 * r].rearrange("p (s g) -> p s g", s=SLOTS) for r in range(2)]
        fT = R4[:, 4096:5120].rearrange("p (j n) -> p j n", j=FG)
        Bb = [R4[:, 5376 + 512 * r:5888 + 512 * r].rearrange("p (g q) -> p g q", g=G) for r in range(2)]
        Cs = [R4[:, 6400 + 512 * r:6912 + 512 * r].rearrange("p (g q) -> p g q", g=G) for r in range(2)]
        CW = [R4[:, 6400 + 512 * r:6912 + 512 * r] for r in range(2)]
        dtmp = R4[:, 7424:9472]
        S2 = R4[:, 7424:9472].rearrange("p (r g c) -> p r g c", r=2, g=G)
        ptmp = R4[:, 9472:11520]
        dft = R4[:, 9472:10752]
        cosC, sinC = dft[:, 0:128], dft[:, 128:256]
        cosL = dft[:, 256:768].rearrange("p (i n) -> p i n", i=NT)
        nsinL = dft[:, 768:1280].rearrange("p (i n) -> p i n", i=NT)
        wf_s = R4[:, 10752:11264]
        parity = R4[:, 11392:11394]
        ones = R4[:, 11264:11392]
        kT = R4[:, 4096:6144].rearrange("p (h n) -> p h n", h=2 * HEADS)
        x1T = R4[:, 6144:8192].rearrange("p (k n) -> p k n", k=KD)
        h2T = R4[:, 8192:9216].rearrange("p (k n) -> p k n", k=KD)
        diag2 = R4[:, 9216:9344]
        zrow = [R1[:, 6144 + 512 * i:6656 + 512 * i] for i in range(4)]
        ident = R5[:, 0:128]
        kmul = R5[:, 128:148]
        iota16 = R5[:, 148:164]
        eyeq = R5[:, 164:180]
        vecT = R5[:, 180:268]
        modS = R5[:, 268:364].rearrange("p (a k w) -> p a k w", a=6, k=KD)
        cact = R5[:, 364:380]
        th_c = R5[:, 380:396]
        Gn1 = R5[:, 396:412].rearrange("p (k w) -> p k w", k=KD)
        Gn2 = R5[:, 412:420]
        A8 = R5[:, 420:548].rearrange("p (k r g) -> p k r g", k=2, r=2)
        half_bg = R5[:, 548:552]
        ss = R5[:, 552:556]
        inv = R5[:, 556:560]
        dE = R5[:, 568:632].rearrange("p (i q) -> p i q", i=4)
        ms, root, newton = R5[:, 560:564], R5[:, 564:568], R5[:, 724:728]
        par = R5[:, 632:728].rearrange("p (a g) -> p a g", a=3)
        vec_nat = R4[0:V_ROWS, 0:128]
        lam_nat = [R4[0:G, 128 * (1 + r):128 * (2 + r)] for r in range(3)]
        ld_nat = R4[0:G, 512:514]
        junk = R4[:, 1024:2048]

        kk_dram = nc.dram_tensor("kk_dram", [G, Q, 15 * Q], F).ap()

        vec_in, const_in, lam_in, b_in, c_in = sem("vec_in"), sem("const_in"), sem("lam_in"), sem("b_in"), sem("c_in")
        xc_in, xl_in, wout_in, wq_in = sem("xc_in"), sem("xl_in"), sem("wout_in"), sem("wq_in")
        win_in = [sem("win_in_u"), sem("win_in_f")]
        glu_in, dft_in, xr_in, keys_in, fg_in = sem("glu_in"), sem("dft_in"), sem("xr_in"), sem("keys_in"), sem("fg_in")
        zc_in = [sem("zc_in_ctx"), sem("zc_in_lat")]
        modT_done, mrow_ready, rows_cleared = sem("modT_done"), sem("mrow_ready"), sem("rows_cleared")
        ca_pool, tab_ready = sem("ca_pool"), sem("tab_ready")
        wq_first_in = sem("wq_first_in")
        vr_done, vr_ready = sem("vr_done"), [sem("vr_ready_act"), sem("vr_ready_dve")]
        kk_out, m_in, out_done = sem("kk_out"), sem("m_in"), sem("out_done")
        wm_in = [sem(f"wm_in{s}") for s in range(WM_RING)]
        u_in = [sem(f"u_in{s}") for s in range(U_RING)]
        v_in = [sem(f"v_in{s}") for s in range(V_RING)]
        dve_step, act_step, pool_step = sem("dve_step"), sem("act_step"), sem("pool_step")
        params_T, x_T = sem("params_T"), sem("x_T")
        mod_done, w_T, z_done, u_T, v_done = sem("mod_done"), sem("w_T"), sem("z_done"), sem("u_T"), sem("v_done")
        f_done, k_done, cw_done = sem("f_done"), sem("k_done"), sem("cw_done")
        gg_done, fft_done, y_done, yt_done = sem("gg_done"), sem("fft_done"), sem("y_done"), sem("yt_done")
        glu_done, keys_T, xt_T, o_done = sem("glu_done"), sem("keys_T"), sem("xt_T"), sem("o_done")
        ss_done, invb_done, h2_pd, q_done = sem("ss_done"), sem("invb_done"), sem("h2_pd"), sem("q_done")
        s_done, g2_done, x1r_done = sem("s_done"), sem("g2_done"), sem("x1r_done")
        v_used = sem("v_used")
        logdt_spread, vec_ready, par_ready, silu_th = sem("logdt_spread"), sem("vec_ready"), sem("par_ready"), sem("silu_th")
        cact_ready, dt_ready, trig_in, trig_out = sem("cact_ready"), sem("dt_ready"), sem("trig_in"), sem("trig_out")
        pw_ready, bb_ready, cs_ready = sem("pw_ready"), sem("bb_ready"), sem("cs_ready")
        wt_dve, wt_pool, w_ready, ca_ready = sem("wt_dve"), sem("wt_pool"), sem("w_ready"), sem("ca_ready")
        x_pos, ss_ready, ms_ready, root_ready = sem("x_pos"), sem("ss_ready"), sem("ms_ready"), sem("root_ready")
        xn_ready, hraw_dve, hraw_act = sem("xn_ready"), sem("hraw_dve"), sem("hraw_act")
        gn1_ready, hc_ready, hl_ready = sem("gn1_ready"), sem("hc_ready"), sem("hl_ready")
        mod_read, z_evac, zg_act, zg_dve = sem("mod_read"), sem("z_evac"), sem("zg_act"), sem("zg_dve")
        u_ready, vs_act, vs_dve = sem("u_ready"), sem("vs_act"), sem("vs_dve")
        scan_step, s2_act, s2_dve = sem("scan_step"), sem("s2_act"), sem("s2_dve")
        f_ready, k_ready, kk_ready = sem("f_ready"), sem("k_ready"), sem("kk_ready")
        cw_ready, gg_ready, mix_f, mix_s5 = sem("cw_ready"), sem("gg_ready"), sem("mix_f"), sem("mix_s5")
        y_act, y_dve, yn_act, yn_dve = sem("y_act"), sem("y_dve"), sem("yn_act"), sem("yn_dve")
        y_sq, y_arg, y_th, g2y_ready, glu_th = sem("y_sq"), sem("y_arg"), sem("y_th"), sem("g2y_ready"), sem("glu_th")
        xr_ready, kt_ready, xt_ready, x1_ready = sem("xr_ready"), sem("kt_ready"), sem("xt_ready"), sem("x1_ready")
        sq_ready, diag2_ready, x1g_ready = sem("sq_ready"), sem("diag2_ready"), sem("x1g_ready")
        h2_ready, q_ready, s_ready, ones_ready = sem("h2_ready"), sem("q_ready"), sem("s_ready"), sem("ones_ready")
        top_ready, exp_ready, idx_ready = sem("top_ready"), sem("exp_ready"), sem("idx_ready")
        idx_copied, u_used = sem("idx_copied"), sem("u_used")
        pool_passed, act_passed, dve_passed = sem("pool_passed"), sem("act_passed"), sem("dve_passed")
        garg_ready, gth_ready, wgt_ready, diag_ready = sem("garg_ready"), sem("gth_ready"), sem("wgt_ready"), sem("diag_ready")
        gdiag_ready, g2b_ready, y_row, fin_ss, out_row = sem("gdiag_ready"), sem("g2b_ready"), sem("y_row"), sem("fin_ss"), sem("out_row")

        class Chain:

            def __init__(self, eng, s):
                self.eng, self.sem, self.n = eng, s, 0

            def step(self, ins):
                ins.then_inc(self.sem, 1)
                self.n += 1

            def after(self):
                self.eng.wait_ge(self.sem, self.n)

            def link(self, ins):
                self.step(ins)
                self.after()

        def queries_before(h):
            if h < HEADS - 2:
                return range(max(h - 2, 0), h - 1)
            first = HEADS - 4 + 2 * (h - (HEADS - 2))
            return range(first, first + 2)

        def query_place(n):
            return (bank[7 - n % 2] if n < HEADS else bank[6])[:, 0:2 * P]

        def projected(i, n):
            return bank[(4, 2)[i] + n // 4][:, P * (n % 4):P * (n % 4 + 1)]

        def score_place(n):
            return (bank[4 + n % 2] if n < HEADS else bank[7])[:, 0:2 * P]

        def wait_alone(eng, s, value, passed):
            eng.wait_ge(s, value)
            if not isinstance(value, int):
                eng.sem_inc(passed, 1)

        def spread(ap, axis, shape):
            return ap.unsqueeze(axis).to_broadcast(shape)

        block = stack.enter_context(nc.Block())

        @block.sync
        def _(sp):
            def load(dst, src, s):
                sp.dma_start(dst, src).then_inc(s, 16)

            load(R5[:, 0:180], small_const, const_in)
            for src, row, rows in ((c, V_C, 8), (c_ctx, V_CCTX, 8), (b_mod, V_BMOD, 48), (norm1_g, V_N1, 8),
                                   (norm2_g, V_N2, 8), (b_glu, V_BGLU, 4), (d_skip, V_D, 4)):
                load(R4[row:row + rows, 0:128], src, vec_in)
            load(lam_nat[0].rearrange("g (d n) -> g d n", d=2), lam_re.rearrange("d g n -> g d n"), lam_in)
            load(lam_nat[1].rearrange("g (d n) -> g d n", d=2), lam_im.rearrange("d g n -> g d n"), lam_in)
            with nc.allow_non_contiguous_dma(reason="64 values"):
                load(ld_nat, log_dt.rearrange("d g -> g d"), lam_in)
            load(xc, ctx_in.rearrange("(i p) n -> p i n", p=P), xc_in)
            load(xl, x.rearrange("(i p) n -> p i n", p=P), xl_in)
            load(pl, pos.rearrange("(i p) n -> p i n", p=P), xl_in)

            def load_mod(n):
                pair, k = n // KD, n % KD
                if n >= WM_RING:
                    sp.wait_ge(mod_done, n - WM_RING + 1)
                load(wm[n % WM_RING], w_mod[P * k:P * (k + 1), 2 * D * pair:2 * D * (pair + 1)], wm_in[n % WM_RING])

            for n in range(KD):
                load_mod(n)
            for half in range(2):
                load(w_in_s[half], w_in[:, SW * half:SW * (half + 1)].rearrange("(k p) n -> p k n", p=P), win_in[half])
            for n in range(KD, KD + 9):
                load_mod(n)
            sp.wait_ge(w_T, 8)
            sp.wait_ge(ca_pool, 3)
            load(dft, dft_const, dft_in)
            load(parity, parity_const, dft_in)
            load(wf_s.rearrange("p (j n) -> p j n", j=FG), w_fourier.rearrange("j c n -> c j n"), dft_in)
            for n in range(KD + 9, KD + 12):
                load_mod(n)
            sp.wait_ge(kk_ready, 1)
            for i in range(4):
                sp.dma_start(kk_dram[8 * i:8 * i + 8].rearrange("g q n -> (g q) n"),
                             KK[:, i].rearrange("p e q -> p (e q)")).then_inc(kk_out, 16)
            sp.wait_ge(kk_out, 64)
            for t in range(T):
                load(M[Q * t:Q * (t + 1)], kk_dram[:, :, Q * (T - 1 - t):Q * (2 * T - 1 - t)].rearrange("g q n -> q g n"), m_in)
            sp.wait_ge(f_done, 2)
            load(w_glu_s, w_glu.rearrange("(k p) n -> p k n", p=P), glu_in)
            load(xr, x.rearrange("(i p) n -> p i n", p=P), xr_in)
            for n in range(KD + 12, KD + 15):
                load_mod(n)
            sp.wait_ge(gg_done, 4)
            load(posr, pos.rearrange("(i p) n -> p i n", p=P), xr_in)
            sp.wait_ge(s2_act, 1)
            sp.wait_ge(s2_dve, 1)
            load(keys_nat, sub_keys.rearrange("h s k d -> k (h s) d"), keys_in)
            load(w_out_s, w_out.rearrange("(k p) n -> p k n", p=P), wout_in)
            load_mod(3 * KD - 1)
            sp.wait_ge(y_done, 1)
            sp.wait_ge(glu_done, 1)
            sp.wait_ge(xt_T, 4)
            load(w_q_s[:, 4:8], peer_w_q[D // 2:D].rearrange("(k p) n -> p k n", p=P), wq_first_in)
            sp.wait_ge(mod_done, 3 * KD)
            for cols, s in ((slice(0, 4 * P), wq_first_in), (slice(4 * P, 2 * HEADS * P), wq_in)):
                load(w_q_s[:, 0:4, cols], peer_w_q[0:D // 2, cols].rearrange("(k p) n -> p k n", p=P), s)
            load(fgb, final_g.partition_broadcast(P), fg_in)
            for i in range(NT):
                sp.wait_ge(out_row, i + 1)
                sp.dma_start(out[P * i:P * (i + 1), :], rowA).then_inc(out_done, 16)
            sp.wait_ge(out_done, 16 * NT)

        @block.tensor
        def _(pe):
            pe.wait_ge(const_in, 16)
            pe.wait_ge(vec_in, 7 * 16)
            nc.tensor.transpose(bank[6][:, 0:V_ROWS], vec_nat, ident[0:V_ROWS, 0:V_ROWS]).then_inc(params_T, 1)
            pe.wait_ge(lam_in, 3 * 16)
            pe.wait_ge(logdt_spread, 1)
            for r in range(3):
                last = nc.tensor.transpose(bank[7][:, G * r:G * (r + 1)], lam_nat[r], ident[0:G, 0:G])
            last.then_inc(params_T, 1)
            pe.wait_ge(b_in, 2 * 16)
            for r in range(2):
                for q in range(Q):
                    last = nc.tensor.transpose(bank[4 + r][:, G * q:G * (q + 1)],
                                               Bnat[r][:, q:2048:Q], ident[0:G, 0:G])
            last.then_inc(params_T, 1)
            pe.wait_ge(c_in, 4 * 16)
            for r in range(2):
                for i in range(4):
                    last = nc.tensor.transpose(bank[2 + r][:, P * i:P * (i + 1)],
                                               Cnat[r][:, i].rearrange("p d n -> p (d n)"), ident)
            last.then_inc(params_T, 1)

            def mod_block(n):
                slot, k = n % WM_RING, n % KD
                pe.wait_ge(wm_in[slot], 16 * (n // WM_RING + 1))
                if n == 0:
                    pe.wait_ge(cact_ready, 1)
                    pe.wait_ge(rows_cleared, 1)
                if k == 0 and n:
                    pe.wait_ge(mrow_ready, n // KD)
                for j in range(4):
                    last = nc.tensor.matmul(bank[6][32 * j:32 * j + 2, :], cact[:, k:16:8],
                                            wm[slot][:, 512 * j:512 * (j + 1)], start=(k == 0), stop=(k == KD - 1))
                last.then_inc(mod_done, 1)

            def mod_transpose(pair):
                pe.wait_ge(mrow_ready, pair + 1)
                if pair:
                    pe.wait_ge(mod_read, 2 * pair)
                else:
                    pe.wait_ge(par_ready, 1)
                for m in range(4):
                    last = nc.tensor.transpose(bank[7][:, P * m:P * (m + 1)], mrow[pair][:, P * m:P * (m + 1)], ident)
                last.then_inc(modT_done, 1)

            for n in range(KD - 2):
                mod_block(n)

            pe.wait_ge(xn_ready, 4)
            for k in range(KD):
                if k in (2, 3):
                    pe.wait_ge(cs_ready, 2)
                if k >= 4:
                    pe.wait_ge(hraw_act if k % 2 else hraw_dve, k // 2 - 1)
                for tt in range(4):
                    src = (xc if tt < 2 else xl)[:, tt % 2, P * k:P * (k + 1)]
                    last = nc.tensor.transpose(bank[k % 4][:, P * tt:P * (tt + 1)], src, ident)
                last.then_inc(x_T, 1)
            for n in range(KD - 2, KD):
                mod_block(n)
            mod_transpose(0)

            def w_transpose(ready, count, tmp, first):
                pe.wait_ge(ready, count)
                if count > 1:
                    pe.wait_ge(w_ready, 4 * (count - 1) - (2 if first == 4 else 0))
                elif first == 4:
                    pe.wait_ge(bb_ready, 1)
                else:
                    pe.wait_ge(mrow_ready, 1)
                    pe.wait_ge(mod_read, 2)
                for r in range(2):
                    for gg in range(4):
                        last = nc.tensor.transpose(bank[first + r][:, P * gg:P * (gg + 1)],
                                                   tmp[:, 1024 * r + P * gg:1024 * r + P * (gg + 1)], ident)
                last.then_inc(w_T, 1)

            def z_tile(tt):
                for k in range(KD):
                    last = nc.tensor.matmul(bank[tt][:, :], hT[:, k, P * tt:P * (tt + 1)], w_in_s[0][:, k, :],
                                            start=(k == 0), stop=(k == KD - 1))
                last.then_inc(z_done, 1)

            def u_transpose():
                pe.wait_ge(zg_act, 1)
                pe.wait_ge(zg_dve, 1)
                pe.wait_ge(z_evac, 4)
                for g in range(G):
                    last = nc.tensor.transpose(bank[g // 8][:, 2 * C * (g % 8):2 * C * (g % 8 + 1)],
                                               Z[64:128, P * g:P * (g + 1)], ident[64:128, 64:128])
                    if g % 8 == 7:
                        last.then_inc(u_T, 1)

            def v_rows(b):
                if b >= 4:
                    pe.wait_ge(vr_ready[b % 2], (b - 4) // 2 + 1)
                for a in range(2):
                    for h in range(2):
                        g = 4 * b + 2 * a + h
                        last = nc.tensor.matmul(bank[b % 4][64 * h:64 * (h + 1), 2 * P * a:2 * P * (a + 1)],
                                                Us[:, g, :], W[:, g, :, :].rearrange("p r n -> p (r n)"), start=True, stop=True)
                last.then_inc(vr_done, 1)

            def v_transpose(b):
                pe.wait_ge(vr_ready[b % 2], b // 2 + 1)
                if b >= len(V_BANKS):
                    pe.wait_ge(vs_act, b - len(V_BANKS) + 1)
                    pe.wait_ge(vs_dve, b - len(V_BANKS) + 1)
                for a in range(2):
                    for r in range(2):
                        at = 2 * P * r + P * a
                        last = nc.tensor.transpose(bank[V_BANKS[b % len(V_BANKS)]][:, at:at + P],
                                                   Vrow[:, b, a, r, :], ident)
                last.then_inc(v_done, 1)

            def v_products():
                pe.wait_ge(u_ready, 4)
                pe.wait_ge(w_ready, 16)
                v_rows(0)
                v_rows(1)
                for b in range(8):
                    v_transpose(b)
                    if b < 6:
                        v_rows(b + 2)

            pe.wait_ge(hc_ready, KD)
            pe.wait_ge(win_in[0], 16)
            for tt in range(4):
                if tt == 2:
                    pe.wait_ge(hl_ready, KD)
                z_tile(tt)
                w_transpose(wt_dve, tt + 1, dtmp, 4)
                w_transpose(wt_pool, tt + 1, ptmp, 6)
            pe.wait_ge(w_ready, 16)
            for n in range(KD, KD + 3):
                mod_block(n)
            u_transpose()
            v_products()
            for n in range(KD + 3, KD + 6):
                mod_block(n)
            pe.wait_ge(vs_act, 8)
            pe.wait_ge(vs_dve, 8)
            pe.wait_ge(ca_ready, 1)
            for i in range(4):
                if i >= 2:
                    pe.wait_ge(ca_pool, (1, 3)[i - 2])
                for h in range(2):
                    for d in range(2):
                        rows, first = slice(64 * d, 64 * (d + 1)), 2 * d
                        at = 2 * P * (i % 2) + P * h
                        for r in range(2):
                            for j in range(4):
                                g = 8 * i + 2 * j
                                last = nc.tensor.matmul(bank[2 + 2 * d + i // 2][32 * j:32 * (j + 1), at:at + P],
                                                        Bb[r][rows, g:g + 2, :].rearrange("p g q -> p (g q)"),
                                                        CA[r][rows, g + h, first:first + T, :].rearrange("p s q -> p (s q)"),
                                                        start=(r == 0), stop=(r == 1))
            last.then_inc(k_done, 1)
            for n in range(KD + 6, KD + 9):
                mod_block(n)
            pe.wait_ge(win_in[1], 16)
            for j in range(FG):
                for k in range(KD):
                    last = nc.tensor.matmul(bank[j // 2][:, SEQ * (j % 2):SEQ * (j % 2 + 1)],
                                            w_in_s[1][:, k, P * j:P * (j + 1)], hT[:, k, SEQ:2 * SEQ],
                                            start=(k == 0), stop=(k == KD - 1))
                if j % 2:
                    last.then_inc(f_done, 1)
            for n in range(KD + 9, KD + 12):
                mod_block(n)
            pe.wait_ge(dft_in, 3 * 16)
            pe.wait_ge(k_ready, 8)
            for r, m in enumerate((cosC, sinC)):
                nc.tensor.matmul(bank[4 + r][:, :], m, wf_s, start=True, stop=True).then_inc(cw_done, 1)
            mod_transpose(1)
            pe.wait_ge(f_ready, 2)
            pe.wait_ge(cw_ready, 2)
            for r in range(2):
                for i in range(NT):
                    for j in range(FG):
                        last = nc.tensor.matmul(bank[2 * r + i][:, P * j:P * (j + 1)], fT[:, j, P * i:P * (i + 1)],
                                                CW[r][:, P * j:P * (j + 1)], start=True, stop=True)
                    last.then_inc(gg_done, 1)
            pe.wait_ge(m_in, T * 16)
            pe.wait_ge(gg_ready, 4)
            pe.wait_ge(s2_act, 1)
            pe.wait_ge(s2_dve, 1)
            for i in range(8):
                for r in (None, 0, 1):
                    for j in range(4):
                        g = 8 * j + i
                        o = bank[2 + i // 4][C * j:C * (j + 1), P * (i % 4):P * (i % 4 + 1)]
                        if r is None:
                            nc.tensor.matmul(o, Us[:, g, C:2 * C], M[:, g, :], start=True, stop=False)
                        else:
                            last = nc.tensor.matmul(o, S2[:, r, g, :], CA[r][:, g, 1:1 + T, :].rearrange("p s q -> p (s q)"),
                                                    start=False, stop=(r == 1))
            last.then_inc(y_done, 1)
            pe.wait_ge(y_act, 1)
            pe.wait_ge(y_dve, 1)
            for j in range(4):
                for t in range(T):
                    last = nc.tensor.transpose(bank[2 + j][:, C * t:C * (t + 1)], Yc[C * j:C * (j + 1), t, :],
                                               ident[C * j:C * (j + 1), C * j:C * (j + 1)])
            last.then_inc(yt_done, 1)

            for j in range(FG):
                for n, (r, i) in enumerate(((0, 0), (0, 1), (1, 0), (1, 1))):
                    last = nc.tensor.matmul(bank[j // 2][:, SEQ * (j % 2):SEQ * (j % 2 + 1)],
                                            GC[r][:, i, P * j:P * (j + 1)], (cosL, nsinL)[r][:, i, :],
                                            start=(n == 0), stop=(n == 3))
                if j % 2:
                    last.then_inc(fft_done, 1)
            pe.wait_ge(g2y_ready, 1)
            pe.wait_ge(glu_in, 16)
            for n in range(4):
                for k in range(4):
                    last = nc.tensor.matmul(bank[4 + n // 2][:, SEQ * (n % 2):SEQ * (n % 2 + 1)],
                                            w_glu_s[:, k, P * n:P * (n + 1)], gA[:, k, :], start=(k == 0), stop=(k == 3))
            last.then_inc(glu_done, 1)
            for n in range(KD + 12, KD + 15):
                mod_block(n)
            pe.wait_ge(xr_ready, 1)
            pe.wait_ge(mix_f, 2)
            for i in range(NT):
                for b in range(2):
                    for k in range(4):
                        last = nc.tensor.transpose(bank[2 * i + b][:, P * k:P * (k + 1)],
                                                   xr[:, i, P * (4 * b + k):P * (4 * b + k + 1)], ident)
                    last.then_inc(xt_T, 1)

            def out_projection(i, first, last_n):
                for n in range(first, last_n):
                    for k in range(KD):
                        last = nc.tensor.matmul(projected(i, n),
                                                w_out_s[:, k, P * n:P * (n + 1)], mixT[:, k, P * i:P * (i + 1)],
                                                start=(k == 0), stop=(k == KD - 1))
                if last_n == KD:
                    last.then_inc(o_done, 1)

            def gate_rows():
                pe.wait_ge(gdiag_ready, 1)
                pe.wait_ge(x1_ready, 2)
                for b in range(2):
                    last = nc.tensor.matmul(bank[2 + b][:, :], ones, gdiag[:, 512 * b:512 * (b + 1)], start=True, stop=True)
                last.then_inc(g2_done, 1)

            def second_norm(i):
                pe.wait_ge(sq_ready, i + 1)
                if i == 0:
                    pe.wait_ge(mrow_ready, 3)
                    pe.wait_ge(mod_read, 6)
                if i:
                    pe.wait_ge(q_ready, HEADS)
                for k in range(KD):
                    last = nc.tensor.matmul(bank[6][:, 0:1], h2T[:, k, :], ones[:, 0:1], start=(k == 0), stop=(k == KD - 1))
                last.then_inc(ss_done, 1)
                if i == 0:
                    pe.wait_ge(kt_ready, 4)
                    out_projection(1, 0, 1)
                else:
                    gate_rows()
                pe.wait_ge(diag2_ready, i + 1)
                nc.tensor.matmul(bank[6][:, P:2 * P], ones, diag2, start=True, stop=True).then_inc(invb_done, 1)
                if i == 0:
                    out_projection(1, 1, 2)
                pe.wait_ge(h2_ready, 2 * i + 1)

            def rows_of_h2(i):
                pe.wait_ge(h2_ready, 2 * i + 2)
                pe.wait_ge(kt_ready, 4)
                for k in range(KD):
                    last = nc.tensor.transpose(bank[2 * i + k // 4][:, P * (k % 4):P * (k % 4 + 1)], h2T[:, k, :], ident)
                last.then_inc(h2_pd, 1)

            def queries(i, h):
                n = HEADS * i + h
                if n >= 2:
                    pe.wait_ge(q_ready, n - 1 if n < HEADS else n)
                for s in range(2):
                    for k in range(KD):
                        if h == 0 and s == 0 and k == KD // 2:
                            pe.wait_ge(h2_ready, 2 * i + 2)
                        at = 2 * P * h + P * s
                        last = nc.tensor.matmul(query_place(n)[:, P * s:P * (s + 1)],
                                                w_q_s[:, k, at:at + P], h2T[:, k, :], start=(k == 0), stop=(k == KD - 1))
                last.then_inc(q_done, 1)

            def scores(i, h):
                n = HEADS * i + h
                pe.wait_ge(q_ready, n + 1)
                if n >= 2:
                    pe.wait_ge(s_ready, n - 1 if n < HEADS else n)
                for s in range(2):
                    last = nc.tensor.matmul(score_place(n)[:, P * s:P * (s + 1)],
                                            qT[:, h % 2, s, :], kT[:, 2 * h + s, :], start=True, stop=True)
                last.then_inc(s_done, 1)

            pe.wait_ge(mix_s5, 1)
            pe.wait_ge(wout_in, 16)
            out_projection(0, 0, KD)
            mod_block(3 * KD - 1)
            pe.wait_ge(keys_in, 16)
            pe.wait_ge(xt_ready, 4)
            for b in range(4):
                for i in range(4):
                    last = nc.tensor.transpose(bank[b][:, P * i:P * (i + 1)], keys_nat[:, 4 * b + i, :], ident)
                last.then_inc(keys_T, 1)
            mod_transpose(2)
            pe.wait_ge(ones_ready, 1)
            pe.wait_ge(xt_ready, 4)
            second_norm(0)
            pe.wait_ge(wq_first_in, 2 * 16)
            queries(0, 0)
            rows_of_h2(0)
            scores(0, 0)
            queries(0, 1)
            scores(0, 1)
            pe.wait_ge(x1_ready, 1)
            out_projection(1, 2, KD)
            pe.wait_ge(wq_in, 16)
            queries(0, 2)
            for h in range(3, HEADS):
                queries(0, h)
                scores(0, h - 1)
            scores(0, HEADS - 1)
            def add_up(h_at, h, first, last_head, ranks=TOPK):
                for j in range(ranks):
                    pe.wait_ge(diag_ready, h_at * TOPK + (j + 1))
                    pe.wait_ge(v_in[j % V_RING], h_at * 32 + 16 * (j // V_RING + 1))
                    for b in range(2):
                        last = nc.tensor.matmul(bank[4 + b][:, :], diag[:, j % 8, :], Vring[:, j % V_RING, 512 * b:512 * (b + 1)],
                                                start=(first and j == 0), stop=(last_head and j == ranks - 1))
                    last.then_inc(v_used, 1)

            def row_of_x1(i):
                pe.wait_ge(s_ready, 2 * HEADS)
                if i:
                    pe.wait_ge(out_row, 1)
                for k in range(KD):
                    last = nc.tensor.transpose(bank[6 + k // 4][:, P * (k % 4):P * (k % 4 + 1)],
                                               x1T[:, k, P * i:P * (i + 1)], ident)
                last.then_inc(x1r_done, 1)

            pe.wait_ge(s_ready, HEADS)
            add_up(0, 0, True, False)
            second_norm(1)
            pe.wait_ge(g2b_ready, 1)
            rows_of_h2(1)
            for h in range(1, HEADS):
                for n in queries_before(h):
                    queries(1, n)
                    scores(1, n)
                add_up(h, h, False, h == HEADS - 1)
            row_of_x1(0)
            pe.wait_ge(y_row, 1)
            add_up(HEADS, 0, True, False)
            with pe.Fori(HEADS + 1, 2 * HEADS - 1) as h:
                add_up(h, None, False, False)
            row_of_x1(1)
            add_up(2 * HEADS - 1, HEADS - 1, False, True, TOPK - DVE_RANKS)

        @block.vector
        def _(dve):
            v = nc.vector
            ch = Chain(dve, dve_step)
            dve.wait_ge(lam_in, 3 * 16)
            v.tensor_copy(lam_nat[2].rearrange("g (d n) -> g d n", d=2), spread(ld_nat, 2, [G, 2, NS])).then_inc(logdt_spread, 1)
            dve.wait_ge(params_T, 1)
            v.tensor_copy(vecT, bank[6][:, 0:V_ROWS]).then_inc(vec_ready, 1)
            dve.wait_ge(vec_ready, 1)
            v.tensor_scalar(half_bg, vecT[:, V_BGLU:V_BGLU + 4], 0.5, None, ALU.mult)
            for i in range(4):
                v.tensor_scalar(dE[:, i, :], eyeq, vecT[:, V_D + i:V_D + i + 1], None, ALU.mult)
            dve.wait_ge(silu_th, 1)
            ch.link(v.scalar_tensor_tensor(cact, th_c, 1.0, vecT[:, 0:16], ALU.add, ALU.mult))
            v.tensor_scalar(cact, cact, 0.5, None, ALU.mult).then_inc(cact_ready, 1)
            dve.wait_ge(params_T, 2)
            v.tensor_copy(par, bank[7][:, 0:3 * G].rearrange("p (a g) -> p a g", a=3)).then_inc(par_ready, 1)
            v.memset(bank[6][:, :], 0.0).then_inc(rows_cleared, 1)
            dve.wait_ge(par_ready, 1)
            lr, li = par[:, 0, :], par[:, 1, :]
            dt_, ld_, y1, t0 = (dtmp[:, 32 * n:32 * (n + 1)] for n in range(4))
            cr, ci = dtmp[:, 1920:1952], dtmp[:, 1952:1984]
            A_, B_, C_ = dtmp[:, 128:768], dtmp[:, 768:1408], ptmp[:, 0:640]
            a3, b3 = (z.rearrange("p (s g) -> p s g", s=SLOTS) for z in (A_, B_))
            shape = [P, SLOTS, G]
            dve.wait_ge(dt_ready, 1)
            ch.link(v.tensor_tensor(y1, li, dt_, ALU.mult))
            ch.step(v.tensor_tensor(ld_, lr, dt_, ALU.mult))
            ch.link(v.tensor_scalar(y1, y1, 0.15915494309189535, None, ALU.mult))
            ch.link(v.tensor_scalar(t0, y1, ROUND, ROUND, ALU.add, ALU.subtract))
            ch.link(v.tensor_tensor(y1, y1, t0, ALU.subtract))
            dve.wait_ge(const_in, 16)
            ch.link(v.tensor_tensor(a3, spread(y1, 1, shape), spread(kmul, 2, shape), ALU.mult))
            ch.step(v.tensor_scalar(B_, A_, ROUND, ROUND, ALU.add, ALU.subtract))
            ch.link(v.tensor_scalar(C_, A_, 0.25, None, ALU.add))
            ch.link(v.tensor_tensor(A_, A_, B_, ALU.subtract))
            ch.link(v.tensor_scalar(B_, C_, ROUND, ROUND, ALU.add, ALU.subtract))
            v.tensor_tensor(C_, C_, B_, ALU.subtract).then_inc(trig_in, 1)
            dve.wait_ge(trig_in, 1)
            v.tensor_tensor(b3, spread(ld_, 1, shape), spread(kmul, 2, shape), ALU.mult).then_inc(trig_in, 1)
            dve.wait_ge(trig_out, 3)
            v.tensor_tensor(Pw[0], Pw[0], b3, ALU.mult).then_inc(pw_ready, 1)
            v.tensor_tensor(Pw[1], Pw[1], b3, ALU.mult).then_inc(pw_ready, 1)
            dve.wait_ge(pw_ready, 2)
            for r in range(2):
                v.tensor_copy(A8[:, 0, r, :], Pw[0][:, 19, :])
                v.tensor_scalar(A8[:, 1, r, :], Pw[1][:, 19, :], (1.0, -1.0)[r], None, ALU.mult)
            ar, ai = t0, Pw[1][:, 18, :]
            den, t1, t2 = y1, dt_, ld_
            ch.step(v.tensor_scalar(ar, Pw[0][:, 18, :], -1.0, None, ALU.add))
            ch.step(v.tensor_tensor(den, lr, lr, ALU.mult))
            ch.link(v.tensor_tensor(t1, li, li, ALU.mult))
            ch.link(v.tensor_tensor(den, den, t1, ALU.add))
            ch.link(v.reciprocal(den, den))
            ch.step(v.tensor_tensor(t1, ar, lr, ALU.mult))
            ch.link(v.tensor_tensor(t2, ai, li, ALU.mult))
            ch.link(v.tensor_tensor(t1, t1, t2, ALU.add))
            ch.link(v.tensor_tensor(cr, t1, den, ALU.mult))
            ch.step(v.tensor_tensor(t1, ai, lr, ALU.mult))
            ch.link(v.tensor_tensor(t2, ar, li, ALU.mult))
            ch.link(v.tensor_tensor(t1, t1, t2, ALU.subtract))
            ch.link(v.tensor_tensor(ci, t1, den, ALU.mult))
            dve.wait_ge(params_T, 3)
            gq = [P, G, Q]
            br, bi = (bank[4 + r][:, :].rearrange("p (q g) -> p g q", q=Q) for r in range(2))
            m1, m2 = (dtmp[:, 128 + 512 * n:640 + 512 * n].rearrange("p (g q) -> p g q", g=G) for n in range(2))
            cr3, ci3 = spread(cr, 2, gq), spread(ci, 2, gq)
            ch.step(v.tensor_tensor(m1, br, cr3, ALU.mult))
            ch.link(v.tensor_tensor(m2, bi, ci3, ALU.mult))
            ch.link(v.tensor_tensor(Bb[0], m1, m2, ALU.subtract))
            ch.step(v.tensor_tensor(m1, bi, cr3, ALU.mult))
            ch.link(v.tensor_tensor(m2, br, ci3, ALU.mult))
            v.tensor_tensor(Bb[1], m1, m2, ALU.add).then_inc(bb_ready, 1)
            dve.wait_ge(bb_ready, 1)

            dve.wait_ge(xl_in, 32)
            v.tensor_tensor(xl[:, :, :], xl[:, :, :], pl[:, :, :], ALU.add).then_inc(x_pos, 1)

            def w_batch(n):
                g0 = 4 * n
                if n:
                    dve.wait_ge(w_T, (0, 1, 3, 5)[n])
                w4 = [P, 4, T, Q]
                for r in range(2):
                    ta, tb = (dtmp[:, 1024 * r + 512 * z:1024 * r + 512 * z + 512].rearrange("p (g t q) -> p g t q", g=4, t=T) for z in range(2))
                    pr, pi = (spread(Pw[z][:, 10:18, g0:g0 + 4].rearrange("p s g -> p g s"), 3, w4) for z in range(2))
                    b0, b1 = (spread(Bb[z][:, g0:g0 + 4, :], 2, w4) for z in range(2))
                    ch.step(v.tensor_tensor(ta, pr, (b0, b1)[r], ALU.mult))
                    ch.link(v.tensor_tensor(tb, pi, (b1, b0)[r], ALU.mult))
                    last = v.tensor_tensor(ta, ta, tb, (ALU.subtract, ALU.add)[r])
                    if r == 0:
                        ch.step(last)
                ch.after()
                last.then_inc(wt_dve, 1)

            def mean_square(n, total, cols):
                v.tensor_scalar(ms[:, 0:cols], total, 1.0 / D, EPS, ALU.mult, ALU.add).then_inc(ms_ready, 1)

            def inverse_root(n, out_, cols):
                m, r, q = ms[:, 0:cols], root[:, 0:cols], newton[:, 0:cols]
                dve.wait_ge(root_ready, n)
                ch.link(v.reciprocal(r, r))
                ch.link(v.tensor_tensor(q, r, r, ALU.mult))
                ch.link(v.tensor_tensor(q, q, m, ALU.mult))
                ch.link(v.tensor_scalar(q, q, -0.5, 1.5, ALU.mult, ALU.add))
                ch.link(v.tensor_tensor(out_, r, q, ALU.mult))

            w_batch(0)
            dve.wait_ge(ss_ready, 4)
            mean_square(1, ss, 4)
            inverse_root(1, inv, 4)
            for tt in range(4):
                src = (xc if tt < 2 else xl)[:, tt % 2, :]
                v.tensor_scalar(src, src, inv[:, tt:tt + 1], None, ALU.mult).then_inc(xn_ready, 1)
            for k in range(0, KD, 2):
                dve.wait_ge(x_T, k + 1)
                v.tensor_copy(hT[:, k, :], bank[k % 4][:, :]).then_inc(hraw_dve, 1)

            def mod_out(pair):
                dve.wait_ge(modT_done, pair + 1)
                for a in range(2):
                    part = 2 * pair + a
                    src = bank[7][:, :].rearrange("p (m a j x) -> p a j m x", m=4, a=2, j=2)[:, a, :, :, 0:2]
                    bias = vecT[:, V_BMOD + KD * part:V_BMOD + KD * (part + 1)].rearrange("p (j m) -> p j m", j=2)
                    v.tensor_tensor(modS[:, part].rearrange("p (j m) w -> p j m w", j=2), src,
                                    spread(bias, 3, [P, 2, 4, 2]), ALU.add).then_inc(mod_read, 1)

            mod_out(0)
            dve.wait_ge(mod_read, 2)
            v.scalar_tensor_tensor(Gn1, modS[:, SC1], 1.0, spread(vecT[:, V_N1:V_N1 + KD], 2, [P, KD, 2]), ALU.add, ALU.mult).then_inc(gn1_ready, 1)
            dve.wait_ge(gn1_ready, 1)
            dve.wait_ge(hraw_act, 4)
            dve.wait_ge(hraw_dve, 4)
            for k in range(KD):
                at = hT[:, k, 0:SEQ]
                v.tensor_scalar(at, at, Gn1[:, k, 1:2], modS[:, SH1, k, 1:2], ALU.mult, ALU.add).then_inc(hc_ready, 1)
            def ca_batch(n):
                g0 = 4 * n
                if n == 0:
                    dve.wait_ge(cs_ready, 2)
                    dve.wait_ge(x_pos, 1)
                if n == 4:
                    dve.wait_ge(w_T, 7)
                c4 = [P, 4, 10, Q]
                pr, pi = (spread(Pw[z][:, 0:10, g0:g0 + 4].rearrange("p s g -> p g s"), 3, c4) for z in range(2))
                c0, c1 = (spread(Cs[z][:, g0:g0 + 4, :], 2, c4) for z in range(2))
                room = dtmp if n == 4 else ca_scr
                ta, tb = (room[:, 640 * z:640 * z + 640].rearrange("p (g s q) -> p g s q", g=4, s=10) for z in range(2))
                ch.step(v.tensor_tensor(ta, pr, c0, ALU.mult))
                ch.link(v.tensor_tensor(tb, pi, c1, ALU.mult))
                ch.link(v.tensor_tensor(CA[0][:, g0:g0 + 4], ta, tb, ALU.subtract))
                fa, fb = room[:, 0:640], room[:, 640:1280]
                ch.step(v.tensor_tensor(ta, pr, c1, ALU.mult))
                ch.link(v.tensor_tensor(tb, pi, c0, ALU.mult))
                last = v.scalar_tensor_tensor(CA[1][:, g0:g0 + 4].rearrange("p g s q -> p (g s q)"), fa, -1.0, fb, ALU.mult, ALU.subtract)
                if n == 4:
                    last.then_inc(ca_ready, 1)
                else:
                    ch.link(last)

            w_batch(1)
            ca_batch(0)
            w_batch(2)
            ca_batch(1)
            w_batch(3)
            ca_batch(2)
            ca_batch(3)

            def z_permute():
                for side in range(2):
                    dve.wait_ge(zc_in[side], 32)
                src = Z[0:64, :].rearrange("p (t g q) -> p g t q", t=T, g=G)
                dst = Z[64:128, :].rearrange("p (g t q) -> p g t q", g=G, t=T)
                v.tensor_copy(dst[:, 0:16], src[:, 0:16]).then_inc(zg_dve, 1)

            def v_backward():
                dve.wait_ge(u_T, 4)
                for b in range(8):
                    if b % 2 == 0:
                        dve.wait_ge(vr_done, b + 2)
                        v.tensor_copy(Vrow[:, b + 1].rearrange("p a r n -> p (a r n)"), bank[(b + 1) % 4][:, :]).then_inc(vr_ready[1], 1)
                    dve.wait_ge(v_done, b + 1)
                    src = bank[V_BANKS[b % len(V_BANKS)]][64:128, :].rearrange("p (r g s c) -> p g r s c", g=4, r=2, s=2)
                    dst = VS[64:128].rearrange("p (s c) r g -> p g r s c", s=2)[:, 4 * b:4 * b + 4]
                    for r in range(2):
                        last = v.tensor_copy(dst[:, :, r], src[:, :, r, :, ::-1])
                    last.then_inc(vs_dve, 1)

            def advance(prev, cur, table, scr, base):
                n = cur.shape[1] if len(cur.shape) == 3 else 1
                shape = [P, 2] + list(cur.shape[1:])
                tab = table if n == 1 else spread(table, 2, shape)
                v.tensor_tensor(scr, spread(prev, 1, shape), tab, ALU.mult).then_inc(scan_step, 1)
                dve.wait_ge(scan_step, base + 1)
                v.tensor_tensor(cur, cur, scr[:, 0], ALU.add).then_inc(scan_step, 1)
                dve.wait_ge(scan_step, base + 2)
                w = "p n (r g) -> p n r g" if n > 1 else "p (r g) -> p r g"
                c4, s4 = cur.rearrange(w, r=2), scr[:, 1].rearrange(w, r=2)
                swapped = s4[:, :, ::-1] if n > 1 else s4[:, ::-1]
                v.tensor_tensor(c4, c4, swapped, ALU.add).then_inc(scan_step, 1)
                dve.wait_ge(scan_step, base + 3)

            z_permute()
            ca_batch(4)
            v_backward()
            dve.wait_ge(vs_act, 8)
            dve.wait_ge(vs_dve, 8)
            seg = VS.rearrange("p (s j) r g -> p s j (r g)", s=SEGS)
            a8 = A8.rearrange("p k r g -> p k (r g)")
            scr_seg = scan_scr[0][:, 0:2 * SEGS * 64].rearrange("p (k s x) -> p k s x", k=2, s=SEGS)
            scr_one = scan_scr[0][:, 0:128].rearrange("p (k x) -> p k x", k=2)
            powers = scan_tab.rearrange("p k j r g -> p k j (r g)")
            for j in range(1, SEG_LEN):
                advance(seg[:, :, j - 1], seg[:, :, j], a8, scr_seg, 3 * (j - 1))
            steps = 3 * (SEG_LEN - 1)
            dve.wait_ge(tab_ready, 1)
            for s in range(1, SEGS):
                advance(seg[:, s - 1, SEG_LEN - 1], seg[:, s, SEG_LEN - 1], powers[:, :, SEG_LEN - 1], scr_one, steps)
                steps += 3
            for s in range(SEGS // 2, SEGS):
                n = SEG_LEN - 1
                scr = scan_scr[s % 2][:, 0:2 * n * 64].rearrange("p (k j x) -> p k j x", k=2, j=n)
                cur = seg[:, s, 0:n]
                v.tensor_tensor(scr, spread(spread(seg[:, s - 1, n], 1, [P, n, 64]), 1, [P, 2, n, 64]), powers[:, :, 0:n], ALU.mult).then_inc(scan_step, 1)
                dve.wait_ge(scan_step, steps + 1)
                v.tensor_tensor(cur, cur, scr[:, 0], ALU.add).then_inc(scan_step, 1)
                dve.wait_ge(scan_step, steps + 2)
                c4, s4 = (z.rearrange("p j (r g) -> p j r g", r=2) for z in (cur, scr[:, 1]))
                v.tensor_tensor(c4, c4, s4[:, :, ::-1], ALU.add).then_inc(scan_step, 1)
                steps += 3
            dve.wait_ge(scan_step, steps)
            for r in range(2):
                last = v.tensor_copy(S2[64:128, r], VS[64:128, C - 1:2 * C - 1, r][:, ::-1, :].rearrange("p c g -> p g c"))
            last.then_inc(s2_dve, 1)
            mod_out(1)
            dve.wait_ge(w_T, 8)
            v.memset(ones, 1.0).then_inc(ones_ready, 1)
            dve.wait_ge(y_done, 1)
            v.tensor_copy(Yc.rearrange("p t (i q) -> p i t q", q=Q)[:, 4:8],
                          bank[3][:, :].rearrange("p (i t q) -> p i t q", i=4, t=T)).then_inc(y_dve, 1)
            dve.wait_ge(yt_done, 1)
            dve.wait_ge(f_done, 2)
            for j in range(2):
                last = v.tensor_copy(gA[:, 2 + j, :].rearrange("p (c t) -> p c t", t=T),
                                     bank[4 + j][:, 0:SEQ].rearrange("p (t c) -> p c t", t=T))
            last.then_inc(yn_dve, 1)
            dve.wait_ge(yn_dve, 1)
            dve.wait_ge(yn_act, 1)
            dve.wait_ge(y_sq, 1)
            ch.link(v.tensor_scalar(gB, gB, GELU_K * GELU_C, GELU_K, ALU.mult, ALU.add))
            v.tensor_tensor(gB, gB, gA, ALU.mult).then_inc(y_arg, 1)
            dve.wait_ge(y_th, 1)
            v.scalar_tensor_tensor(gA, gB, 1.0, gA, ALU.add, ALU.mult).then_inc(g2y_ready, 1)
            dve.wait_ge(glu_th, 4)
            dve.wait_ge(g2y_ready, 1)
            ch.link(v.tensor_scalar(gB, gB, 0.25, 0.25, ALU.mult, ALU.add))
            v.tensor_tensor(mixT[:, 0:4, :], gB, gA, ALU.mult).then_inc(mix_s5, 1)

            def residual(i):
                at = slice(P * i, P * (i + 1))
                dve.wait_ge(o_done, i + 1)
                dve.wait_ge(xt_ready, 4)
                dve.wait_ge(mod_read, 4)
                for n in range(KD):
                    last = v.scalar_tensor_tensor(x1T[:, n, at], projected(i, n),
                                                  modS[:, G1, n, 0:1], x1T[:, n, at], ALU.mult, ALU.add)
                last.then_inc(x1_ready, 1)

            def norm_two(i):
                at = slice(P * i, P * (i + 1))
                v.tensor_tensor(x1g, x1T[:, :, at], spread(Gn2, 2, [P, KD, P]), ALU.mult).then_inc(x1g_ready, 1)
                dve.wait_ge(ss_done, i + 1)
                mean_square(2 + i, bank[6][:, 0:1], 1)
                inverse_root(2 + i, inv[:, 0:1], 1)
                v.tensor_scalar(diag2, ident, inv[:, 0:1], None, ALU.mult).then_inc(diag2_ready, 1)
                dve.wait_ge(invb_done, i + 1)
                dve.wait_ge(x1g_ready, i + 1)
                for half in (slice(0, KD // 2), slice(KD // 2, KD)):
                    shape = [P, KD // 2, P]
                    ch.link(v.tensor_tensor(h2T[:, half, :], spread(bank[6][:, P:2 * P], 1, shape), x1g[:, half, :], ALU.mult))
                    v.tensor_tensor(h2T[:, half, :], h2T[:, half, :], spread(modS[:, SH2, half, 0], 2, shape), ALU.add).then_inc(h2_ready, 1)

            def top_k(n, h, base):
                k = [0]

                def link(ins, wait=True):
                    ins.then_inc(dve_step, 1)
                    k[0] += 1
                    if wait:
                        wait_alone(dve, dve_step, base + k[0], dve_passed)

                wait_alone(dve, s_ready, n + 1, dve_passed)
                hs = wrk.rearrange("p (s n) -> p s n", s=2)
                link(v.tensor_copy(hs, sc[:, h] if isinstance(h, int) else sc[:, bass.ds(h, 1)][:, 0]))
                for s in range(2):
                    link(v.max(sv[:, s, 0:8], hs[:, s]))
                    link(v.max_index(si[:, s, 0:8], sv[:, s, 0:8], hs[:, s]), False)
                    link(v.match_replace(wrk1[:, s], sv[:, s, 0:8], hs[:, s], LOWEST))
                    link(v.max(sv[:, s, 8:16], wrk1[:, s]))
                    link(v.max_index(si[:, s, 8:16], sv[:, s, 8:16], wrk1[:, s]))
                sq = [P, TOPK, TOPK]
                c3 = cand.rearrange("p (a b) -> p a b", a=TOPK)
                w3 = wrk.rearrange("p (a b) -> p a b", a=TOPK)
                link(v.tensor_copy(sif, si), False)
                link(v.tensor_tensor(c3, spread(sv[:, 0, :], 2, sq), spread(sv[:, 1, :], 1, sq), ALU.add))
                link(v.max(best[:, 0:8], cand))
                link(v.max_index(flat[:, 0:8], best[:, 0:8], cand), False)
                link(v.match_replace(wrk, best[:, 0:8], cand, LOWEST))
                link(v.max(best[:, 8:16], wrk))
                link(v.max_index(flat[:, 8:16], best[:, 8:16], wrk))
                eh = e_all[:, bass.ds(n * TOPK, TOPK)]
                v.tensor_scalar(eh, best, best[:, 0:1], None, ALU.subtract).then_inc(top_ready, 1)
                link(v.tensor_scalar(fij[:, 0, :], flat, 4, None, ALU.logical_shift_right), False)
                link(v.tensor_scalar(fij[:, 1, :], flat, 15, None, ALU.bitwise_and))
                link(v.tensor_copy(fijf, fij))
                io = spread(iota16, 1, sq)
                link(v.tensor_tensor(c3, spread(fijf[:, 0, :], 2, sq), io, ALU.is_equal), False)
                link(v.tensor_tensor(w3, spread(fijf[:, 1, :], 2, sq), io, ALU.is_equal))
                link(v.tensor_scalar(sif[:, 0, :], sif[:, 0, :], float(KEYS), None, ALU.mult))
                link(v.tensor_tensor(c3, c3, spread(sif[:, 0, :], 1, sq), ALU.mult), False)
                link(v.tensor_tensor(w3, w3, spread(sif[:, 1, :], 1, sq), ALU.mult))
                link(v.tensor_tensor(cand, cand, wrk, ALU.add))
                link(v.tensor_reduce(pick, c3, AX, ALU.add))
                wait_alone(dve, top_ready, n + 1, dve_passed)
                v.tensor_copy(idx_all[:, bass.ds(n * TOPK, TOPK)], pick).then_inc(idx_ready, 1)
                dve.wait_ge(idx_ready, n + 1)
                return k[0]

            def dot_products(n, tile, base):
                k = [0]

                def link(ins, wait=True):
                    ins.then_inc(dve_step, 1)
                    k[0] += 1
                    if wait:
                        wait_alone(dve, dve_step, base + k[0], dve_passed)

                h2 = bank_pair[tile]
                dd = dots[:, 0, :]
                for j in range(TOPK):
                    dve.wait_ge(u_in[j % U_RING], n * 32 + 16 * (j // U_RING + 1))
                    ur = Uring[:, j % U_RING, :]
                    v.scalar_tensor_tensor(ur, ur, 1.0, h2, ALU.mult, ALU.mult, accum_out=dd[:, j:j + 1]).then_inc(u_used, 1)
                dve.wait_ge(u_used, n * TOPK + TOPK)
                link(v.tensor_tensor(garg, dd, dd, ALU.mult))
                link(v.tensor_scalar(garg, garg, GELU_K * GELU_C, GELU_K, ALU.mult, ALU.add))
                v.tensor_tensor(garg, garg, dd, ALU.mult).then_inc(garg_ready, 1)
                wait_alone(dve, exp_ready, n + 1, dve_passed)
                link(v.reciprocal(rsum[:, 0:1], esum[:, bass.ds(n, 1)]))
                link(v.tensor_scalar(rsum[:, 1:2], rsum[:, 0:1], 0.5, None, ALU.mult), False)
                link(v.tensor_tensor(dd, dd, e_all[:, bass.ds(n * TOPK, TOPK)], ALU.mult))
                dve.wait_ge(gth_ready, n + 1)
                link(v.scalar_tensor_tensor(dd, gth, 1.0, dd, ALU.add, ALU.mult))
                v.tensor_scalar(wgt[:, bass.ds(n * TOPK, TOPK)], dd, rsum[:, 1:2], None, ALU.mult).then_inc(wgt_ready, 1)
                dve.wait_ge(wgt_ready, n + 1)
                return k[0]

            def last_ranks():
                for j in range(TOPK - DVE_RANKS, TOPK):
                    if j == TOPK - 1:
                        dve.wait_ge(v_used, 2 * HEADS * TOPK - DVE_RANKS)
                        for b in range(2):
                            half = last_sum[:, 512 * b:512 * (b + 1)]
                            ch.step(v.tensor_tensor(half, half, bank[4 + b][:, :], ALU.add))
                        ch.after()
                    dve.wait_ge(v_in[j % V_RING], (2 * HEADS - 1) * 32 + 16 * (j // V_RING + 1))
                    row, w = Vring[:, j % V_RING, :], wgt[:, (2 * HEADS - 1) * TOPK + j:(2 * HEADS - 1) * TOPK + j + 1]
                    if j == TOPK - DVE_RANKS:
                        ch.link(v.tensor_scalar(last_sum, row, w, None, ALU.mult))
                    else:
                        ch.link(v.scalar_tensor_tensor(last_sum, row, w, last_sum, ALU.mult, ALU.add))

            def finish(i):
                if i:
                    last_ranks()
                    dve.wait_ge(x1r_done, 2)
                    dve.wait_ge(out_done, 16)
                    ch.link(v.tensor_tensor(rowB, last_sum, g2b, ALU.mult))
                else:
                    dve.wait_ge(v_used, TOPK * HEADS)
                    dve.wait_ge(x1r_done, 1)
                    for b in range(2):
                        ch.step(v.tensor_tensor(rowB[:, 512 * b:512 * (b + 1)], bank[4 + b][:, :], g2b[:, 512 * b:512 * (b + 1)], ALU.mult))
                    ch.after()
                for b in range(2):
                    last = v.tensor_tensor(rowB[:, 512 * b:512 * (b + 1)], rowB[:, 512 * b:512 * (b + 1)], bank[6 + b][:, :], ALU.add)
                last.then_inc(y_row, 1)
                dve.wait_ge(fin_ss, i + 1)
                mean_square(4 + i, ss[:, 0:1], 1)
                inverse_root(4 + i, inv[:, 0:1], 1)
                dve.wait_ge(fg_in, 16)
                v.scalar_tensor_tensor(rowA, rowB, inv[:, 0:1], fgb, ALU.mult, ALU.mult).then_inc(out_row, 1)

            bank_pair = [None, None]
            for i in range(NT):
                bank_pair[i] = psum[:, D * i:D * (i + 1)]
            residual(0)
            mod_out(2)
            dve.wait_ge(mod_read, 6)
            ch.link(v.scalar_tensor_tensor(Gn2, modS[:, SC2, :, 0], 1.0, vecT[:, V_N2:V_N2 + KD], ALU.add, ALU.mult))
            norm_two(0)
            ch.n += top_k(0, 0, ch.n)
            ch.n += top_k(1, 1, ch.n)
            dve.wait_ge(h2_pd, 1)
            ch.n += dot_products(0, 0, ch.n)
            ch.n += top_k(2, 2, ch.n)
            residual(1)
            v.tensor_tensor(gdiag.rearrange("p (k n) -> p k n", k=KD), spread(ident, 1, [P, KD, P]),
                            spread(modS[:, G2, :, 0], 2, [P, KD, P]), ALU.mult).then_inc(gdiag_ready, 1)
            ch.n += dot_products(1, 0, ch.n)
            norm_two(1)
            dve.wait_ge(g2_done, 1)
            for b in range(2):
                last = v.tensor_copy(g2b[:, 512 * b:512 * (b + 1)], bank[2 + b][:, :])
            last.then_inc(g2b_ready, 1)
            ch.n += top_k(3, 3, ch.n)
            n0, per = ch.n, 34
            with dve.Fori(2, HEADS - 2) as h:
                a = dot_products(h, 0, (h - 2) * per + n0)
                b_ = top_k(h + 2, h + 2, (h - 2) * per + (n0 + a))
                assert a + b_ == per, (a, b_)
            n0 += per * (HEADS - 4)
            dve.wait_ge(h2_pd, 2)
            with dve.Fori(HEADS - 2, HEADS) as h:
                a = dot_products(h, 0, (h - (HEADS - 2)) * per + n0)
                top_k(h + 2, h - (HEADS - 2), (h - (HEADS - 2)) * per + (n0 + a))
            n0 += 2 * per
            ch.n = n0
            ch.n += dot_products(HEADS, 1, ch.n)
            ch.n += top_k(HEADS + 2, 2, ch.n)
            finish(0)
            n0 = ch.n
            with dve.Fori(HEADS + 1, 2 * HEADS - 2) as h:
                a = dot_products(h, 1, (h - (HEADS + 1)) * per + n0)
                top_k(h + 2, h - (HEADS - 2), (h - (HEADS + 1)) * per + (n0 + a))
            ch.n = n0 + per * (HEADS - 3)
            for h in range(2 * HEADS - 2, 2 * HEADS):
                ch.n += dot_products(h, 1, ch.n)
            finish(1)

        @block.scalar
        def _(act):
            a = nc.scalar
            ch = Chain(act, act_step)
            for r, t in enumerate((b_re, b_im)):
                act.dma_start(Bnat[r].rearrange("g (d m) -> g d m", d=2), t.rearrange("d g n q -> g d (n q)")).then_inc(b_in, 16)
            for r, t in enumerate((c_re, c_im)):
                for d in range(2):
                    act.dma_start(Cnat[r][:, :, d, :], t[d].rearrange("(i g) q n -> (g q) i n", g=8)).then_inc(c_in, 16)
            act.wait_ge(vec_ready, 1)
            a.activation(th_c, vecT[:, 0:16], ACT.Tanh, scale=0.5).then_inc(silu_th, 1)
            act.wait_ge(par_ready, 1)
            a.activation(dtmp[:, 0:32], par[:, 2, :], ACT.Exp).then_inc(dt_ready, 1)
            act.wait_ge(trig_in, 1)
            a.activation(Pw[1].rearrange("p s g -> p (s g)"), dtmp[:, 128:768], ACT.Sin, scale=TWO_PI).then_inc(trig_out, 1)
            a.activation(Pw[0].rearrange("p s g -> p (s g)"), ptmp[:, 0:640], ACT.Sin, scale=TWO_PI).then_inc(trig_out, 1)
            act.wait_ge(trig_in, 2)
            a.activation(dtmp[:, 768:1408], dtmp[:, 768:1408], ACT.Exp).then_inc(trig_out, 1)
            act.wait_ge(params_T, 4)
            for r in range(2):
                a.copy(Cs[r].rearrange("p g q -> p (g q)"), bank[2 + r][:, :]).then_inc(cs_ready, 1)
            act.wait_ge(xc_in, 16)
            for tt in range(4):
                if tt == 2:
                    act.wait_ge(x_pos, 1)
                if tt:
                    act.wait_ge(ss_ready, tt)
                a.activation(junk, (xc if tt < 2 else xl)[:, tt % 2, :], ACT.Square, accum_out=ss[:, tt:tt + 1]).then_inc(ss_ready, 1)

            def square_root(n, cols):
                act.wait_ge(ms_ready, n)
                a.activation(root[:, 0:cols], ms[:, 0:cols], ACT.Sqrt).then_inc(root_ready, 1)

            def mod_rows(pair):
                act.wait_ge(mod_done, KD * (pair + 1))
                a.copy(mrow[pair], bank[6][:, :]).then_inc(mrow_ready, 1)

            square_root(1, 4)
            for k in range(1, KD, 2):
                act.wait_ge(x_T, k + 1)
                a.copy(hT[:, k, :], bank[k % 4][:, :]).then_inc(hraw_act, 1)
            mod_rows(0)

            act.wait_ge(gn1_ready, 1)
            act.wait_ge(hraw_act, 4)
            act.wait_ge(hraw_dve, 4)
            for k in range(KD):
                at = hT[:, k, SEQ:2 * SEQ]
                a.activation(at, at, ACT.Identity, scale=Gn1[:, k, 0:1], bias=modS[:, SH1, k, 0:1]).then_inc(hl_ready, 1)

            def w_out_of_psum(n, g0):
                act.wait_ge(w_T, n + 1)
                for r in range(2):
                    a.copy(W[:, g0:g0 + 4, r, :], bank[(6 if n % 2 else 4) + r][:, :].rearrange("p (g n) -> p g n", g=4)).then_inc(w_ready, 1)


            def z_out(tt):
                act.wait_ge(z_done, tt + 1)
                a.copy(zrow[tt], bank[tt][:, :]).then_inc(z_evac, 1)
                act.wait_ge(z_evac, tt + 1)
                lo = C * (tt // 2) + 16 * (tt % 2)
                act.dma_start(Z[lo:lo + 16, :].rearrange("c (t n) -> c t n", t=T), zrow[tt]).then_inc(zc_in[tt // 2], 16)

            def z_permute():
                for side in range(2):
                    act.wait_ge(zc_in[side], 32)
                src = Z[0:64, :].rearrange("p (t g q) -> p g t q", t=T, g=G)
                dst = Z[64:128, :].rearrange("p (g t q) -> p g t q", g=G, t=T)
                a.copy(dst[:, 16:32], src[:, 16:32]).then_inc(zg_act, 1)

            for tt in range(4):
                z_out(tt)
                w_out_of_psum(2 * tt, 4 * tt)
                w_out_of_psum(2 * tt + 1, 16 + 4 * tt)
            z_permute()
            for b in range(4):
                act.wait_ge(u_T, b + 1)
                a.copy(Us[:, 8 * b:8 * (b + 1), :], bank[b][:, :].rearrange("p (g c) -> p g c", g=8)).then_inc(u_ready, 1)
            for b in range(8):
                if b % 2 == 0:
                    act.wait_ge(vr_done, b + 1)
                    a.copy(Vrow[:, b].rearrange("p a r n -> p (a r n)"), bank[b % 4][:, :]).then_inc(vr_ready[0], 1)
                act.wait_ge(v_done, b + 1)
                src = bank[V_BANKS[b % len(V_BANKS)]][0:64, :].rearrange("p (r g c) -> p g r c", g=4, r=2)
                for r in range(2):
                    last = a.copy(VS[0:64, :, r, 4 * b:4 * b + 4].rearrange("p c g -> p g c"), src[:, :, r, :])
                last.then_inc(vs_act, 1)
            act.wait_ge(dft_in, 3 * 16)
            act.wait_ge(k_done, 1)
            for d in (1, 0):
                for h in range(2):
                    for b in range(2):
                        src = bank[2 + 2 * d + b][:, :].rearrange("p (i h n) -> p i h n", i=2, h=2)[:, :, h]
                        a.activation(Khalf[d][h][:, 2 * b:2 * b + 2], src, ACT.Copy, scale=parity[:, h:h + 1]).then_inc(k_ready, 1)
            mod_rows(1)
            act.wait_ge(ca_ready, 1)
            act.wait_ge(ca_pool, 3)
            for b in range(2):
                act.wait_ge(f_done, b + 1)
                a.copy(fT[:, 2 * b:2 * b + 2, :], bank[b][:, :].rearrange("p (j n) -> p j n", j=2)).then_inc(f_ready, 1)
            act.wait_ge(scan_step, 3 * (SEG_LEN - 1 + SEGS - 1 + SEGS // 2))
            for r in range(2):
                last = a.copy(S2[0:64, r], VS[0:64, C - 1:2 * C - 1, r].rearrange("p c g -> p g c"))
            last.then_inc(s2_act, 1)
            for r in range(2):
                act.wait_ge(cw_done, r + 1)
                a.copy(CW[r], bank[4 + r][:, :]).then_inc(cw_ready, 1)
            for r in range(2):
                for i in range(NT):
                    act.wait_ge(gg_done, 2 * r + i + 1)
                    if r == 0 and i == 0:
                        act.wait_ge(modT_done, 2)
                    a.copy(GC[r][:, i, :], bank[2 * r + i][:, :]).then_inc(gg_ready, 1)
            act.wait_ge(y_done, 1)
            a.copy(Yc.rearrange("p t (i q) -> p i t q", q=Q)[:, 0:4],
                   bank[2][:, :].rearrange("p (i t q) -> p i t q", i=4, t=T)).then_inc(y_act, 1)
            act.wait_ge(yt_done, 1)
            for j in range(2):
                last = a.copy(gA[:, j, :].rearrange("p (c t) -> p c t", t=T),
                              bank[2 + j][:, 0:SEQ].rearrange("p (t c) -> p c t", t=T))
            last.then_inc(yn_act, 1)
            act.wait_ge(yn_act, 1)
            act.wait_ge(yn_dve, 1)
            a.activation(gB, gA, ACT.Square).then_inc(y_sq, 1)

            act.wait_ge(y_arg, 1)
            a.activation(gB, gB, ACT.Tanh).then_inc(y_th, 1)
            for b in range(2):
                act.wait_ge(fft_done, b + 1)
                a.copy(mixT[:, 4 + 2 * b:6 + 2 * b, :], bank[b][:, :].rearrange("p (j n) -> p j n", j=2)).then_inc(mix_f, 1)
            act.wait_ge(glu_done, 1)
            for n in range(4):
                a.activation(gB[:, n, :], bank[4 + n // 2][:, SEQ * (n % 2):SEQ * (n % 2 + 1)], ACT.Tanh,
                             bias=half_bg[:, n:n + 1], scale=0.25).then_inc(glu_th, 1)
            for n in range(4):
                i, b = n // 2, n % 2
                act.wait_ge(xt_T, n + 1)
                a.copy(x1T[:, 4 * b:4 * b + 4, P * i:P * (i + 1)],
                       bank[n][:, :].rearrange("p (k n) -> p k n", k=4)).then_inc(xt_ready, 1)

            def squares(i):
                act.wait_ge(x1_ready, i + 1)
                if i:
                    act.wait_ge(q_done, HEADS)
                a.activation(h2T[:, :, :], x1T[:, :, P * i:P * (i + 1)], ACT.Square).then_inc(sq_ready, 1)

            def query_out(n):
                act.wait_ge(q_done, n + 1)
                if n >= 2:
                    act.wait_ge(s_done, n - 1)
                w = n % 2
                a.copy(qT[:, w], query_place(n).rearrange("p (s n) -> p s n", s=2)).then_inc(q_ready, 1)

            def scores_out(n):
                act.wait_ge(s_done, n + 1)
                if n == 0:
                    act.wait_ge(mix_s5, 1)
                if n >= HEADS:
                    act.wait_ge(idx_ready, n - HEADS + 1)
                a.copy(sc[:, n % HEADS], score_place(n).rearrange("p (s n) -> p s n", s=2)).then_inc(s_ready, 1)

            def softmax_exp(n):
                wait_alone(act, top_ready, n + 1, act_passed)
                eh = e_all[:, bass.ds(n * TOPK, TOPK)]
                a.activation(eh, eh, ACT.Exp, accum_out=esum[:, bass.ds(n, 1)]).then_inc(exp_ready, 1)

            def gelu_tanh(n):
                act.wait_ge(garg_ready, n + 1)
                a.activation(gth, garg, ACT.Tanh).then_inc(gth_ready, 1)

            def diagonals(n, ranks=TOPK):
                wait_alone(act, wgt_ready, n + 1, act_passed)
                for j in range(ranks):
                    if not (isinstance(n, int) and n == 0 and j < 8):
                        wait_alone(act, v_used, n * TOPK + (j - 7), act_passed)
                    a.activation(diag[:, j % 8, :], ident, ACT.Copy, scale=wgt[:, bass.ds(n * TOPK + j, 1)]).then_inc(diag_ready, 1)

            def row_squares(i):
                act.wait_ge(y_row, i + 1)
                a.activation(rowA, rowB, ACT.Square, accum_out=ss[:, 0:1]).then_inc(fin_ss, 1)

            mod_rows(2)
            squares(0)
            act.wait_ge(xr_ready, 1)
            for b in range(4):
                act.wait_ge(keys_T, b + 1)
                a.copy(kT[:, 4 * b:4 * b + 4, :], bank[b][:, :].rearrange("p (h n) -> p h n", h=4)).then_inc(kt_ready, 1)
            square_root(2, 1)
            query_out(0)
            scores_out(0)
            query_out(1)
            scores_out(1)
            query_out(2)
            for n in range(3, HEADS):
                query_out(n)
                scores_out(n - 1)
            scores_out(HEADS - 1)
            softmax_exp(0)
            softmax_exp(1)
            gelu_tanh(0)
            diagonals(0)
            softmax_exp(2)
            squares(1)
            gelu_tanh(1)
            square_root(3, 1)
            for h in range(1, HEADS):
                for n in queries_before(h):
                    query_out(HEADS + n)
                    scores_out(HEADS + n)
                diagonals(h)
                softmax_exp(h + 2)
                gelu_tanh(h + 1)
            row_squares(0)
            square_root(4, 1)
            diagonals(HEADS)
            softmax_exp(HEADS + 2)
            gelu_tanh(HEADS + 1)
            with act.Fori(HEADS + 1, 2 * HEADS - 2) as h:
                diagonals(h)
                softmax_exp(h + 2)
                gelu_tanh(h + 1)
            diagonals(2 * HEADS - 2)
            gelu_tanh(2 * HEADS - 1)
            diagonals(2 * HEADS - 1, TOPK - DVE_RANKS)
            row_squares(1)
            square_root(5, 1)

        @block.gpsimd
        def _(pool):
            g_ = nc.gpsimd
            ch = Chain(pool, pool_step)
            pool.wait_ge(pw_ready, 2)
            pool.wait_ge(bb_ready, 1)
            w4 = [P, 4, T, Q]
            for n in range(4):
                g0 = 16 + 4 * n
                if n:
                    pool.wait_ge(w_T, 2 * n)
                for r in range(2):
                    ta, tb = (ptmp[:, 1024 * r + 512 * z:1024 * r + 512 * z + 512].rearrange("p (g t q) -> p g t q", g=4, t=T) for z in range(2))
                    pr, pi = (spread(Pw[z][:, 10:18, g0:g0 + 4].rearrange("p s g -> p g s"), 3, w4) for z in range(2))
                    b0, b1 = (spread(Bb[z][:, g0:g0 + 4, :], 2, w4) for z in range(2))
                    ch.step(g_.tensor_tensor(ta, pr, (b0, b1)[r], ALU.mult))
                    ch.link(g_.tensor_tensor(tb, pi, (b1, b0)[r], ALU.mult))
                    last = g_.tensor_tensor(ta, ta, tb, (ALU.subtract, ALU.add)[r])
                    if r == 0:
                        ch.step(last)
                ch.after()
                last.then_inc(wt_pool, 1)
            pool.wait_ge(cs_ready, 2)
            pool.wait_ge(w_T, 8)
            c4 = [P, 4, 10, Q]
            ta, tb = (ptmp[:, 640 * z:640 * z + 640].rearrange("p (g s q) -> p g s q", g=4, s=10) for z in range(2))
            for n in range(5, 8):
                if n > 5:
                    pool.wait_ge(ca_pool, n - 5)
                g0 = 4 * n
                pr, pi = (spread(Pw[z][:, 0:10, g0:g0 + 4].rearrange("p s g -> p g s"), 3, c4) for z in range(2))
                c0, c1 = (spread(Cs[z][:, g0:g0 + 4, :], 2, c4) for z in range(2))
                ch.step(g_.tensor_tensor(ta, pr, c0, ALU.mult))
                ch.link(g_.tensor_tensor(tb, pi, c1, ALU.mult))
                ch.link(g_.tensor_tensor(CA[0][:, g0:g0 + 4], ta, tb, ALU.subtract))
                ch.step(g_.tensor_tensor(ta, pr, c1, ALU.mult))
                ch.link(g_.tensor_tensor(tb, pi, c0, ALU.mult))
                ch.link(g_.tensor_tensor(ta, ta, tb, ALU.add))
                last = g_.tensor_scalar(CA[1][:, g0:g0 + 4].rearrange("p g s q -> p (g s q)"), ptmp[:, 0:640], -1.0, None, ALU.mult)
                last.then_inc(ca_pool, 1)
            pool.wait_ge(v_done, 8)
            re, im = scan_tab[:, 0, :, 0], scan_tab[:, 1, :, 0]
            ch.step(g_.tensor_copy(re[:, 0], A8[:, 0, 0]))
            ch.link(g_.tensor_copy(im[:, 0], A8[:, 1, 0]))
            n = 1
            while n < SEG_LEN:
                shape = [P, n, G]
                t0, t1 = (R2[:, 128 * z:128 * z + G * n].rearrange("p (n g) -> p n g", n=n) for z in range(2))
                xr_, xi_, yr_, yi_ = re[:, 0:n], im[:, 0:n], spread(re[:, n - 1], 1, shape), spread(im[:, n - 1], 1, shape)
                for out_, a0, a1, b0, b1, op in ((re, xr_, yr_, xi_, yi_, ALU.subtract), (im, xr_, yi_, xi_, yr_, ALU.add)):
                    ch.step(g_.tensor_tensor(t0, a0, a1, ALU.mult))
                    ch.link(g_.tensor_tensor(t1, b0, b1, ALU.mult))
                    ch.link(g_.tensor_tensor(out_[:, n:2 * n], t0, t1, op))
                n *= 2
            ch.link(g_.tensor_copy(scan_tab[:, 0, :, 1], re))
            g_.tensor_scalar(scan_tab[:, 1, :, 1], im, -1.0, None, ALU.mult).then_inc(tab_ready, 1)
            back, fwd = ([x.rearrange("p i (e q) -> p i e q", e=T) for x in Khalf[d]] for d in (1, 0))
            pool.wait_ge(k_ready, 4)
            ch.step(g_.tensor_tensor(KK[:, :, 0:T, :], back[0], back[1], ALU.add))
            pool.wait_ge(k_ready, 8)
            ch.step(g_.tensor_tensor(KK[:, :, T:2 * T - 1, :], fwd[0][:, :, 1:T], fwd[1][:, :, 1:T], ALU.add))
            ch.link(g_.tensor_tensor(Ktmp, fwd[0][:, :, 0], fwd[1][:, :, 0], ALU.add))
            ch.link(g_.tensor_tensor(KK[:, :, T - 1, :], KK[:, :, T - 1, :], Ktmp, ALU.add))
            g_.tensor_tensor(KK[:, :, T - 1, :], KK[:, :, T - 1, :], dE, ALU.add).then_inc(kk_ready, 1)
            pool.wait_ge(xr_in, 2 * 16)
            g_.tensor_tensor(xr[:, :, :], xr[:, :, :], posr[:, :, :], ALU.add).then_inc(xr_ready, 1)

            def fetch_indices(n, to, copies):
                wait_alone(pool, idx_ready, n + 1, pool_passed)
                g_.tensor_copy(to, idx_all[:, bass.ds(n * TOPK, TOPK)]).then_inc(idx_copied, 1)
                wait_alone(pool, idx_copied, copies, pool_passed)

            def gather(dst, table, idx, s):
                pool.indirect_dma_start(dst, None, table, bass.IndirectOffsetOnAxis(ap=idx, axis=0)).then_inc(s, 16)

            def gather_u(n, w, j):
                gather(Uring[:, j % U_RING, :], peer_u, idx_u[:, w, j:j + 1], u_in[j % U_RING])

            def gather_v(n, w, j):
                gather(Vring[:, j % V_RING, :], peer_v, idx_v[:, w, j:j + 1], v_in[j % V_RING])

            def both(n, w):
                fetch_indices(n + 1, idx_u[:, 1 - w, :], 2 * n + 2)
                fetch_indices(n, idx_v[:, w, :], 2 * n + 3)
                for j in range(TOPK):
                    wait_alone(pool, u_used, (n + 1) * TOPK + (j - (U_RING - 1)), pool_passed)
                    gather_u(n + 1, 1 - w, j)
                    if not (isinstance(n, int) and n == 0 and j < V_RING):
                        wait_alone(pool, v_used, n * TOPK + (j - (V_RING - 1)), pool_passed)
                    gather_v(n, w, j)

            pool.wait_ge(y_done, 1)
            fetch_indices(0, idx_u[:, 0, :], 1)
            for j in range(TOPK):
                if j >= U_RING:
                    wait_alone(pool, u_used, j - (U_RING - 1), pool_passed)
                gather_u(0, 0, j)
            pool.wait_ge(o_done, NT)
            both(0, 0)
            with pool.Fori(1, 2 * HEADS - 3, 2) as m:
                both(m, 1)
                both(m + 1, 0)
            last = 2 * HEADS - 2
            both(last - 1, 1)
            both(last, 0)
            fetch_indices(last + 1, idx_v[:, 1, :], 2 * last + 4)
            for j in range(TOPK):
                wait_alone(pool, v_used, (last + 1) * TOPK + (j - (V_RING - 1)), pool_passed)
                gather_v(last + 1, 1, j)


_IN_ORDER = ["x", "c", "ctx", "c_ctx", "w_mod", "b_mod", "norm1_g", "norm2_g", "w_in", "w_out", "s5_lam_re",
             "s5_lam_im", "s5_log_dt", "s5_b_re", "s5_b_im", "s5_c_re", "s5_c_im", "s5_d", "w_glu", "b_glu",
             "w_fourier", "peer_w_q", "peer_sub_keys", "peer_u", "peer_v", "final_g"]
_VIEWS = {"x": (SEQ, D), "c": (8, P), "ctx": (SEQ, D), "c_ctx": (8, P), "w_mod": (D, 6 * D), "b_mod": (48, P),
          "norm1_g": (8, P), "norm2_g": (8, P), "w_in": (D, D), "w_out": (D, D), "s5_lam_re": (2, G, NS),
          "s5_lam_im": (2, G, NS), "s5_log_dt": (2, G), "s5_b_re": (2, G, NS, Q), "s5_b_im": (2, G, NS, Q),
          "s5_c_re": (2, G, Q, NS), "s5_c_im": (2, G, Q, NS), "s5_d": (4, P), "w_glu": (SW, SW), "b_glu": (4, P),
          "w_fourier": (FG, P, P), "peer_w_q": (D, 2 * HEADS * P), "peer_sub_keys": (HEADS, 2, KEYS, P),
          "peer_u": (KEYS * KEYS, D), "peer_v": (KEYS * KEYS, D), "final_g": (D,)}


def shape_constants():
    f32 = np.float32
    quarter = D // 4
    omega = (f32(1.0) / (f32(10000.0) ** (np.arange(quarter, dtype=f32) / f32(quarter)))).astype(f32)
    rows = SEQ // GRID_W
    r = np.repeat(np.arange(rows, dtype=f32), GRID_W)[:, None] * omega
    col = np.tile(np.arange(GRID_W, dtype=f32), rows)[:, None] * omega
    pos = np.concatenate([np.sin(r), np.cos(r), np.sin(col), np.cos(col)], axis=-1).astype(f32)
    fwd = [0, 1, 2, 3, 4, 5, 6, 7, 8, 0] + [7 - t for t in range(T)] + [1, 8]
    bwd = [0, 8, 7, 6, 5, 4, 3, 2, 1, 0] + [t for t in range(T)] + [1, 8]
    small = np.zeros((P, 180), f32)
    small[:, 0:128] = np.eye(P)
    small[0:64, 128:148] = fwd
    small[64:128, 128:148] = bwd
    small[:, 148:164] = np.arange(16)
    small[:, 164:180] = np.tile(np.eye(Q), (8, 1))
    dft = np.zeros((P, 1280), f32)
    ang = 2 * np.pi * (np.outer(np.arange(P), np.arange(P)) % P) / P
    dft[:, 0:128], dft[:, 128:256] = np.cos(ang) / np.sqrt(P), np.sin(ang) / np.sqrt(P)
    ang = 2 * np.pi * (np.outer(np.arange(SEQ), np.arange(SEQ)) % SEQ) / SEQ
    for at, m in ((256, np.cos(ang)), (768, -np.sin(ang))):
        dft[:, at:at + 512] = (m / np.sqrt(SEQ)).reshape(NT, P, SEQ).transpose(1, 0, 2).reshape(P, 512)
    group = np.arange(P) // Q
    parity = np.stack([group % 2 == 0, group % 2 == 1], axis=1).astype(f32)
    return {"pos": pos, "small_const": small, "dft_const": dft, "parity_const": parity}


def kernel(**inputs):
    import concourse.bacc as bacc
    from concourse.bass_utils import run_bass_kernel_spmd

    nc = bacc.Bacc("TRN2", target_bir_lowering=False, num_devices=1)
    arrays = {n: np.ascontiguousarray(np.asarray(inputs[n]).reshape(_VIEWS[n])) for n in _IN_ORDER}
    constants = shape_constants()
    args = []
    for n, a in [(n, arrays[n]) for n in _IN_ORDER] + list(constants.items()):
        arrays["in_" + n] = a
        args.append(nc.dram_tensor("in_" + n, a.shape, mybir.dt.float32, kind="ExternalInput").ap())
    arrays = {n: a for n, a in arrays.items() if n.startswith("in_")}
    args.append(nc.dram_tensor("out", (SEQ, D), mybir.dt.float32, kind="ExternalOutput").ap())
    hybrid_layer(nc, *args)
    r = run_bass_kernel_spmd(nc, [arrays], core_ids=[0])
    return np.asarray(r.results[0]["out"]).reshape(1, SEQ, D)
```
